# Optimizing a Trainium2 kernel written in Bass

```python
import math
import jax, jax.numpy as jnp
from jax import lax
import numpy as np

D_MODEL = 1024
BATCH = 1
SEQ = 512
DEPTH = 2

N_HEADS = 16
D_NOPE = 64
D_V = 64
D_CQ = 256
D_CKV = 128
IDX_HEADS = 8
IDX_DIM = 64
TOPK_MAX = 256
Q_BLOCK = 128
W_IN_COLS = D_CQ + D_CKV + IDX_DIM + IDX_HEADS
CONV_WIDTH = 31
D_FF = 4 * D_MODEL
NUM_BUCKETS = 32
MAX_EXACT = 16
MAX_DISTANCE = 128
EPS = 1e-6
N_ATTN_LAYERS = (DEPTH + 1) // 2
N_CONV_LAYERS = DEPTH // 2

kernel_name = "dsa_conformer_interleaved_hybrid"

def rmsnorm(x, g):
    xf = x.astype(jnp.float32)
    y = xf * lax.rsqrt(jnp.mean(xf * xf, axis=-1, keepdims=True) + EPS)
    return (y * g.astype(jnp.float32)).astype(x.dtype)

def layernorm(x, g, b):
    xf = x.astype(jnp.float32)
    mu = jnp.mean(xf, axis=-1, keepdims=True)
    var = jnp.mean(jnp.square(xf - mu), axis=-1, keepdims=True)
    y = (xf - mu) * lax.rsqrt(var + EPS)
    return (y * g.astype(jnp.float32) + b.astype(jnp.float32)).astype(x.dtype)

def t5_bucket(dist):
    n = jnp.maximum(dist, 0)
    nf = jnp.maximum(n, 1).astype(jnp.float32)
    large = MAX_EXACT + (jnp.log(nf / MAX_EXACT) / math.log(MAX_DISTANCE / MAX_EXACT)
                         * (NUM_BUCKETS - MAX_EXACT)).astype(jnp.int32)
    large = jnp.minimum(large, NUM_BUCKETS - 1)
    return jnp.where(n < MAX_EXACT, n, large)

def dsa_mla(h, rel_bias, w_in, q_norm, kv_norm, kidx_norm, w_qidx, w_uq, w_uk, w_uv, w_o):
    B, S, _ = h.shape
    k_sel = min(TOPK_MAX, S // 4)
    proj = h @ w_in
    c_q, c_kv, k_idx, w_idx = jnp.split(proj, [D_CQ, D_CQ + D_CKV, D_CQ + D_CKV + IDX_DIM], axis=-1)
    c_q = rmsnorm(c_q, q_norm)
    c_kv = rmsnorm(c_kv, kv_norm)
    k_idx = rmsnorm(k_idx, kidx_norm)
    q_idx = (c_q @ w_qidx).reshape(B, S, IDX_HEADS, IDX_DIM) * (IDX_DIM ** -0.5)
    w_idx = w_idx * (IDX_HEADS ** -0.5)
    q_h = (c_q @ w_uq).reshape(B, S, N_HEADS, D_NOPE)
    q_lat = jnp.einsum('bshd,chd->bshc', q_h, w_uk) * (D_NOPE ** -0.5)
    s_pos = jnp.arange(S, dtype=jnp.int32)

    def block(i):
        q0 = i * Q_BLOCK
        qi = lax.dynamic_slice_in_dim(q_idx, q0, Q_BLOCK, axis=1)
        wi = lax.dynamic_slice_in_dim(w_idx, q0, Q_BLOCK, axis=1)
        ql = lax.dynamic_slice_in_dim(q_lat, q0, Q_BLOCK, axis=1)
        t = q0 + jnp.arange(Q_BLOCK, dtype=jnp.int32)
        score = jnp.einsum('bqh,bqhs->bqs', wi,
                           jax.nn.relu(jnp.einsum('bqhd,bsd->bqhs', qi, k_idx)))
        causal = s_pos[None, None, :] <= t[None, :, None]
        score = jnp.where(causal, score.astype(jnp.float32), -jnp.inf)
        _, idx = lax.top_k(score, k_sel)
        valid = idx <= t[None, :, None]
        kv = jax.vmap(lambda c, j: c[j])(c_kv, idx)
        logits = jnp.einsum('bqhc,bqkc->bqhk', ql, kv).astype(jnp.float32)
        bias = rel_bias[t5_bucket(t[None, :, None] - idx)]
        logits = logits + jnp.moveaxis(bias, -1, 2).astype(jnp.float32)
        logits = jnp.where(valid[:, :, None, :], logits, -jnp.inf)
        p = jax.nn.softmax(logits, axis=-1).astype(kv.dtype)
        o_lat = jnp.einsum('bqhk,bqkc->bqhc', p, kv)
        o = jnp.einsum('bqhc,chd->bqhd', o_lat, w_uv)
        return o.reshape(B, Q_BLOCK, N_HEADS * D_V)

    out = lax.map(block, jnp.arange(S // Q_BLOCK, dtype=jnp.int32))
    out = jnp.transpose(out, (1, 0, 2, 3)).reshape(B, S, N_HEADS * D_V)
    return out @ w_o

def conformer_conv(h, w_pw1, b_pw1, w_dw, b_dw, ln_g, ln_b, w_pw2, b_pw2):
    u = h @ w_pw1 + b_pw1
    a, g = jnp.split(u, 2, axis=-1)
    u = a * jax.nn.sigmoid(g)
    u = lax.conv_general_dilated(u, w_dw[:, None, :], window_strides=(1,),
                                 padding=[(CONV_WIDTH - 1, 0)],
                                 dimension_numbers=('NWC', 'WIO', 'NWC'),
                                 feature_group_count=D_MODEL) + b_dw
    u = layernorm(u, ln_g, ln_b)
    u = jax.nn.silu(u)
    return u @ w_pw2 + b_pw2

def sqrelu_mlp(h, w_up, w_down):
    return jnp.square(jax.nn.relu(h @ w_up)) @ w_down

def setup_inputs(seed: int = 0) -> dict:
    key = jax.random.key(seed)
    ks = iter(jax.random.split(key, 32))
    nrm = lambda shape, scale: jax.random.normal(next(ks), shape, jnp.float32) * scale
    gain = lambda shape: 1.0 + 0.05 * jax.random.normal(next(ks), shape, jnp.float32)
    nA, nB, D = N_ATTN_LAYERS, N_CONV_LAYERS, D_MODEL
    return {
        "x": nrm((BATCH, SEQ, D), 1.0),
        "norm_mix": gain((DEPTH, D)),
        "norm_mlp": gain((DEPTH, D)),
        "norm_final": gain((D,)),
        "rel_bias": nrm((NUM_BUCKETS, N_HEADS), 0.5),
        "attn_w_in": nrm((nA, D, W_IN_COLS), D ** -0.5),
        "attn_q_norm": gain((nA, D_CQ)),
        "attn_kv_norm": gain((nA, D_CKV)),
        "attn_kidx_norm": gain((nA, IDX_DIM)),
        "attn_w_qidx": nrm((nA, D_CQ, IDX_HEADS * IDX_DIM), D_CQ ** -0.5),
        "attn_w_uq": nrm((nA, D_CQ, N_HEADS * D_NOPE), D_CQ ** -0.5),
        "attn_w_uk": nrm((nA, D_CKV, N_HEADS, D_NOPE), D_CKV ** -0.5),
        "attn_w_uv": nrm((nA, D_CKV, N_HEADS, D_V), D_CKV ** -0.5),
        "attn_w_o": nrm((nA, N_HEADS * D_V, D), (N_HEADS * D_V) ** -0.5),
        "conv_w_pw1": nrm((nB, D, 2 * D), D ** -0.5),
        "conv_b_pw1": nrm((nB, 2 * D), 0.02),
        "conv_w_dw": nrm((nB, CONV_WIDTH, D), CONV_WIDTH ** -0.5),
        "conv_b_dw": nrm((nB, D), 0.02),
        "conv_ln_g": gain((nB, D)),
        "conv_ln_b": nrm((nB, D), 0.02),
        "conv_w_pw2": nrm((nB, D, D), D ** -0.5),
        "conv_b_pw2": nrm((nB, D), 0.02),
        "mlp_w_up": nrm((DEPTH, D, D_FF), D ** -0.5),
        "mlp_w_down": nrm((DEPTH, D_FF, D), D_FF ** -0.5),
    }

def reference(x, norm_mix, norm_mlp, norm_final, rel_bias,
              attn_w_in, attn_q_norm, attn_kv_norm, attn_kidx_norm, attn_w_qidx,
              attn_w_uq, attn_w_uk, attn_w_uv, attn_w_o,
              conv_w_pw1, conv_b_pw1, conv_w_dw, conv_b_dw, conv_ln_g, conv_ln_b,
              conv_w_pw2, conv_b_pw2, mlp_w_up, mlp_w_down):
    for i in range(DEPTH):
        h = rmsnorm(x, norm_mix[i])
        j = i // 2
        if i % 2 == 0:
            x = x + dsa_mla(h, rel_bias, attn_w_in[j], attn_q_norm[j], attn_kv_norm[j],
                            attn_kidx_norm[j], attn_w_qidx[j], attn_w_uq[j], attn_w_uk[j],
                            attn_w_uv[j], attn_w_o[j])
        else:
            x = x + conformer_conv(h, conv_w_pw1[j], conv_b_pw1[j], conv_w_dw[j], conv_b_dw[j],
                                   conv_ln_g[j], conv_ln_b[j], conv_w_pw2[j], conv_b_pw2[j])
        h = rmsnorm(x, norm_mlp[i])
        x = x + sqrelu_mlp(h, mlp_w_up[i], mlp_w_down[i])
    return rmsnorm(x, norm_final)


_drawn_inputs = setup_inputs


def setup_inputs(seed=0):
    import zlib

    import numpy as np

    out = dict(_drawn_inputs(seed))
    spreads = {}
    factors = {'attn_kv_norm': 3.133,
     'conv_b_pw1': 6.557,
     'conv_b_dw': 3.889,
     'conv_ln_b': 7.811,
     'conv_b_pw2': 4.455,
     'conv_ln_g': 3.833}
    for name, (base, spread) in spreads.items():
        noise = np.random.default_rng([zlib.crc32(name.encode()), seed]).standard_normal(out[name].shape)
        drawn = base * np.exp(spread * noise) if base else spread * noise
        out[name] = __import__('jax').numpy.asarray(drawn.astype(out[name].dtype))
    for name, factor in factors.items():
        out[name] = (out[name] * factor).astype(out[name].dtype)
    return out
```

```python
from contextlib import ExitStack

import concourse.bass as bass
from concourse import mybir
from concourse.alu_op_type import AluOpType as ALU

F32 = mybir.dt.float32
F32R = mybir.dt.float32r
ACT = mybir.ActivationFunctionType

P = 128
SEQ = 512
D = 1024
KT = D // P
QB = SEQ // P
HEADS = 16
PAIRS = HEADS // 2
D_NOPE = 64
D_CQ, D_CKV = 256, 128
IDX_HEADS, IDX_DIM = 8, 64
W_IN = D_CQ + D_CKV + IDX_DIM + IDX_HEADS
TOPK = min(256, SEQ // 4)
NB = 32
TAPS = 31
ACT_TAPS = 13
DVE_TAPS = TAPS - ACT_TAPS
D_FF = 4 * D
EPS = 1e-6
MASKED = -1e30
NOT_YET = -3e38
TAKEN = -3.4e38

CHUNK = 16 * P
GROUPS = D_FF // P // 8
REV = SEQ + P

BLK = [0, 128, 384, 768, 1280]
SBLK = [None, 0, 256, 640, 1152]

V_NMIX, V_NMLP, V_BP1, V_BDW, V_LNG, V_LNB, V_BP2, V_NFIN, V_QN, V_KVN, V_KIN = (
    0, 16, 32, 48, 56, 64, 72, 80, 88, 90, 91)
V_ROWS = 92
V_DW = V_ROWS
V_ALL = V_DW + TAPS * KT

C_WIN, C_QIDX, C_WO = 0, 2, 3
C_MLP0 = C_WO + 4
C_PW1 = C_MLP0 + 8 * GROUPS
C_PW2 = C_PW1 + 8
C_MLP1 = C_PW2 + 4


UPD_MLP = (KT, KT + KT * GROUPS + KT)
UPD_FINAL = (0, KT * GROUPS, KT * GROUPS + KT, 2 * KT * GROUPS + KT)
HID_MLP = (0, 8 * GROUPS + KT)
CREDITS = 2


def tile_of(c):
    return 2 * (c - C_WO)


def raw_value(c):
    return sum(32 if C_PW1 <= d < C_PW2 else 16 for d in range(c % 2, c + 1, 2))


def program(nc, x, norm_mix, norm_mlp, norm_final, rel_bias, w_in, q_norm, kv_norm, kidx_norm, w_qidx, w_uq, w_uk,
            w_uv, w_o, w_pw1, b_pw1, w_dw, b_dw, ln_g, ln_b, w_pw2, b_pw2, w_up, w_down, bucket_rows, out):
    rev_dram = nc.dram_tensor("reversed_bias", (HEADS, P, REV), F32, kind="Internal").ap()
    ctx = ExitStack()
    with ctx:
        def sb(name, shape, dt=F32):
            return ctx.enter_context(nc.sbuf_tensor(name, shape, dt))

        def sem(name):
            return ctx.enter_context(nc.semaphore(name))

        xT = sb("xT", [P, KT, SEQ])
        movh = sb("movh", [P, KT, SEQ], F32R)
        movl = sb("movl", [P, KT, SEQ], F32R)
        hidh = sb("hidh", [P, KT, SEQ], F32R)
        hidl = sb("hidl", [P, KT, SEQ], F32R)
        raw = sb("raw", [P, 2, CHUNK])
        wh = sb("wh", [P, 2, CHUNK], F32R)
        wl = sb("wl", [P, 2, CHUNK], F32R)
        ch = sb("ch", [P, 4, SEQ], F32R)
        cl = sb("cl", [P, 4, SEQ], F32R)
        ptH = sb("ptH", [P, QB, SEQ], F32R)
        ptL = sb("ptL", [P, QB, SEQ], F32R)
        S1 = sb("S1", [P, 11264])
        ident = sb("ident", [P, P])
        ones = sb("ones", [P, P])
        vcol = sb("vcol", [P, V_ALL])
        small = sb("small", [P, 224])

        junk = S1[:, 0:4096].rearrange("p (i n) -> p i n", i=QB)
        vrow = S1[:, 4096:4480].rearrange("p (r n) -> p r n", r=3)
        relb = S1[0:NB, 4480:4480 + HEADS]
        revs = S1[0:HEADS, 4496:4496 + REV]
        brow = S1[0:NB, 5136:5136 + REV]
        proj = S1[:, 4096:4096 + QB * W_IN].rearrange("p (i n) -> p i n", i=QB)
        projn = S1[:, 5920:5920 + QB * 512].rearrange("p (i n) -> p i n", i=QB)
        xtok = S1[:, 7168:11264].rearrange("p (i n) -> p i n", i=QB)
        rawqkv = S1[:, 0:4096].rearrange("p (w n) -> p w n", w=4)
        mask = S1[:, 4096:5376]
        tb = S1[:, 5376:7424].rearrange("p (b e n) -> p b e n", b=2, e=2)
        score = S1[:, 7424:8576]
        relu_s = S1[:, 8576:9600].rearrange("p (b n) -> p b n", b=2)
        L = S1[:, 7424:9984].rearrange("p (b n) -> p b n", b=2)
        bm = S1[:, 9984:11264]
        def pair_parts(t):
            f = t[:, :, :].rearrange("p k n -> p (k n)")
            part = lambda o: f[:, o:o + 1024].rearrange("p (b n) -> p b n", b=2)
            return f[:, 0:512].rearrange("p (w n) -> p w n", w=4), part(512), part(1536), part(2560)
        swH, qH, kH, vH = pair_parts(movh)
        swL, qL, kL, vL = pair_parts(movl)
        rt = S1[:, 0:1024].rearrange("p (b n) -> p b n", b=2)
        sqt = S1[:, 1024:2048].rearrange("p (b n) -> p b n", b=2)
        dt = S1[:, 2048:3072].rearrange("p (b n) -> p b n", b=2)
        sqx = S1[:, 3072:4096].rearrange("p (b n) -> p b n", b=2)
        ss = S1[:, 4096:4608]
        rbc = S1[:, 4608:5120]
        GW = TAPS - 1 + SEQ
        RING = 4
        conv = S1[:, 0:4096].rearrange("p (k n) -> p k n", k=KT)
        glu = S1[:, 5120:5120 + RING * GW].rearrange("p (b n) -> p b n", b=RING)
        tg = S1[:, 7296:8320].rearrange("p (b n) -> p b n", b=2)
        partial = S1[:, 8320:9344].rearrange("p (b n) -> p b n", b=2)
        tapb = S1[:, 9344:10880].rearrange("p (b n) -> p b n", b=3)
        sg, mean = tapb[:, 0:2, :], tapb[:, 2, :]
        otok = S1[:, 5120:9216].rearrange("p (i n) -> p i n", i=QB)
        ft = S1[:, 9216:10240].rearrange("p (b n) -> p b n", b=2)

        ssq = small[:, 0:4]
        r1 = small[:, 4:8]
        n4 = small[:, 8:24].rearrange("p (a n) -> p a n", a=4)
        stat = small[:, 24:36]
        rs = small[:, 36:48]
        n12 = small[:, 48:96].rearrange("p (a n) -> p a n", a=4)
        wsc = small[:, 96:128]
        m8 = small[:, 128:136]
        rmax = small[:, 136:144].rearrange("p (b n) -> p b n", b=2)
        nmax = small[:, 144:152].rearrange("p (b n) -> p b n", b=2)
        n4f = small[:, 168:184].rearrange("p (a n) -> p a n", a=4)
        rfin = small[:, 184:188]
        sums = small[:, 152:160].rearrange("p (b n) -> p b n", b=2)
        rsum = small[:, 160:168].rearrange("p (b n) -> p b n", b=2)

        ps = ctx.enter_context(nc.psum_tensor("ps", [P, 8, 512], F32))

        x_in = [sem(f"x_in{i}") for i in range(QB)]
        raw_in = [sem(f"raw_in{b}") for b in range(2)]
        tb_in = [sem(f"tb_in{b}") for b in range(2)]
        vec_in, relb_in, qkv_in, rev_out, out_done = map(sem, ("vec_in", "relb_in", "qkv_in", "rev_out", "out_done"))
        w_hi, w_lo = map(sem, ("w_hi", "w_lo"))
        const_rdy, vt_rdy, vcol_rdy, rev_mm, rev_rdy = map(sem, ("const_rdy", "vt_rdy", "vcol_rdy", "rev_mm",
                                                                 "rev_rdy"))
        xt_rdy, xt_copied, mv_hi, mv_lo = map(sem, ("xt_rdy", "xt_copied", "mv_hi", "mv_lo"))
        ssq_rdy, inv_rdy, act_root, chain, r1_rdy = map(sem, ("ssq_rdy", "inv_rdy", "act_root", "chain", "r1_rdy"))
        pin_rdy, proj_rdy, stat_rdy, projn_rdy = map(sem, ("pin_rdy", "proj_rdy", "stat_rdy", "projn_rdy"))
        ct_rdy, c_hi, c_lo, qi_rdy, qi_hi, qi_lo = map(sem, ("ct_rdy", "c_hi", "c_lo", "qi_rdy", "qi_hi", "qi_lo"))
        sc_rdy, sc_relu, sc_acc, sc_causal, taken = map(sem, ("sc_rdy", "sc_relu", "sc_acc", "sc_causal", "taken"))
        mask0_rdy, mask_rdy = map(sem, ("mask0_rdy", "mask_rdy"))
        sw_hi, sw_lo, pr_rdy, pr_hi, pr_lo = map(sem, ("sw_hi", "sw_lo", "pr_rdy", "pr_hi", "pr_lo"))
        bm_rdy, lg_rdy, lg_done, nm_rdy, ex_done = map(sem, ("bm_rdy", "lg_rdy", "lg_done", "nm_rdy", "ex_done"))
        rc_seen, lg_seen = map(sem, ("rc_seen", "lg_seen"))
        rc_rdy, nr_done, pt_rdy, pt_hi, pt_lo = map(sem, ("rc_rdy", "nr_done", "pt_rdy", "pt_hi", "pt_lo"))
        pv_rdy, o_hi, o_lo = map(sem, ("pv_rdy", "o_hi", "o_lo"))
        mm_done, x_upd, sq_rdy, ss_add, ss_mm = map(sem, ("mm_done", "x_upd", "sq_rdy", "ss_add", "ss_mm"))
        relu_rdy, sqt_rdy, hid_hi, hid_lo, dt_rdy = map(sem, ("relu_rdy", "sqt_rdy", "hid_hi", "hid_lo", "dt_rdy"))
        pad_rdy, gate_read, sg_rdy, glu_rdy, conv_rdy = map(sem, ("pad_rdy", "gate_read", "sg_rdy", "glu_rdy",
                                                                  "conv_rdy"))
        tp_rdy, part_add, dve_taps = map(sem, ("tp_rdy", "part_add", "dve_taps"))
        mean_mm, dev_rdy, dsq_rdy, var_mm = map(sem, ("mean_mm", "dev_rdy", "dsq_rdy", "var_mm"))
        zt_rdy, zs_rdy, ft_rdy, ftt_rdy, ft_copied, fss_mm = map(sem, ("zt_rdy", "zs_rdy", "ft_rdy", "ftt_rdy",
                                                                       "ft_copied", "fss_mm"))
        rfin_rdy, o_dve, o_act = map(sem, ("rfin_rdy", "o_dve", "o_act"))

        def col(v, k=0):
            return vcol[:, v + k:v + k + 1]

        def flat(ap):
            return ap.rearrange("p a n -> p (a n)")

        def tap_products():
            for q in range(KT // 2):
                for s in range(ACT_TAPS):
                    for e in range(2):
                        yield 2 * q + e, s, e, 2 * (q * (ACT_TAPS - 1) + s - 1) + e

        block = ctx.enter_context(nc.Block())

        @block.sync
        def _(sp):
            def chunk_load(c, src):
                if c >= 2:
                    sp.wait_ge(w_lo, c - 1)
                k, n = src.shape[1], src.shape[2]
                sp.dma_start(raw[:, c % 2, 0:k * n].rearrange("p (k n) -> p k n", k=k), src).then_inc(
                    raw_in[c % 2], 16)

            x_v = x.rearrange("o (i p) d -> (o p) i d", p=P)
            for i in range(QB):
                sp.dma_start(xtok[:, i, :], x_v[:, i, :]).then_inc(x_in[i], 16)
            for v, src in ((V_NMIX, norm_mix), (V_NMLP, norm_mlp), (V_BP1, b_pw1), (V_BDW, b_dw), (V_LNG, ln_g),
                           (V_LNB, ln_b), (V_BP2, b_pw2), (V_NFIN, norm_final), (V_QN, q_norm), (V_KVN, kv_norm)):
                rows = src.rearrange("l (k p) -> (l k) p", p=P)
                sp.dma_start(vrow[v:v + rows.shape[0], 0, :], rows).then_inc(vec_in, 16)
            for half in range(2):
                sp.dma_start(vrow[V_KIN:V_KIN + 1, 0, 64 * half:64 * half + 64], kidx_norm).then_inc(vec_in, 16)
            dw_rows = w_dw.rearrange("o j (k p) -> (o j k) p", p=P)
            sp.dma_start(vrow[:, 1, :], dw_rows[0:P, :]).then_inc(vec_in, 16)
            sp.dma_start(vrow[0:TAPS * KT - P, 2, :], dw_rows[P:TAPS * KT, :]).then_inc(vec_in, 16)
            sp.dma_start(relb, rel_bias).then_inc(relb_in, 16)
            sp.dma_start(brow, bucket_rows).then_inc(relb_in, 16)
            w_in_v = w_in.rearrange("o (c k p) n -> (o p) c k n", p=P, k=4)
            for c in range(2):
                chunk_load(C_WIN + c, w_in_v[:, c])
            sp.wait_ge(rev_rdy, 2)
            for h in range(0, HEADS, 4):
                sp.dma_start(rev_dram[h:h + 4], revs[h:h + 4, :].unsqueeze(1).to_broadcast([4, P, REV])).then_inc(
                    rev_out, 16)
            chunk_load(C_QIDX, w_qidx.rearrange("o (k p) n -> (o p) k n", p=P))
            sp.wait_ge(stat_rdy, QB)
            sp.dma_start(rawqkv[:, 0:2, :], w_uq.rearrange("o (k p) n -> (o p) k n", p=P)).then_inc(qkv_in, 16)
            sp.dma_start(rawqkv[:, 2, :], w_uk.rearrange("o c h d -> (o c) (h d)")).then_inc(qkv_in, 16)
            sp.dma_start(rawqkv[:, 3, :], w_uv.rearrange("o c h d -> (o c) (h d)")).then_inc(qkv_in, 16)
            w_o_v = w_o.rearrange("o (k p) (c n) -> (o p) c k n", p=P, n=256)
            chunk_load(C_WO, w_o_v[:, 0])
            sp.wait_ge(rev_out, 64)
            sp.wait_ge(c_lo, 4)
            for p in range(PAIRS):
                b = p % 2
                if p >= 2:
                    sp.wait_ge(bm_rdy, 4 * (2 * (p - 2) + 2))
                for e in range(2):
                    src = rev_dram[2 * p + e]
                    src = bass.AP(src.tensor, src.offset + P - 1, [[REV - 1, P], [1, SEQ]])
                    sp.dma_start(tb[:, b, e, :], src).then_inc(tb_in[b], 16)
            for c in range(1, 4):
                chunk_load(C_WO + c, w_o_v[:, c])

            def mlp_loads(layer, c0):
                up_v = w_up.rearrange("l (k p) n -> l p k n", p=P)[layer]
                down_v = w_down.rearrange("l (g k p) n -> l p g k n", p=P, k=8)[layer]
                with sp.Fori(0, GROUPS) as g:
                    for j in range(8):
                        c = c0 + j
                        sp.wait_ge(w_lo, 8 * g + (c - 1))
                        if j < 4:
                            src = up_v[:, :, bass.ds(g * 1024 + j * 256, 256)]
                        else:
                            src = down_v[:, bass.ds(g, 1), :, (j - 4) * 256:(j - 3) * 256].rearrange(
                                "p o k n -> p (o k) n")
                        sp.dma_start(raw[:, c % 2, :].rearrange("p (k n) -> p k n", k=8), src).then_inc(
                            raw_in[c % 2], 16)

            mlp_loads(0, C_MLP0)
            pw1_v = w_pw1.rearrange("o (k p) (h c n) -> (o p) c k h n", p=P, h=2, n=P)
            for i in range(8):
                c = C_PW1 + i
                sp.wait_ge(w_lo, c - 1)
                for h in range(2):
                    sp.dma_start(raw[:, c % 2, :].rearrange("p (k h n) -> p k h n", k=KT, h=2)[:, :, h, :],
                                 pw1_v[:, i, :, h, :]).then_inc(raw_in[c % 2], 16)
            pw2_v = w_pw2.rearrange("o (k p) (c n) -> (o p) c k n", p=P, n=256)
            for c in range(4):
                chunk_load(C_PW2 + c, pw2_v[:, c])
            mlp_loads(1, C_MLP1)
            out_v = out.rearrange("o (i p) d -> (o p) i d", p=P)
            for i in range(QB):
                sp.wait_ge(o_dve if i < 2 else o_act, i % 2 + 1)
                sp.dma_start(out_v[:, i, :], otok[:, i, :]).then_inc(out_done, 16)
            sp.wait_ge(out_done, 16 * QB)

        @block.gpsimd
        def _(pool):
            pool.memset(ident[:, :], 0.0).then_inc(const_rdy, 1)
            pool.memset(ones[:, :], 1.0).then_inc(const_rdy, 1)
            pool.wait_ge(const_rdy, 2)
            pool.affine_select(out=ident[:, :], in_=ident[:, :], compare_op=ALU.not_equal, fill=1.0, base=0,
                               pattern=[[-1, P]], channel_multiplier=1).then_inc(const_rdy, 1)
            pool.wait_ge(projn_rdy, 1)
            pool.memset(mask[:, 0:P], 0.0).then_inc(mask0_rdy, 1)
            pool.wait_ge(mask0_rdy, 1)
            pool.affine_select(out=mask[:, 0:P], in_=mask[:, 0:P], compare_op=ALU.is_ge, fill=MASKED, base=0,
                               pattern=[[-1, P]], channel_multiplier=1).then_inc(mask0_rdy, 1)
            for i in range(1, QB):
                pool.wait_ge(sc_acc, IDX_HEADS * i)
                diag = score[:, SBLK[i + 1] - P:SBLK[i + 1]]
                pool.affine_select(out=diag, in_=diag, compare_op=ALU.is_ge, fill=NOT_YET, base=0,
                                   pattern=[[-1, P]], channel_multiplier=1).then_inc(sc_causal, 1)

            def bias_and_mask(n, hh, loaded):
                b, e = hh // 2 % 2, hh % 2
                pool.wait_ge(tb_in[b], loaded)
                for i in range(QB):
                    if not (isinstance(n, int) and n == 0):
                        pool.wait_ge(lg_done, 4 * n + (i - 3))
                    pool.tensor_tensor(bm[:, BLK[i]:BLK[i + 1]], tb[:, b, e, SEQ - P * (i + 1):SEQ],
                                       mask[:, BLK[i]:BLK[i + 1]], ALU.add).then_inc(bm_rdy, 1)

            def normalise(n, hh):
                pool.wait_ge(rc_rdy, n + 1)
                pool.sem_inc(rc_seen, 1)
                for i in range(QB):
                    part = L[:, hh % 2, BLK[i]:BLK[i + 1]]
                    pool.tensor_scalar(part, part, rsum[:, hh % 2, i:i + 1], 1.0, ALU.mult, ALU.mult).then_inc(
                        nr_done, 1)

            pool.wait_ge(mask0_rdy, 2)
            pool.wait_ge(mask_rdy, QB - 1)
            bias_and_mask(0, 0, 32)
            bias_and_mask(1, 1, 32)
            normalise(0, 0)
            bias_and_mask(2, 2, 32)

            def head_step(g, hh):
                n, last = 4 * g + hh, isinstance(g, int)
                if not last or hh < 3:
                    normalise(n + 1, hh + 1)
                if not last or hh < 1:
                    bias_and_mask(n + 3, (hh + 3) % 4, 32 * g + 32 * ((hh + 3) // 4 + 1))

            with pool.Fori(0, HEADS // 4 - 1) as g:
                for hh in range(4):
                    head_step(g, hh)
            for hh in range(4):
                head_step(HEADS // 4 - 1, hh)

            def sum_squares(f):
                for m in range(KT):
                    pool.wait_ge(sq_rdy, KT * f + m + 1)
                    if m == 0:
                        pool.tensor_scalar(ss, sqx[:, 0, :], 1.0, 1.0, ALU.mult, ALU.mult).then_inc(ss_add, 1)
                    else:
                        pool.wait_ge(ss_add, KT * f + m)
                        pool.tensor_tensor(ss, ss, sqx[:, m % 2, :], ALU.add).then_inc(ss_add, 1)

            sum_squares(0)
            for b in range(RING):
                pool.memset(glu[:, b, 0:TAPS - 1], 0.0).then_inc(pad_rdy, 1)
            pool.wait_ge(ss_mm, 1)
            sum_squares(1)
            for i, s, e, k in tap_products():
                if s:
                    pool.wait_ge(tp_rdy, k + 2 * (i // 2 + 1) + 1)
                    if s > 1:
                        pool.wait_ge(part_add, k - 1)
                    pool.tensor_tensor(partial[:, e, :], partial[:, e, :], tapb[:, k % 3, :], ALU.add).then_inc(part_add, 1)
            pool.wait_ge(ss_mm, 2)
            sum_squares(2)
            pool.wait_ge(ss_mm, 3)
            sum_squares(3)

        @block.scalar
        def _(act):
            def split_hi(c, n=CHUNK):
                act.wait_ge(raw_in[c % 2], raw_value(c))
                if c in (C_QIDX, C_WO):
                    act.wait_ge(pin_rdy, QB)
                elif c == C_WO + 1:
                    act.wait_ge(qi_rdy, 4)
                elif c > C_WO + 1:
                    act.wait_ge(mm_done, tile_of(c) - 2)
                act.activation(wh[:, c % 2, 0:n], raw[:, c % 2, 0:n], ACT.Copy).then_inc(w_hi, 1)

            def square_x(f, m):
                if f or m >= 2:
                    act.wait_ge(ss_add, KT * f + m - 1)
                act.activation(sqx[:, m % 2, :], xT[:, m, :], ACT.Square).then_inc(sq_rdy, 1)

            def finish_x(f, m, gain):
                act.wait_ge(x_upd, UPD_FINAL[f] + m + 1)
                act.activation(movh[:, m, :], xT[:, m, :], ACT.Copy, scale=gain).then_inc(mv_hi, 1)
                square_x(f, m)

            def root(dst, src, n):
                act.wait_ge(inv_rdy, n)
                act.activation(dst, src, ACT.Sqrt).then_inc(act_root, 1)

            split_hi(C_WIN, 4 * W_IN)
            split_hi(C_WIN + 1, 4 * W_IN)
            act.wait_ge(vcol_rdy, 1)
            for i in range(QB):
                act.wait_ge(x_in[i], 16)
                act.activation(junk[:, i, :], xtok[:, i, :], ACT.Square, accum_out=ssq[:, i:i + 1]).then_inc(
                    ssq_rdy, 1)
            for k in range(KT):
                act.wait_ge(xt_copied, k + 1)
                act.activation(movh[:, k, :], xT[:, k, :], ACT.Copy, scale=col(V_NMIX, k)).then_inc(mv_hi, 1)
            root(n4[:, 2, :], n4[:, 1, :], 1)
            act.wait_ge(r1_rdy, 1)
            act.wait_ge(rev_out, 64)
            for i in range(QB):
                act.wait_ge(pin_rdy, i + 1)
                act.activation(proj[:, i, :], ps[:, 4 + i, 0:W_IN], ACT.Copy, scale=r1[:, i:i + 1]).then_inc(
                    proj_rdy, 1)
            for i in range(QB):
                act.wait_ge(proj_rdy, i + 1)
                for s, (a, b) in enumerate(((0, 256), (256, 384), (384, 448))):
                    last = act.activation(junk[:, i, a:b], proj[:, i, a:b], ACT.Square,
                                          accum_out=stat[:, 4 * s + i:4 * s + i + 1])
                last.then_inc(stat_rdy, 1)
            root(n12[:, 2, :], n12[:, 1, :], 2)
            split_hi(C_QIDX, 1024)
            for t in range(4):
                act.wait_ge(ct_rdy, t + 1)
                act.activation(ch[:, t, :], ps[:, t, :], ACT.Copy, scale=col(V_QN, t)).then_inc(c_hi, 1)
            for t in range(4):
                act.wait_ge(qi_rdy, t + 1)
                act.activation(hidh[:, t, :], ps[:, 4 + t, :], ACT.Copy).then_inc(qi_hi, 1)
            s = 0
            for i in range(1, QB):
                for h in range(IDX_HEADS):
                    act.wait_ge(sc_rdy, s + 1)
                    if s >= 2:
                        act.wait_ge(sc_acc, s - 1)
                    act.activation(relu_s[:, s % 2, 0:P * (i + 1)], ps[:, s % 4, 0:P * (i + 1)],
                                   ACT.Relu).then_inc(sc_relu, 1)
                    s += 1

            def stage_hi(src):
                act.activation(swH, src, ACT.Copy).then_inc(sw_hi, 1)

            def pair_hi(p, b, which):
                act.wait_ge(pr_rdy, 3 * p + (which + 1))
                act.activation((qH, kH, vH)[which][:, b, :], ps[:, which % 2, :], ACT.Copy,
                               scale=D_NOPE ** -0.5 if which == 0 else 1.0).then_inc(pr_hi, 1)

            def exponentials(n, hh):
                act.wait_ge(nm_rdy, n + 1)
                for i in range(QB):
                    part = L[:, hh % 2, BLK[i]:BLK[i + 1]]
                    act.activation(part, part, ACT.Exp, bias=nmax[:, hh % 2, i:i + 1],
                                   accum_out=sums[:, hh % 2, i:i + 1]).then_inc(ex_done, 1)

            act.wait_ge(qkv_in, 48)
            for p in range(2):
                if p:
                    act.wait_ge(pr_rdy, 3)
                stage_hi(rawqkv[:, :, P * p:P * p + P])
                for which in range(3):
                    pair_hi(p, p, which)
            exponentials(0, 0)

            def head_step(g, hh):
                n, last = 4 * g + hh, isinstance(g, int)
                ahead = hh % 2 and not last
                p, b = 2 * g + (hh + 3) // 2, (hh + 3) // 2 % 2
                if ahead:
                    act.wait_ge(pr_rdy, 3 * p)
                    stage_hi(rawqkv[:, :, bass.ds(p * P, P)])
                for i in range(QB):
                    act.wait_ge(pt_rdy, 4 * n + (i + 1))
                    act.activation(ptH[:, 0:i + 1, P * i:P * i + P],
                                   ps[:, 4 + i % 2, 0:P * (i + 1)].rearrange("p (j n) -> p j n", n=P),
                                   ACT.Copy).then_inc(pt_hi, 1)
                if not last or hh < 3:
                    exponentials(n + 1, hh + 1)
                if ahead:
                    pair_hi(p, b, 0)
                    pair_hi(p, b, 1)
                e, p_out = hh % 2, 2 * g + hh // 2
                half = hidh[64 * e:64 * e + 64, p_out, :] if last else flat(
                    hidh[64 * e:64 * e + 64, bass.ds(p_out, 1), :])
                act.wait_ge(pv_rdy, n + 1)
                act.activation(half, ps[64 * e:64 * e + 64, 6 + e, :], ACT.Copy).then_inc(o_hi, 1)
                if ahead:
                    pair_hi(p, b, 2)

            with act.Fori(0, HEADS // 4 - 1) as g:
                for hh in range(4):
                    head_step(g, hh)
            for hh in range(4):
                head_step(HEADS // 4 - 1, hh)

            split_hi(C_WO)
            split_hi(C_WO + 1)
            for c in range(4):
                if c:
                    split_hi(C_WO + c + 1)
                for m in (2 * c, 2 * c + 1):
                    finish_x(0, m, col(V_NMLP, m))

            def mlp(layer, c0, finish):
                t0, r0, h0 = tile_of(c0), 8 * GROUPS * layer, HID_MLP[layer]

                def group(g, last):
                    for j in range(8):
                        c = c0 + j + 1
                        if not (last and j == 7):
                            act.wait_ge(raw_in[c % 2], 64 * g + raw_value(c))
                            act.wait_ge(mm_done, 16 * g + (t0 + 2 * j))
                            act.activation(wh[:, c % 2, :], raw[:, c % 2, :], ACT.Copy).then_inc(w_hi, 1)
                        elif layer == 0:
                            split_hi(C_PW1)
                        for m in (2 * j, 2 * j + 1):
                            if j < 4:
                                act.wait_ge(mm_done, 16 * g + (t0 + m + 1))
                                act.wait_ge(hid_lo, 8 * g + (CREDITS + h0 + m - 1))
                                act.activation(rt[:, m % 2, :], ps[:, (t0 + m) % 4, :],
                                               ACT.Relu).then_inc(relu_rdy, 1)
                                act.wait_ge(relu_rdy, 8 * g + (r0 + m + 1))
                                act.activation(hidh[:, m, :], rt[:, m % 2, :], ACT.Square).then_inc(hid_hi, 1)
                            elif last:
                                finish(m - 8)

                with act.Fori(0, GROUPS - 1) as g:
                    group(g, False)
                group(GROUPS - 1, True)

            mlp(0, C_MLP0, lambda m: finish_x(1, m, col(V_NMIX, KT + m)))

            split_hi(C_PW1 + 1)
            root(sg[:, 1, :], sg[:, 0, :], 3)

            def sigmoids(i):
                for h in range(2):
                    act.wait_ge(gate_read, 2 * (i + h) + 2)
                    act.activation(tg[:, h, :], tg[:, h, :], ACT.Sigmoid, bias=col(V_BP1, KT + i + h)).then_inc(
                        sg_rdy, 1)

            split_hi(C_PW1 + 2)
            sigmoids(0)
            split_hi(C_PW1 + 3)
            for i, s, e, k in tap_products():
                if s == 0:
                    act.wait_ge(glu_rdy, i + 1)
                    if i >= 2:
                        act.wait_ge(conv_rdy, i - 1)
                    dst = partial[:, e, :]
                else:
                    if k >= 3:
                        act.wait_ge(part_add, k - 2)
                    dst = tapb[:, k % 3, :]
                if k < 3:
                    act.wait_ge(r1_rdy, 2)
                j = DVE_TAPS + s
                act.activation(dst, glu[:, i % RING, j:j + SEQ], ACT.Copy, scale=col(V_DW, KT * j + i)).then_inc(
                    tp_rdy, 1)
                if e == 1 and i < KT - 1 and s == ACT_TAPS - 4:
                    split_hi(C_PW1 + i + 3)
                if e == 1 and i < KT - 1 and s == ACT_TAPS - 1:
                    sigmoids(i + 1)
                    split_hi(C_PW1 + i + 4)
            for m in range(KT):
                act.wait_ge(dev_rdy, m + 1)
                if m >= 2:
                    act.wait_ge(var_mm, m - 1)
                act.activation(tg[:, m % 2, :], conv[:, m, :], ACT.Square).then_inc(dsq_rdy, 1)
            root(sg[:, 1, :], sg[:, 0, :], 4)
            act.wait_ge(r1_rdy, 3)
            z0 = HID_MLP[1] - KT
            for m in range(KT):
                act.wait_ge(zt_rdy, m + 1)
                if m >= 2:
                    act.wait_ge(hid_lo, CREDITS + z0 + m - 1)
                act.activation(sg[:, m % 2, :], tg[:, m % 2, :], ACT.Silu, scale=col(V_LNG, m),
                               bias=col(V_LNB, m)).then_inc(zs_rdy, 1)
                act.wait_ge(zs_rdy, m + 1)
                act.activation(hidh[:, m, :], sg[:, m % 2, :], ACT.Copy).then_inc(hid_hi, 1)
            for c in range(4):
                if c:
                    split_hi(C_PW2 + c + 1)
                for m in (2 * c, 2 * c + 1):
                    finish_x(2, m, col(V_NMLP, KT + m))

            def copy_out(m):
                act.wait_ge(ftt_rdy, m + 1)
                act.activation(otok[:, :, P * m:P * m + P], ps[:, 5 + m % 2, :].rearrange("p (i n) -> p i n", n=P),
                               ACT.Copy).then_inc(ft_copied, 1)

            def finish_last(m):
                act.wait_ge(x_upd, UPD_FINAL[3] + m + 1)
                square_x(3, m)
                if m:
                    copy_out(m - 1)

            mlp(1, C_MLP1, finish_last)
            copy_out(KT - 1)
            root(n4f[:, 2, :], n4f[:, 1, :], 5)
            act.wait_ge(rfin_rdy, 1)
            act.wait_ge(ft_copied, KT)
            for i in range(2, QB):
                act.activation(otok[:, i, :], otok[:, i, :], ACT.Copy, scale=rfin[:, i:i + 1]).then_inc(o_act, 1)

        @block.vector
        def _(dve):
            links = [0]

            def link(ins):
                links[0] += 1
                ins.then_inc(chain, 1)
                dve.wait_ge(chain, links[0])

            def split_lo(c, n=CHUNK):
                dve.wait_ge(w_hi, c + 1)
                dve.tensor_tensor(wl[:, c % 2, 0:n], raw[:, c % 2, 0:n], wh[:, c % 2, 0:n].bitcast(F32),
                                  ALU.subtract).then_inc(w_lo, 1)

            def inverse_root(v, inv, y, t, r, n):
                dve.reciprocal(inv, v).then_inc(inv_rdy, 1)
                dve.wait_ge(act_root, n)
                link(dve.tensor_tensor(t, y, y, ALU.mult))
                link(dve.tensor_tensor(t, t, v, ALU.mult))
                link(dve.tensor_scalar(t, t, -0.5, 1.5, ALU.mult, ALU.add))
                return dve.tensor_tensor(r, y, t, ALU.mult)

            def x_lo(n, m, gain):
                dve.wait_ge(mv_hi, n + 1)
                dve.scalar_tensor_tensor(movl[:, m, :], xT[:, m, :], gain, movh[:, m, :].bitcast(F32), ALU.mult,
                                         ALU.subtract).then_inc(mv_lo, 1)

            dve.sem_inc(hid_lo, CREDITS)
            dve.sem_inc(pt_lo, CREDITS)
            dve.sem_inc(o_lo, CREDITS)
            dve.wait_ge(vt_rdy, 1)
            dve.tensor_copy(vcol[:, :], ps[:, 7, 0:V_ALL]).then_inc(vcol_rdy, 1)
            dve.wait_ge(rev_mm, 1)
            for h in range(2):
                dve.tensor_copy(revs[:, 320 * h:320 * h + 320], ps[0:HEADS, 5 + h, 0:320]).then_inc(rev_rdy, 1)
            dve.wait_ge(vcol_rdy, 1)
            split_lo(C_WIN, 4 * W_IN)
            split_lo(C_WIN + 1, 4 * W_IN)
            for k in range(KT):
                dve.wait_ge(xt_rdy, k + 1)
                dve.tensor_copy(xT[:, k, :], ps[:, k % 4, :]).then_inc(xt_copied, 1)
                if k:
                    x_lo(k - 1, k - 1, col(V_NMIX, k - 1))
            x_lo(KT - 1, KT - 1, col(V_NMIX, KT - 1))
            dve.wait_ge(ssq_rdy, QB)
            link(dve.tensor_scalar(n4[:, 0, :], ssq, 1.0 / D, EPS, ALU.mult, ALU.add))
            inverse_root(n4[:, 0, :], n4[:, 1, :], n4[:, 2, :], n4[:, 3, :], r1, 1).then_inc(r1_rdy, 1)
            dve.wait_ge(stat_rdy, QB)
            for s, n in enumerate((D_CQ, D_CKV, IDX_DIM)):
                link(dve.tensor_scalar(n12[:, 0, 4 * s:4 * s + 4], stat[:, 4 * s:4 * s + 4], 1.0 / n, EPS, ALU.mult,
                                       ALU.add))
            link(inverse_root(n12[:, 0, :], n12[:, 1, :], n12[:, 2, :], n12[:, 3, :], rs, 2))
            for i in range(QB):
                dve.tensor_scalar(projn[:, i, 0:256], proj[:, i, 0:256], rs[:, i:i + 1], None, ALU.mult)
                dve.tensor_scalar(projn[:, i, 256:384], proj[:, i, 256:384], rs[:, 4 + i:5 + i], None, ALU.mult)
                for h in range(2):
                    dve.tensor_scalar(projn[:, i, 384 + 64 * h:448 + 64 * h], proj[:, i, 384:448],
                                      rs[:, 8 + i:9 + i], None, ALU.mult)
                last = dve.tensor_scalar(wsc[:, 8 * i:8 * i + 8], proj[:, i, 448:456],
                                         IDX_HEADS ** -0.5 * IDX_DIM ** -0.5, None, ALU.mult)
            last.then_inc(projn_rdy, 1)
            split_lo(C_QIDX, 1024)
            for t in range(4):
                dve.wait_ge(c_hi, t + 1)
                dve.scalar_tensor_tensor(cl[:, t, :], ps[:, t, :], col(V_QN, t), ch[:, t, :].bitcast(F32), ALU.mult,
                                         ALU.subtract).then_inc(c_lo, 1)
            for t in range(4):
                dve.wait_ge(qi_hi, t + 1)
                dve.tensor_tensor(hidl[:, t, :], ps[:, 4 + t, :], hidh[:, t, :].bitcast(F32), ALU.subtract).then_inc(
                    qi_lo, 1)
            dve.wait_ge(projn_rdy, 1)
            s = 0
            for i in range(1, QB):
                for h in range(IDX_HEADS):
                    part, w = score[:, SBLK[i]:SBLK[i + 1]], wsc[:, 8 * i + h:8 * i + h + 1]
                    dve.wait_ge(sc_relu, s + 1)
                    if h == 0:
                        dve.tensor_scalar(part, relu_s[:, s % 2, 0:P * (i + 1)], w, None, ALU.mult).then_inc(sc_acc, 1)
                    else:
                        dve.wait_ge(sc_acc, s)
                        dve.scalar_tensor_tensor(part, relu_s[:, s % 2, 0:P * (i + 1)], w, part, ALU.mult,
                                                 ALU.add).then_inc(sc_acc, 1)
                    s += 1

            def stage_lo(p, src):
                dve.wait_ge(sw_hi, p + 1)
                dve.tensor_tensor(swL, src, swH.bitcast(F32), ALU.subtract).then_inc(sw_lo, 1)

            def pair_lo(p, b, which):
                dve.wait_ge(pr_hi, 3 * p + (which + 1))
                dve.scalar_tensor_tensor((qL, kL, vL)[which][:, b, :], ps[:, which % 2, :],
                                         D_NOPE ** -0.5 if which == 0 else 1.0,
                                         (qH, kH, vH)[which][:, b, :].bitcast(F32),
                                         ALU.mult, ALU.subtract).then_inc(pr_lo, 1)

            for p in range(2):
                stage_lo(p, rawqkv[:, :, P * p:P * p + P])
                for which in range(3):
                    pair_lo(p, p, which)

            n = 0
            for i in range(1, QB):
                part = score[:, SBLK[i]:SBLK[i + 1]]
                dve.wait_ge(sc_causal, i)
                for _ in range(TOPK // 8):
                    dve.max(m8, part).then_inc(taken, 1)
                    dve.wait_ge(taken, n + 1)
                    dve.match_replace(part, m8, part, TAKEN).then_inc(taken, 1)
                    dve.wait_ge(taken, n + 2)
                    n += 2
                dve.tensor_scalar(mask[:, BLK[i]:BLK[i + 1]], part, TAKEN, MASKED, ALU.not_equal,
                                  ALU.mult).then_inc(mask_rdy, 1)
            dve.wait_ge(mask_rdy, QB - 1)

            def logits(n, hh):
                b = hh % 2
                if not (isinstance(n, int) and n < 2):
                    dve.wait_ge(pt_rdy, 4 * n - 4)
                for i in range(QB):
                    dve.wait_ge(bm_rdy, 4 * n + (i + 1))
                    dve.wait_ge(lg_rdy, 4 * n + (i + 1))
                    dve.sem_inc(lg_seen, 1)
                    dve.tensor_tensor_reduce(L[:, b, BLK[i]:BLK[i + 1]], ps[:, 2 + i % 2, 0:P * (i + 1)],
                                             bm[:, BLK[i]:BLK[i + 1]], 1.0, -3e38, ALU.add, ALU.max,
                                             rmax[:, b, i:i + 1]).then_inc(lg_done, 1)
                dve.wait_ge(lg_done, 4 * n + 4)
                dve.tensor_scalar(nmax[:, b, :], rmax[:, b, :], -1.0, None, ALU.mult).then_inc(nm_rdy, 1)

            def reciprocals(n, hh):
                dve.wait_ge(ex_done, 4 * n + 4)
                dve.reciprocal(rsum[:, hh % 2, :], sums[:, hh % 2, :]).then_inc(rc_rdy, 1)

            logits(0, 0)
            logits(1, 1)
            reciprocals(0, 0)

            def head_step(g, hh):
                n, last = 4 * g + hh, isinstance(g, int)
                ahead = hh % 2 and not last
                p, b = 2 * g + (hh + 3) // 2, (hh + 3) // 2 % 2
                if ahead:
                    stage_lo(p, rawqkv[:, :, bass.ds(p * P, P)])
                for i in range(QB):
                    dve.wait_ge(pt_hi, 4 * n + (i + 1))
                    dve.tensor_tensor(ptL[:, 0:i + 1, P * i:P * i + P],
                                      ps[:, 4 + i % 2, 0:P * (i + 1)].rearrange("p (j n) -> p j n", n=P),
                                      ptH[:, 0:i + 1, P * i:P * i + P].bitcast(F32), ALU.subtract).then_inc(pt_lo, 1)
                if not last or hh < 2:
                    logits(n + 2, hh + 2)
                if not last or hh < 3:
                    reciprocals(n + 1, hh + 1)
                if ahead:
                    pair_lo(p, b, 0)
                    pair_lo(p, b, 1)
                e, p_out = hh % 2, 2 * g + hh // 2
                half = lambda t: t[64 * e:64 * e + 64, p_out, :] if last else flat(
                    t[64 * e:64 * e + 64, bass.ds(p_out, 1), :])
                dve.wait_ge(o_hi, n + 1)
                dve.tensor_tensor(half(hidl), ps[64 * e:64 * e + 64, 6 + e, :], half(hidh).bitcast(F32),
                                  ALU.subtract).then_inc(o_lo, 1)
                if ahead:
                    pair_lo(p, b, 2)

            with dve.Fori(0, HEADS // 4 - 1) as g:
                for hh in range(4):
                    head_step(g, hh)
            for hh in range(4):
                head_step(HEADS // 4 - 1, hh)

            split_lo(C_WO)
            split_lo(C_WO + 1)
            for c in range(4):
                if c:
                    split_lo(C_WO + c + 1)
                for m in (2 * c, 2 * c + 1):
                    dve.wait_ge(mm_done, m + 1)
                    dve.tensor_tensor(xT[:, m, :], ps[:, m % 4, :], xT[:, m, :], ALU.add).then_inc(x_upd, 1)
                    dve.wait_ge(x_upd, m + 1)
                    x_lo(KT + m, m, col(V_NMLP, m))

            def mlp(layer, c0, finish):
                t0, r0, h0, u0 = tile_of(c0), 8 * GROUPS * layer, HID_MLP[layer], UPD_MLP[layer]
                dve.wait_ge(ss_mm, 2 * layer + 1)
                link(dve.tensor_scalar(rbc, ps[:, 4, :], 1.0 / D, EPS, ALU.mult, ALU.add))
                link(dve.reciprocal(rbc, rbc))

                def group(g, last):
                    for j in range(8):
                        c = c0 + j + 1
                        if not (last and j == 7):
                            dve.wait_ge(w_hi, 8 * g + (c + 1))
                            dve.tensor_tensor(wl[:, c % 2, :], raw[:, c % 2, :], wh[:, c % 2, :].bitcast(F32),
                                              ALU.subtract).then_inc(w_lo, 1)
                        elif layer == 0:
                            split_lo(C_PW1)
                        for m in (2 * (j % 4), 2 * (j % 4) + 1):
                            if j < 4:
                                dve.wait_ge(relu_rdy, 8 * g + (r0 + m + 1))
                                dve.wait_ge(hid_lo, 8 * g + (CREDITS + h0 + m - 1))
                                dve.tensor_tensor(sqt[:, m % 2, :], rt[:, m % 2, :], rt[:, m % 2, :],
                                                  ALU.mult).then_inc(sqt_rdy, 1)
                                dve.wait_ge(sqt_rdy, 8 * g + (r0 + m + 1))
                                dve.wait_ge(hid_hi, 8 * g + (h0 + m + 1))
                                dve.tensor_tensor(hidl[:, m, :], sqt[:, m % 2, :], hidh[:, m, :].bitcast(F32),
                                                  ALU.subtract).then_inc(hid_lo, 1)
                            else:
                                dve.wait_ge(mm_done, 16 * g + (t0 + 8 + m + 1))
                                dve.wait_ge(x_upd, 8 * g + (u0 + m - 1))
                                dve.tensor_tensor(dt[:, m % 2, :], ps[:, (t0 + m) % 4, :], rbc,
                                                  ALU.mult).then_inc(dt_rdy, 1)
                                dve.wait_ge(dt_rdy, 8 * g + (r0 + m + 1))
                                dve.tensor_tensor(xT[:, m, :], xT[:, m, :], dt[:, m % 2, :], ALU.add).then_inc(
                                    x_upd, 1)
                                if last:
                                    finish(m)

                with dve.Fori(0, GROUPS - 1) as g:
                    group(g, False)
                group(GROUPS - 1, True)

            mlp(0, C_MLP0, lambda m: x_lo(2 * KT + m, m, col(V_NMIX, KT + m)))

            split_lo(C_PW1 + 1)
            dve.wait_ge(ss_mm, 2)
            link(dve.tensor_scalar(rbc, ps[:, 4, :], 1.0 / D, EPS, ALU.mult, ALU.add))
            inverse_root(rbc, sg[:, 0, :], sg[:, 1, :], sg[:, 0, :], rbc, 3).then_inc(r1_rdy, 1)
            dve.wait_ge(r1_rdy, 2)
            dve.wait_ge(pad_rdy, RING)
            t0 = tile_of(C_PW1)

            def gates(i):
                for h in range(2):
                    u = glu[:, (i + h) % RING, TAPS - 1:GW]
                    for gate, dst in enumerate((u, tg[:, h, :])):
                        n = 2 * (i + h) + gate
                        dve.wait_ge(mm_done, t0 + n + 1)
                        if i >= 2:
                            dve.wait_ge(glu_rdy, i)
                        if i >= RING:
                            dve.wait_ge(conv_rdy, i - 2)
                        dve.tensor_tensor(dst, ps[:, (t0 + n) % 4, :], rbc, ALU.mult).then_inc(gate_read, 1)
                split_lo(C_PW1 + i + 2)

            def gated(i):
                for h in range(2):
                    u = glu[:, (i + h) % RING, TAPS - 1:GW]
                    dve.wait_ge(sg_rdy, i + h + 1)
                    dve.wait_ge(gate_read, 2 * (i + h) + 1)
                    dve.scalar_tensor_tensor(u, u, col(V_BP1, i + h), tg[:, h, :], ALU.add, ALU.mult).then_inc(
                        glu_rdy, 1)

            def add_partial(i):
                dve.wait_ge(dve_taps, DVE_TAPS * (i + 2))
                for h in range(2):
                    dve.wait_ge(part_add, (ACT_TAPS - 1) * (i + 2) - 1 + h)
                    dve.tensor_tensor(conv[:, i + h, :], conv[:, i + h, :], partial[:, h, :], ALU.add).then_inc(
                        conv_rdy, 1)

            gates(0)
            gated(0)
            for i in range(0, KT, 2):
                for j in range(DVE_TAPS):
                    if j == 3:
                        split_lo(C_PW1 + i + 3)
                    if j == DVE_TAPS - 5 and i + 2 < KT:
                        gates(i + 2)
                    for h in range(2):
                        m, n = i + h, DVE_TAPS * i + 2 * j + h
                        u = glu[:, m % RING, j:j + SEQ]
                        if j == 0:
                            dve.wait_ge(glu_rdy, m + 1)
                            ins = dve.tensor_scalar(conv[:, m, :], u, col(V_DW, m), col(V_BDW, m), ALU.mult, ALU.add)
                        else:
                            dve.wait_ge(dve_taps, n - 1)
                            ins = dve.scalar_tensor_tensor(conv[:, m, :], u, col(V_DW, KT * j + m), conv[:, m, :],
                                                           ALU.mult, ALU.add)
                        ins.then_inc(dve_taps, 1)
                if i + 2 < KT:
                    gated(i + 2)
                add_partial(i)
            dve.wait_ge(mean_mm, 1)
            link(dve.tensor_scalar(mean, ps[:, 5, :], 1.0 / D, None, ALU.mult))
            dve.wait_ge(conv_rdy, KT)
            for m in range(KT):
                dve.tensor_tensor(conv[:, m, :], conv[:, m, :], mean, ALU.subtract).then_inc(dev_rdy, 1)
            dve.wait_ge(var_mm, KT)
            dve.wait_ge(dev_rdy, KT)
            link(dve.tensor_scalar(rbc, ps[:, 6, :], 1.0 / D, EPS, ALU.mult, ALU.add))
            inverse_root(rbc, sg[:, 0, :], sg[:, 1, :], sg[:, 0, :], rbc, 4).then_inc(r1_rdy, 1)
            dve.wait_ge(r1_rdy, 3)
            z0 = HID_MLP[1] - KT

            def z_lo(m):
                dve.wait_ge(hid_hi, z0 + m + 1)
                dve.tensor_tensor(hidl[:, m, :], sg[:, m % 2, :], hidh[:, m, :].bitcast(F32),
                                  ALU.subtract).then_inc(hid_lo, 1)

            for m in range(KT):
                if m >= 2:
                    dve.wait_ge(zs_rdy, m - 1)
                dve.tensor_tensor(tg[:, m % 2, :], conv[:, m, :], rbc, ALU.mult).then_inc(zt_rdy, 1)
                if m:
                    z_lo(m - 1)
            z_lo(KT - 1)
            t0, u0 = tile_of(C_PW2), UPD_FINAL[2]
            for c in range(4):
                if c:
                    split_lo(C_PW2 + c + 1)
                for m in (2 * c, 2 * c + 1):
                    dve.wait_ge(mm_done, t0 + m + 1)
                    dve.scalar_tensor_tensor(xT[:, m, :], ps[:, (t0 + m) % 4, :], col(V_BP2, m), xT[:, m, :], ALU.add,
                                             ALU.add).then_inc(x_upd, 1)
                    dve.wait_ge(x_upd, u0 + m + 1)
                    x_lo(3 * KT + m, m, col(V_NMLP, KT + m))

            def finish_last(m):
                dve.wait_ge(x_upd, UPD_FINAL[3] + m + 1)
                if m >= 2:
                    dve.wait_ge(ftt_rdy, m - 1)
                dve.tensor_scalar(ft[:, m % 2, :], xT[:, m, :], col(V_NFIN, m), None, ALU.mult).then_inc(ft_rdy, 1)

            mlp(1, C_MLP1, finish_last)
            dve.wait_ge(fss_mm, 1)
            link(dve.tensor_scalar(n4f[:, 0, :], ps[:, 7, 0:QB], 1.0 / D, EPS, ALU.mult, ALU.add))
            inverse_root(n4f[:, 0, :], n4f[:, 1, :], n4f[:, 2, :], n4f[:, 3, :], rfin, 5).then_inc(rfin_rdy, 1)
            dve.wait_ge(rfin_rdy, 1)
            dve.wait_ge(ft_copied, KT)
            for i in range(2):
                dve.tensor_scalar(otok[:, i, :], otok[:, i, :], rfin[:, i:i + 1], None, ALU.mult).then_inc(o_dve, 1)

        @block.tensor
        def _(pe):
            def product(dst, ah, al, bh, bl, start, stop):
                pe.matmul(dst, ah, bl, start=start, stop=False)
                pe.matmul(dst, ah, bh, start=False, stop=False)
                return pe.matmul(dst, al, bh, start=False, stop=stop)

            pe.wait_ge(const_rdy, 3)
            pe.wait_ge(vec_in, 16 * 14)
            pe.transpose(ps[:, 7, 0:V_ROWS], vrow[0:V_ROWS, 0, :], ident[0:V_ROWS, 0:V_ROWS])
            pe.transpose(ps[:, 7, V_DW:V_DW + P], vrow[:, 1, :], ident[:, :])
            rest = TAPS * KT - P
            pe.transpose(ps[:, 7, V_DW + P:V_ALL], vrow[0:rest, 2, :], ident[0:rest, 0:rest]).then_inc(vt_rdy, 1)
            pe.wait_ge(relb_in, 32)
            for h in range(2):
                last = pe.matmul(ps[0:HEADS, 5 + h, 0:320], relb, brow[:, 320 * h:320 * h + 320], start=True, stop=True)
            last.then_inc(rev_mm, 1)
            for i in range(QB):
                pe.wait_ge(x_in[i], 16)
            for k in range(KT):
                if k >= 4:
                    pe.wait_ge(xt_copied, k - 3)
                for i in range(QB):
                    last = pe.transpose(ps[:, k % 4, P * i:P * i + P], xtok[:, i, P * k:P * k + P], ident[:, :])
                last.then_inc(xt_rdy, 1)
            pe.wait_ge(rev_rdy, 2)
            pe.wait_ge(vcol_rdy, 1)
            for k in range(KT):
                pe.wait_ge(mv_lo, k + 1)
                c, kk = C_WIN + k // 4, k % 4
                if kk == 0:
                    pe.wait_ge(w_lo, c + 1)
                w = slice(W_IN * kk, W_IN * kk + W_IN)
                for i in range(QB):
                    t = slice(P * i, P * i + P)
                    last = product(ps[:, 4 + i, 0:W_IN], movh[:, k, t], movl[:, k, t], wh[:, c, w], wl[:, c, w],
                                   k == 0, k == KT - 1)
                    if k == KT - 1:
                        last.then_inc(pin_rdy, 1)
            pe.wait_ge(projn_rdy, 1)
            for t in range(4):
                for i in range(QB):
                    last = pe.transpose(ps[:, t, P * i:P * i + P], projn[:, i, P * t:P * t + P], ident[:, :])
                last.then_inc(ct_rdy, 1)

            pe.wait_ge(c_lo, 4)
            pe.wait_ge(proj_rdy, QB)
            pe.wait_ge(w_lo, C_QIDX + 1)
            for t in range(4):
                for k in range(2):
                    w = slice(512 * k + P * t, 512 * k + P * t + P)
                    last = product(ps[:, 4 + t, :], wh[:, C_QIDX % 2, w], wl[:, C_QIDX % 2, w], ch[:, k, :],
                                   cl[:, k, :], k == 0, k == 1)
                last.then_inc(qi_rdy, 1)
            pe.wait_ge(qi_lo, 4)
            s = 0
            for i in range(1, QB):
                for h in range(IDX_HEADS):
                    if s >= 4:
                        pe.wait_ge(sc_relu, s - 3)
                    half, t, n = slice(64 * (h % 2), 64 * (h % 2) + 64), slice(P * i, P * i + P), P * (i + 1)
                    product(ps[:, s % 4, 0:n], hidh[half, h // 2, t], hidl[half, h // 2, t], ch[half, 3, 0:n],
                            cl[half, 3, 0:n], True, True).then_inc(sc_rdy, 1)
                    s += 1

            def pair_qk(p):
                pe.wait_ge(sw_lo, p + 1)
                if isinstance(p, int) and p == 0:
                    pe.wait_ge(sc_relu, s)
                else:
                    pe.wait_ge(pr_lo, 3 * p)
                for k in range(2):
                    last = product(ps[:, 0, :], swH[:, k, :], swL[:, k, :], ch[:, k, :], cl[:, k, :], k == 0, k == 1)
                last.then_inc(pr_rdy, 1)
                product(ps[:, 1, :], swH[:, 2, :], swL[:, 2, :], ch[:, 2, :], cl[:, 2, :], True, True).then_inc(
                    pr_rdy, 1)

            def pair_v(p):
                pe.wait_ge(pr_lo, 3 * p + 1)
                for j in range(QB):
                    t = slice(P * j, P * j + P)
                    last = product(ps[:, 0, t], ch[:, 2, t], cl[:, 2, t], swH[:, 3, :], swL[:, 3, :], True, True)
                last.then_inc(pr_rdy, 1)

            def logits(n, hh, p):
                b, half = hh // 2 % 2, slice(64 * (hh % 2), 64 * (hh % 2) + 64)
                pe.wait_ge(pr_lo, 3 * p + 2)
                for i in range(QB):
                    t, w = slice(P * i, P * i + P), slice(0, P * (i + 1))
                    if not (isinstance(n, int) and 4 * n + i < 2):
                        pe.wait_ge(lg_done, 4 * n + (i - 1))
                    product(ps[:, 2 + i % 2, w], qH[half, b, t], qL[half, b, t], kH[half, b, w], kL[half, b, w],
                            True, True).then_inc(lg_rdy, 1)

            def transposes(n, hh):
                for i in range(QB):
                    pe.wait_ge(nr_done, 4 * n + (i + 1))
                    pe.wait_ge(pt_lo, 4 * n + (CREDITS + i - 1))
                    for j in range(i + 1):
                        t = slice(BLK[i] + P * j, BLK[i] + P * j + P)
                        last = pe.transpose(ps[:, 4 + i % 2, P * j:P * j + P], L[:, hh % 2, t], ident[:, :])
                    last.then_inc(pt_rdy, 1)

            def head_output(n, hh, p):
                b = hh // 2 % 2
                pe.wait_ge(pt_lo, 4 * n + (CREDITS + 4))
                pe.wait_ge(pr_lo, 3 * p + 3)
                pe.wait_ge(o_lo, n + (CREDITS - 1))
                for j in range(QB):
                    t = slice(P * j, P * j + P)
                    last = product(ps[:, 6 + hh % 2, P * j:SEQ], vH[:, b, t], vL[:, b, t], ptH[:, j, P * j:SEQ],
                                   ptL[:, j, P * j:SEQ], j == 0, j == QB - 1)
                last.then_inc(pv_rdy, 1)

            for p in range(2):
                pair_qk(p)
                pair_v(p)
            logits(0, 0, 0)
            logits(1, 1, 0)

            def head_step(g, hh):
                n, last = 4 * g + hh, isinstance(g, int)
                ahead = hh % 2 and not last
                transposes(n, hh)
                if not last or hh < 2:
                    logits(n + 2, hh + 2, 2 * g + (hh + 2) // 2)
                if ahead:
                    pair_qk(2 * g + (hh + 3) // 2)
                head_output(n, hh, 2 * g + hh // 2)
                if ahead:
                    pair_v(2 * g + (hh + 3) // 2)

            with pe.Fori(0, HEADS // 4 - 1) as g:
                for hh in range(4):
                    head_step(g, hh)
            for hh in range(4):
                head_step(HEADS // 4 - 1, hh)

            def weight_product(bank, c, h, k, n, mh, ml):
                w = slice(256 * k + P * h, 256 * k + P * h + P)
                return product(ps[:, bank, :], wh[:, c % 2, w], wl[:, c % 2, w], mh[:, k, :], ml[:, k, :], k == 0,
                               k == n - 1)

            for t in range(KT):
                c, h = C_WO + t // 2, t % 2
                if h == 0:
                    pe.wait_ge(w_lo, c + 1)
                if t >= 4:
                    pe.wait_ge(x_upd, t - 3)
                for k in range(KT):
                    if t == 0:
                        pe.wait_ge(o_lo, CREDITS + 2 * k + 2)
                    last = weight_product(t % 4, c, h, k, KT, hidh, hidl)
                last.then_inc(mm_done, 1)

            def square_sums(f):
                pe.wait_ge(ss_add, KT * (f + 1))
                pe.matmul(ps[:, 4, :], ones[:, :], ss, start=True, stop=True).then_inc(ss_mm, 1)

            def mlp(layer, c0, mv0, f, after):
                t0 = tile_of(c0)

                def tile(g, u):
                    c, h = c0 + u // 2, u % 2
                    if h == 0:
                        pe.wait_ge(w_lo, 8 * g + (c + 1))
                    if u < 4:
                        pe.wait_ge(x_upd, 8 * g + (UPD_MLP[layer] - 4 + u + 1))
                    elif u < 12:
                        pe.wait_ge(relu_rdy, 8 * g + (8 * GROUPS * layer + u - 3))
                    else:
                        pe.wait_ge(x_upd, 8 * g + (UPD_MLP[layer] + u - 11))
                    for k in range(KT):
                        if u == 0 and isinstance(g, int) and g == 0:
                            pe.wait_ge(mv_lo, mv0 + k + 1)
                        if u == 8:
                            pe.wait_ge(hid_lo, 8 * g + (CREDITS + HID_MLP[layer] + k + 1))
                        mh, ml = (movh, movl) if u < 8 else (hidh, hidl)
                        last = weight_product((t0 + u) % 4, c, h, k, KT, mh, ml)
                    last.then_inc(mm_done, 1)

                for u in range(16):
                    tile(0, u)
                    if u == 0:
                        square_sums(f)
                with pe.Fori(1, GROUPS - (1 if after else 0)) as g:
                    for u in range(16):
                        tile(g, u)
                if after:
                    for u in range(16):
                        tile(GROUPS - 1, u)
                        if u > 8:
                            after(u - 9)

            mlp(0, C_MLP0, KT, 0, None)

            t0 = tile_of(C_PW1)
            for t in range(2 * KT):
                c, h = C_PW1 + t // 2, t % 2
                if h == 0:
                    pe.wait_ge(w_lo, c + 1)
                if t < 4:
                    pe.wait_ge(x_upd, UPD_FINAL[1] + KT - 4 + t + 1)
                else:
                    pe.wait_ge(gate_read, t - 3)
                for k in range(KT):
                    if t == 0:
                        pe.wait_ge(mv_lo, 2 * KT + k + 1)
                    last = weight_product((t0 + t) % 4, c, h, k, KT, movh, movl)
                last.then_inc(mm_done, 1)
                if t == 1:
                    square_sums(1)
            for m in range(KT):
                pe.wait_ge(conv_rdy, m + 1)
                last = pe.matmul(ps[:, 5, :], ones[:, :], conv[:, m, :], start=m == 0, stop=m == KT - 1)
            last.then_inc(mean_mm, 1)
            for m in range(KT):
                pe.wait_ge(dsq_rdy, m + 1)
                pe.matmul(ps[:, 6, :], ones[:, :], tg[:, m % 2, :], start=m == 0, stop=m == KT - 1).then_inc(var_mm, 1)
            t0 = tile_of(C_PW2)
            for t in range(KT):
                c, h = C_PW2 + t // 2, t % 2
                if h == 0:
                    pe.wait_ge(w_lo, c + 1)
                if t >= 4:
                    pe.wait_ge(x_upd, UPD_FINAL[2] + t - 3)
                else:
                    pe.wait_ge(gate_read, 2 * KT - 3 + t)
                for k in range(KT):
                    if t == 0:
                        pe.wait_ge(hid_lo, CREDITS + HID_MLP[1] - KT + k + 1)
                    last = weight_product((t0 + t) % 4, c, h, k, KT, hidh, hidl)
                last.then_inc(mm_done, 1)

            def transpose_out(m):
                pe.wait_ge(ft_rdy, m + 1)
                if m >= 2:
                    pe.wait_ge(ft_copied, m - 1)
                for i in range(QB):
                    last = pe.transpose(ps[:, 5 + m % 2, P * i:P * i + P], ft[:, m % 2, P * i:P * i + P], ident[:, :])
                last.then_inc(ftt_rdy, 1)

            mlp(1, C_MLP1, 3 * KT, 2, transpose_out)
            transpose_out(KT - 1)
            pe.wait_ge(ss_add, 4 * KT)
            for i in range(QB):
                last = pe.matmul(ps[:, 7, i:i + 1], ss[:, P * i:P * i + P], ones[:, 0:1], start=True, stop=True)
            last.then_inc(fss_mm, 1)


def kernel(**inputs):
    import math as _math
    import numpy as _np
    import concourse.bacc as _bacc
    from concourse import mybir as _mybir
    from concourse.bass_utils import run_bass_kernel_spmd as _run

    dist = _np.maximum(SEQ - 1 - _np.arange(REV), 0)
    near = NB // 2
    large = near + (_np.log(_np.maximum(dist, 1).astype(_np.float32) / near) / _np.float32(_math.log(128 / near))
                    * (NB - near)).astype(_np.int32)
    bucket = _np.where(dist < near, dist, _np.minimum(large, NB - 1))
    bucket_rows = (bucket[None, :] == _np.arange(NB)[:, None]).astype(_np.float32)

    nc = _bacc.Bacc("TRN2", target_bir_lowering=False, num_devices=1)
    names = ("x", "norm_mix", "norm_mlp", "norm_final", "rel_bias", "attn_w_in", "attn_q_norm", "attn_kv_norm",
             "attn_kidx_norm", "attn_w_qidx", "attn_w_uq", "attn_w_uk", "attn_w_uv", "attn_w_o", "conv_w_pw1",
             "conv_b_pw1", "conv_w_dw", "conv_b_dw", "conv_ln_g", "conv_ln_b", "conv_w_pw2", "conv_b_pw2",
             "mlp_w_up", "mlp_w_down")
    arrays, args = {}, []
    for name in names:
        arrays[name] = _np.ascontiguousarray(inputs[name])
    arrays["norm_final"] = arrays["norm_final"].reshape(1, D)
    arrays["bucket_rows"] = bucket_rows
    for name, a in arrays.items():
        args.append(nc.dram_tensor(name, a.shape, _mybir.dt.float32, kind="ExternalInput").ap())
    args.append(nc.dram_tensor("out", (1, SEQ, D), _mybir.dt.float32, kind="ExternalOutput").ap())
    program(nc, *args)
    r = _run(nc, [arrays], core_ids=[0])
    return r.results[0]["out"]
```

```python
from contextlib import ExitStack

import concourse.bass as bass
from concourse import mybir
from concourse.alu_op_type import AluOpType as ALU

F32 = mybir.dt.float32
F32R = mybir.dt.float32r
ACT = mybir.ActivationFunctionType

P = 128
SEQ = 512
D = 1024
KT = D // P
QB = SEQ // P
HEADS = 16
PAIRS = HEADS // 2
D_NOPE = 64
D_CQ, D_CKV = 256, 128
IDX_HEADS, IDX_DIM = 8, 64
W_IN = D_CQ + D_CKV + IDX_DIM + IDX_HEADS
TOPK = min(256, SEQ // 4)
NB = 32
TAPS = 31
ACT_TAPS = 13
DVE_TAPS = TAPS - ACT_TAPS
D_FF = 4 * D
EPS = 1e-6
MASKED = -1e30
NOT_YET = -3e38
TAKEN = -3.4e38

CHUNK = 16 * P
GROUPS = D_FF // P // 8
REV = SEQ + P

BLK = [0, 128, 384, 768, 1280]
OFF = [0, 128, 0, 384]
STEPS = 2 * HEADS
SBLK = [None, 0, 256, 640, 1152]

V_NMIX, V_NMLP, V_BP1, V_BDW, V_LNG, V_LNB, V_BP2, V_NFIN, V_QN, V_KVN, V_KIN = (
    0, 16, 32, 48, 56, 64, 72, 80, 88, 90, 91)
V_ROWS = 92
V_DW = V_ROWS
V_ALL = V_DW + TAPS * KT

C_WIN, C_QIDX, C_WO = 0, 2, 4
C_MLP0 = C_WO + 4
C_PW1 = C_MLP0 + 8 * GROUPS
C_PW2 = C_PW1 + 8
C_MLP1 = C_PW2 + 4


UPD_MLP = (KT, KT + KT * GROUPS + KT)
UPD_FINAL = (0, KT * GROUPS, KT * GROUPS + KT, 2 * KT * GROUPS + KT)
HID_MLP = (0, 8 * GROUPS + KT)
CREDITS = 2
FREE = 6


def tile_of(c):
    return 2 * (c - C_WO)


def raw_value(c):
    return sum(32 if C_PW1 <= d < C_PW2 else 16 for d in range(c % 2, c + 1, 2))


def program(nc, x, norm_mix, norm_mlp, norm_final, rel_bias, w_in, q_norm, kv_norm, kidx_norm, w_qidx, w_uq, w_uk,
            w_uv, w_o, w_pw1, b_pw1, w_dw, b_dw, ln_g, ln_b, w_pw2, b_pw2, w_up, w_down, bucket_rows, out):
    rev_dram = nc.dram_tensor("reversed_bias", (HEADS, P * REV), F32, kind="Internal").ap()
    ctx = ExitStack()
    with ctx:
        def sb(name, shape, dt=F32):
            return ctx.enter_context(nc.sbuf_tensor(name, shape, dt))

        def sem(name):
            return ctx.enter_context(nc.semaphore(name))

        xT = sb("xT", [P, KT, SEQ])
        movh = sb("movh", [P, KT, SEQ], F32R)
        movl = sb("movl", [P, KT, SEQ], F32R)
        hidh = sb("hidh", [P, KT, SEQ], F32R)
        hidl = sb("hidl", [P, KT, SEQ], F32R)
        raw = sb("raw", [P, 2, CHUNK])
        wh = sb("wh", [P, 2, CHUNK], F32R)
        wl = sb("wl", [P, 2, CHUNK], F32R)
        ch = sb("ch", [P, 4, SEQ], F32R)
        cl = sb("cl", [P, 4, SEQ], F32R)
        ptH = sb("ptH", [P, 2, QB, 2 * P], F32R)
        ptL = sb("ptL", [P, 2, QB, 2 * P], F32R)
        S1 = sb("S1", [P, 11264])
        ident = sb("ident", [P, P])
        ones = sb("ones", [P, P])
        vcol = sb("vcol", [P, V_ALL])
        small = sb("small", [P, 224])

        junk = S1[:, 0:4096].rearrange("p (i n) -> p i n", i=QB)
        vrow = S1[:, 4096:4480].rearrange("p (r n) -> p r n", r=3)
        relb = S1[0:NB, 4480:4480 + HEADS]
        revs = S1[0:HEADS, 4496:4496 + REV]
        brow = S1[0:NB, 5136:5136 + REV]
        proj = S1[:, 4096:4096 + QB * W_IN].rearrange("p (i n) -> p i n", i=QB)
        projn = S1[:, 5920:5920 + QB * 512].rearrange("p (i n) -> p i n", i=QB)
        xtok = S1[:, 7168:11264].rearrange("p (i n) -> p i n", i=QB)
        rawqkv = S1[:, 0:4096].rearrange("p (w n) -> p w n", w=4)
        mask = S1[:, 4096:5376]
        tb = S1[:, 5376:6400].rearrange("p (b n) -> p b n", b=2)
        bm = (S1[:, 10368:11264], S1[:, 6400:7296])
        score = S1[:, 7424:8576]
        relu_s = S1[:, 8576:9600].rearrange("p (b n) -> p b n", b=2)
        L = S1[:, 8576:10368].rearrange("p (b n) -> p b n", b=2)
        four = lambda t: t.rearrange("p b n -> p (b n)").rearrange("p (k n) -> p k n", n=SEQ)
        qkvH, qkvL = (hidh, movh, four(wh[:, :, :])), (hidl, movl, four(wl[:, :, :]))
        qiH, qiL = (t[:, :, :, :].rearrange("p b j n -> p (b j n)").rearrange("p (k n) -> p k n", n=SEQ)
                    for t in (ptH, ptL))
        swH, swL = (t[:, 0:2, :].rearrange("p b (w n) -> p b w n", n=P) for t in (qiH, qiL))
        rt = S1[:, 0:1024].rearrange("p (b n) -> p b n", b=2)
        sqt = S1[:, 1024:2048].rearrange("p (b n) -> p b n", b=2)
        dt = S1[:, 2048:3072].rearrange("p (b n) -> p b n", b=2)
        sqx = S1[:, 3072:4096].rearrange("p (b n) -> p b n", b=2)
        ss = S1[:, 4096:4608]
        rbc = S1[:, 4608:5120]
        GW = TAPS - 1 + SEQ
        RING = 4
        conv = S1[:, 0:4096].rearrange("p (k n) -> p k n", k=KT)
        glu = S1[:, 5120:5120 + RING * GW].rearrange("p (b n) -> p b n", b=RING)
        tg = S1[:, 7296:8320].rearrange("p (b n) -> p b n", b=2)
        partial = S1[:, 8320:9344].rearrange("p (b n) -> p b n", b=2)
        tapb = S1[:, 9344:10880].rearrange("p (b n) -> p b n", b=3)
        sg, mean = tapb[:, 0:2, :], tapb[:, 2, :]
        otok = S1[:, 5120:9216].rearrange("p (i n) -> p i n", i=QB)
        ft = S1[:, 9216:10240].rearrange("p (b n) -> p b n", b=2)

        ssq = small[:, 0:4]
        r1 = small[:, 4:8]
        n4 = small[:, 8:24].rearrange("p (a n) -> p a n", a=4)
        stat = small[:, 24:36]
        rs = small[:, 36:48]
        n12 = small[:, 48:96].rearrange("p (a n) -> p a n", a=4)
        wsc = small[:, 96:128]
        m8 = (small[:, 128:136], small[:, 188:196])
        rmax = small[:, 136:144].rearrange("p (b n) -> p b n", b=2)
        nmax = small[:, 144:152].rearrange("p (b n) -> p b n", b=2)
        n4f = small[:, 168:184].rearrange("p (a n) -> p a n", a=4)
        rfin = small[:, 184:188]
        sums = small[:, 152:160].rearrange("p (b n) -> p b n", b=2)
        rsum = small[:, 160:168].rearrange("p (b n) -> p b n", b=2)

        ps = ctx.enter_context(nc.psum_tensor("ps", [P, 8, 512], F32))

        x_in = [sem(f"x_in{i}") for i in range(QB)]
        raw_in = [sem(f"raw_in{b}") for b in range(2)]
        tb_in = [sem(f"tb_in{b}") for b in range(2)]
        vec_in, relb_in, qkv_in, rev_out, out_done = map(sem, ("vec_in", "relb_in", "qkv_in", "rev_out", "out_done"))
        w_hi, w_lo = map(sem, ("w_hi", "w_lo"))
        const_rdy, vt_rdy, vcol_rdy, rev_mm, rev_rdy = map(sem, ("const_rdy", "vt_rdy", "vcol_rdy", "rev_mm",
                                                                 "rev_rdy"))
        xt_rdy, xt_copied, mv_hi, mv_lo = map(sem, ("xt_rdy", "xt_copied", "mv_hi", "mv_lo"))
        ssq_rdy, inv_rdy, act_root, chain, r1_rdy = map(sem, ("ssq_rdy", "inv_rdy", "act_root", "chain", "r1_rdy"))
        pin_rdy, proj_rdy, stat_rdy, projn_rdy = map(sem, ("pin_rdy", "proj_rdy", "stat_rdy", "projn_rdy"))
        rs_rdy, projn_q = map(sem, ("rs_rdy", "projn_q"))
        ct_rdy, c_hi, c_lo, qi_rdy, qi_hi, qi_lo = map(sem, ("ct_rdy", "c_hi", "c_lo", "qi_rdy", "qi_hi", "qi_lo"))
        sc_rdy, sc_relu, sc_acc, sc_causal, taken = map(sem, ("sc_rdy", "sc_relu", "sc_acc", "sc_causal", "taken"))
        mask0_rdy, mask_rdy = map(sem, ("mask0_rdy", "mask_rdy"))
        sw_hi, sw_lo, pr_rdy, pr_hi, pr_lo = map(sem, ("sw_hi", "sw_lo", "pr_rdy", "pr_hi", "pr_lo"))
        seen = sem("seen")
        bm_rdy, lg_rdy, lg_done, nm_rdy, ex_done = map(sem, ("bm_rdy", "lg_rdy", "lg_done", "nm_rdy", "ex_done"))
        rc_rdy, nr_done, pt_rdy, pt_hi, pt_lo = map(sem, ("rc_rdy", "nr_done", "pt_rdy", "pt_hi", "pt_lo"))
        pv_rdy, o_hi, o_lo = map(sem, ("pv_rdy", "o_hi", "o_lo"))
        mm_done, x_upd, sq_rdy, ss_add, ss_mm = map(sem, ("mm_done", "x_upd", "sq_rdy", "ss_add", "ss_mm"))
        relu_rdy, sqt_rdy, hid_hi, hid_lo, dt_rdy = map(sem, ("relu_rdy", "sqt_rdy", "hid_hi", "hid_lo", "dt_rdy"))
        pad_rdy, gate_read, sg_rdy, glu_rdy, conv_rdy = map(sem, ("pad_rdy", "gate_read", "sg_rdy", "glu_rdy",
                                                                  "conv_rdy"))
        tp_rdy, part_add, dve_taps = map(sem, ("tp_rdy", "part_add", "dve_taps"))
        mean_mm, dev_rdy, dsq_rdy, var_mm = map(sem, ("mean_mm", "dev_rdy", "dsq_rdy", "var_mm"))
        zt_rdy, zs_rdy, ft_rdy, ftt_rdy, ft_copied, fss_mm = map(sem, ("zt_rdy", "zs_rdy", "ft_rdy", "ftt_rdy",
                                                                       "ft_copied", "fss_mm"))
        rfin_rdy, o_dve, o_act = map(sem, ("rfin_rdy", "o_dve", "o_act"))

        def col(v, k=0):
            return vcol[:, v + k:v + k + 1]

        def flat(ap):
            return ap.rearrange("p a n -> p (a n)")

        def tap_products():
            for q in range(KT // 2):
                for s in range(ACT_TAPS):
                    for e in range(2):
                        yield 2 * q + e, s, e, 2 * (q * (ACT_TAPS - 1) + s - 1) + e

        def later(f, g, hh, d):
            step, pair, e = 2 * g + (HEADS * f + hh + d), g + (hh + d) // 2, (hh + d) % 2
            if isinstance(g, int) and pair >= PAIRS:
                f, pair = f + 1, pair - PAIRS
            return (step, f, pair, e) if f < 2 else None

        def passes(engine, step):
            for f in range(2):
                with engine.Fori(0, PAIRS - 1) as g:
                    for hh in range(2):
                        step(f, g, hh)
                for hh in range(2):
                    step(f, PAIRS - 1, hh)

        def wait_apart(engine):
            engine.sem_inc(seen, 1)

        block = ctx.enter_context(nc.Block())

        @block.sync
        def _(sp):
            def chunk_load(c, src):
                if c >= 2:
                    sp.wait_ge(w_lo, c - 1)
                k, n = src.shape[1], src.shape[2]
                sp.dma_start(raw[:, c % 2, 0:k * n].rearrange("p (k n) -> p k n", k=k), src).then_inc(
                    raw_in[c % 2], 16)

            x_v = x.rearrange("o (i p) d -> (o p) i d", p=P)
            for i in range(QB):
                sp.dma_start(xtok[:, i, :], x_v[:, i, :]).then_inc(x_in[i], 16)
            w_in_v = w_in.rearrange("o (c k p) n -> (o p) c k n", p=P, k=4)
            for c in range(2):
                chunk_load(C_WIN + c, w_in_v[:, c])
            sp.wait_ge(rev_rdy, 2)
            for h in range(0, HEADS, 4):
                sp.dma_start(rev_dram[h:h + 4].rearrange("h (r n) -> h r n", r=P),
                             revs[h:h + 4, :].unsqueeze(1).to_broadcast([4, P, REV])).then_inc(rev_out, 16)
            w_qidx_v = w_qidx.rearrange("o (k p) n -> (o p) k n", p=P)
            for k in range(2):
                chunk_load(C_QIDX + k, w_qidx_v[:, k:k + 1, :])
            sp.wait_ge(stat_rdy, 2 * QB)
            sp.dma_start(rawqkv[:, 0:2, :], w_uq.rearrange("o (k p) n -> (o p) k n", p=P)).then_inc(qkv_in, 16)
            sp.dma_start(rawqkv[:, 2, :], w_uk.rearrange("o c h d -> (o c) (h d)")).then_inc(qkv_in, 16)
            sp.dma_start(rawqkv[:, 3, :], w_uv.rearrange("o c h d -> (o c) (h d)")).then_inc(qkv_in, 16)
            w_o_v = w_o.rearrange("o (k p) (c n) -> (o p) c k n", p=P, n=256)
            chunk_load(C_WO, w_o_v[:, 0])
            sp.wait_ge(rev_out, 64)
            chunk_load(C_WO + 1, w_o_v[:, 1])
            sp.wait_ge(c_lo, 4)
            def bias_load(step, f, p, e):
                toeplitz = rev_dram[bass.ds(2 * p + e, 1), P - 1:P - 1 + P * (REV - 1)].rearrange(
                    "o (r n) -> (o r) n", r=P)
                near = slice(SEQ - 2 * P * (f + 1), SEQ)
                sp.dma_start(tb[:, e, near], toeplitz[:, near]).then_inc(tb_in[e], 16)

            def bias_step(f, g, hh):
                head = later(f, g, hh, 2)
                if head:
                    sp.wait_ge(bm_rdy, 2 * head[0] - 2)
                    bias_load(*head)

            bias_load(0, 0, 0, 0)
            bias_load(1, 0, 0, 1)
            passes(sp, bias_step)
            for c in range(2, 4):
                chunk_load(C_WO + c, w_o_v[:, c])

            def mlp_loads(layer, c0):
                up_v = w_up.rearrange("l (k p) n -> l p k n", p=P)[layer]
                down_v = w_down.rearrange("l (g k p) n -> l p g k n", p=P, k=8)[layer]
                with sp.Fori(0, GROUPS) as g:
                    for j in range(8):
                        c = c0 + j
                        sp.wait_ge(w_lo, 8 * g + (c - 1))
                        if j < 4:
                            src = up_v[:, :, bass.ds(g * 1024 + j * 256, 256)]
                        else:
                            src = down_v[:, bass.ds(g, 1), :, (j - 4) * 256:(j - 3) * 256].rearrange(
                                "p o k n -> p (o k) n")
                        sp.dma_start(raw[:, c % 2, :].rearrange("p (k n) -> p k n", k=8), src).then_inc(
                            raw_in[c % 2], 16)

            mlp_loads(0, C_MLP0)
            pw1_v = w_pw1.rearrange("o (k p) (h c n) -> (o p) c k h n", p=P, h=2, n=P)
            for i in range(8):
                c = C_PW1 + i
                sp.wait_ge(w_lo, c - 1)
                for h in range(2):
                    sp.dma_start(raw[:, c % 2, :].rearrange("p (k h n) -> p k h n", k=KT, h=2)[:, :, h, :],
                                 pw1_v[:, i, :, h, :]).then_inc(raw_in[c % 2], 16)
            pw2_v = w_pw2.rearrange("o (k p) (c n) -> (o p) c k n", p=P, n=256)
            for c in range(4):
                chunk_load(C_PW2 + c, pw2_v[:, c])
            mlp_loads(1, C_MLP1)
            out_v = out.rearrange("o (i p) d -> (o p) i d", p=P)
            for i in range(QB):
                sp.wait_ge(o_dve if i < 2 else o_act, i % 2 + 1)
                sp.dma_start(out_v[:, i, :], otok[:, i, :]).then_inc(out_done, 16)
            sp.wait_ge(out_done, 16 * QB)

        @block.gpsimd
        def _(pool):
            pool.memset(ident[:, :], 0.0).then_inc(const_rdy, 1)
            pool.memset(ones[:, :], 1.0).then_inc(const_rdy, 1)
            pool.wait_ge(const_rdy, 2)
            pool.affine_select(out=ident[:, :], in_=ident[:, :], compare_op=ALU.not_equal, fill=1.0, base=0,
                               pattern=[[-1, P]], channel_multiplier=1).then_inc(const_rdy, 1)
            pool.wait_ge(projn_rdy, 1)
            pool.wait_ge(projn_q, QB)
            pool.memset(mask[:, 0:P], 0.0).then_inc(mask0_rdy, 1)
            pool.wait_ge(mask0_rdy, 1)
            pool.affine_select(out=mask[:, 0:P], in_=mask[:, 0:P], compare_op=ALU.is_ge, fill=MASKED, base=0,
                               pattern=[[-1, P]], channel_multiplier=1).then_inc(mask0_rdy, 1)
            for i in range(1, QB):
                pool.wait_ge(sc_acc, IDX_HEADS * i)
                diag = score[:, SBLK[i + 1] - P:SBLK[i + 1]]
                pool.affine_select(out=diag, in_=diag, compare_op=ALU.is_ge, fill=NOT_YET, base=0,
                                   pattern=[[-1, P]], channel_multiplier=1).then_inc(sc_causal, 1)

            with pool.Fori(0, PAIRS // 2) as g:
                for b in range(2):
                    pool.wait_ge(sw_hi, 2 * g + (b + 1))
                    wait_apart(pool)
                    pool.tensor_tensor(swL[:, b, :, :], rawqkv[:, :, bass.ds((2 * g + b) * P, P)],
                                       swH[:, b, :, :].bitcast(F32), ALU.subtract).then_inc(sw_lo, 1)

            def bias_and_mask(step, f, p, e):
                pool.wait_ge(tb_in[e], (HEADS // 2 * f + 1 + p) * 16)
                if isinstance(step, int) and step < 2:
                    pool.wait_ge(mask0_rdy, 2)
                else:
                    pool.wait_ge(lg_done, 2 * step - 2)
                if isinstance(step, int) and step == HEADS * f:
                    pool.wait_ge(mask_rdy, 2 * f + 1)
                for ii in range(2):
                    i = 2 * f + ii
                    pool.tensor_tensor(bm[e][:, OFF[i]:OFF[i] + P * (i + 1)], tb[:, e, SEQ - P * (i + 1):SEQ],
                                       mask[:, BLK[i]:BLK[i + 1]], ALU.add).then_inc(bm_rdy, 1)

            def normalise(step, f, p, e):
                pool.wait_ge(rc_rdy, step + 1)
                wait_apart(pool)
                for ii in range(2):
                    i = 2 * f + ii
                    block = L[:, e, OFF[i]:OFF[i] + P * (i + 1)]
                    pool.tensor_scalar(block, block, rsum[:, e, ii:ii + 1], 1.0, ALU.mult, ALU.mult).then_inc(
                        nr_done, 1)

            def pool_step(f, g, hh):
                normalise(*later(f, g, hh, 0))
                if later(f, g, hh, 2):
                    bias_and_mask(*later(f, g, hh, 2))

            bias_and_mask(0, 0, 0, 0)
            bias_and_mask(1, 0, 0, 1)
            passes(pool, pool_step)

            def sum_squares(f):
                for m in range(KT):
                    pool.wait_ge(sq_rdy, KT * f + m + 1)
                    if m == 0:
                        pool.tensor_scalar(ss, sqx[:, 0, :], 1.0, 1.0, ALU.mult, ALU.mult).then_inc(ss_add, 1)
                    else:
                        pool.wait_ge(ss_add, KT * f + m)
                        pool.tensor_tensor(ss, ss, sqx[:, m % 2, :], ALU.add).then_inc(ss_add, 1)

            sum_squares(0)
            for b in range(RING):
                pool.memset(glu[:, b, 0:TAPS - 1], 0.0).then_inc(pad_rdy, 1)
            pool.wait_ge(ss_mm, 1)
            sum_squares(1)
            for i, s, e, k in tap_products():
                if s:
                    pool.wait_ge(tp_rdy, k + 2 * (i // 2 + 1) + 1)
                    if s > 1:
                        pool.wait_ge(part_add, k - 1)
                    pool.tensor_tensor(partial[:, e, :], partial[:, e, :], tapb[:, k % 3, :], ALU.add).then_inc(part_add, 1)
            pool.wait_ge(ss_mm, 2)
            sum_squares(2)
            pool.wait_ge(ss_mm, 3)
            sum_squares(3)

        @block.scalar
        def _(act):
            def split_hi(c, n=CHUNK):
                act.wait_ge(raw_in[c % 2], raw_value(c))
                if c in (C_QIDX, C_QIDX + 1):
                    act.wait_ge(pin_rdy, QB)
                elif c in (C_WO, C_WO + 1):
                    act.wait_ge(pv_rdy, HEADS + HEADS // 2 * (c - C_WO + 1))
                elif c > C_WO + 1:
                    act.wait_ge(mm_done, tile_of(c) - 2)
                act.activation(wh[:, c % 2, 0:n], raw[:, c % 2, 0:n], ACT.Copy).then_inc(w_hi, 1)

            def square_x(f, m):
                if f or m >= 2:
                    act.wait_ge(ss_add, KT * f + m - 1)
                act.activation(sqx[:, m % 2, :], xT[:, m, :], ACT.Square).then_inc(sq_rdy, 1)

            def finish_x(f, m, gain):
                act.wait_ge(x_upd, UPD_FINAL[f] + m + 1)
                act.activation(movh[:, m, :], xT[:, m, :], ACT.Copy, scale=gain).then_inc(mv_hi, 1)
                square_x(f, m)

            def root(dst, src, n):
                act.wait_ge(inv_rdy, n)
                act.activation(dst, src, ACT.Sqrt).then_inc(act_root, 1)

            for v, src in ((V_NMIX, norm_mix), (V_NMLP, norm_mlp), (V_BP1, b_pw1), (V_BDW, b_dw), (V_LNG, ln_g),
                           (V_LNB, ln_b), (V_BP2, b_pw2), (V_NFIN, norm_final), (V_QN, q_norm), (V_KVN, kv_norm)):
                rows = src.rearrange("l (k p) -> (l k) p", p=P)
                act.dma_start(vrow[v:v + rows.shape[0], 0, :], rows).then_inc(vec_in, 16)
            for half in range(2):
                act.dma_start(vrow[V_KIN:V_KIN + 1, 0, 64 * half:64 * half + 64], kidx_norm).then_inc(vec_in, 16)
            dw_rows = w_dw.rearrange("o j (k p) -> (o j k) p", p=P)
            act.dma_start(vrow[:, 1, :], dw_rows[0:P, :]).then_inc(vec_in, 16)
            act.dma_start(vrow[0:TAPS * KT - P, 2, :], dw_rows[P:TAPS * KT, :]).then_inc(vec_in, 16)
            act.dma_start(relb, rel_bias).then_inc(relb_in, 16)
            act.dma_start(brow, bucket_rows).then_inc(relb_in, 16)
            split_hi(C_WIN, 4 * W_IN)
            act.wait_ge(vcol_rdy, 1)
            for k in range(KT):
                if k == 2:
                    split_hi(C_WIN + 1, 4 * W_IN)
                act.wait_ge(xt_copied, k + 1)
                act.activation(movh[:, k, :], xT[:, k, :], ACT.Copy, scale=col(V_NMIX, k)).then_inc(mv_hi, 1)
            for i in range(QB):
                act.wait_ge(x_in[i], 16)
                act.activation(junk[:, i, :], xtok[:, i, :], ACT.Square, accum_out=ssq[:, i:i + 1]).then_inc(
                    ssq_rdy, 1)
            root(n4[:, 2, :], n4[:, 1, :], 1)
            act.wait_ge(r1_rdy, 1)
            act.wait_ge(rev_out, 64)
            for i in range(QB):
                act.wait_ge(pin_rdy, i + 1)
                act.activation(proj[:, i, :], ps[:, 4 + i, 0:W_IN], ACT.Copy, scale=r1[:, i:i + 1]).then_inc(
                    proj_rdy, 1)
                act.wait_ge(proj_rdy, i + 1)
                act.activation(junk[:, i, 0:256], proj[:, i, 0:256], ACT.Square,
                               accum_out=stat[:, i:i + 1]).then_inc(stat_rdy, 1)
            root(n12[:, 2, :], n12[:, 1, :], 2)
            act.wait_ge(rs_rdy, 1)
            for i in range(QB):
                act.activation(projn[:, i, 0:256], proj[:, i, 0:256], ACT.Copy, scale=rs[:, i:i + 1]).then_inc(
                    projn_q, 1)
            split_hi(C_QIDX, SEQ)
            split_hi(C_QIDX + 1, SEQ)
            for t in range(4):
                act.wait_ge(ct_rdy, t + 1)
                act.activation(ch[:, t, :], ps[:, t, :], ACT.Copy, scale=col(V_QN, t)).then_inc(c_hi, 1)
            for t in range(4):
                act.wait_ge(qi_rdy, t + 1)
                act.activation(qiH[:, t, :], ps[:, 4 + t, :], ACT.Copy).then_inc(qi_hi, 1)
            s = 0
            for i in range(1, QB):
                for h in range(IDX_HEADS):
                    act.wait_ge(sc_rdy, s + 1)
                    if s >= 2:
                        act.wait_ge(sc_acc, s - 1)
                    act.activation(relu_s[:, s % 2, 0:P * (i + 1)], ps[:, s % 4, 0:P * (i + 1)],
                                   ACT.Relu).then_inc(sc_relu, 1)
                    s += 1

            act.wait_ge(qkv_in, 48)
            def slices_hi(p, b):
                act.wait_ge(pr_rdy, 3 * p + (FREE - 3))
                act.activation(swH[:, b, :, :], rawqkv[:, :, bass.ds(p * P, P)], ACT.Copy).then_inc(sw_hi, 1)

            def pair_hi(p, b):
                for which in range(3):
                    act.wait_ge(pr_rdy, 3 * p + (FREE + which + 1))
                    act.activation(flat(qkvH[which][:, bass.ds(p, 1), :]), ps[:, 3 * b + which, :], ACT.Copy,
                                   scale=D_NOPE ** -0.5 if which == 0 else 1.0).then_inc(pr_hi, 1)

            slices_hi(0, 0)
            with act.Fori(0, PAIRS // 2 - 1) as g:
                for b in range(2):
                    slices_hi(2 * g + (b + 1), 1 - b)
                    pair_hi(2 * g + b, b)
            slices_hi(PAIRS - 1, 1)
            pair_hi(PAIRS - 2, 0)
            pair_hi(PAIRS - 1, 1)

            def exponentials(step, f, p, e):
                act.wait_ge(nm_rdy, step + 1)
                for ii in range(2):
                    i = 2 * f + ii
                    block = L[:, e, OFF[i]:OFF[i] + P * (i + 1)]
                    act.activation(block, block, ACT.Exp, bias=nmax[:, e, ii:ii + 1],
                                   accum_out=sums[:, e, ii:ii + 1]).then_inc(ex_done, 1)

            def probs_hi(step, f, p, e):
                for ii in range(2):
                    i = 2 * f + ii
                    act.wait_ge(pt_rdy, 2 * step + (ii + 1))
                    act.activation(ptH[:, e, 0:i + 1, P * ii:P * ii + P],
                                   ps[:, 4 + ii, 0:P * (i + 1)].rearrange("p (j n) -> p j n", n=P),
                                   ACT.Copy).then_inc(pt_hi, 1)

            def output_hi(step, f, p, e):
                act.wait_ge(pv_rdy, step + 1)
                act.activation(flat(hidh[64 * e:64 * e + 64, bass.ds(p, 1), 2 * P * f:2 * P * (f + 1)]),
                               ps[64 * e:64 * e + 64, 6 + e, 0:2 * P], ACT.Copy).then_inc(o_hi, 1)

            def act_step(f, g, hh):
                for work, d in ((probs_hi, 1), (exponentials, 2), (output_hi, 0)):
                    head = later(f, g, hh, d)
                    if head:
                        work(*head)
                if f == 1 and isinstance(g, int) and hh == 0:
                    split_hi(C_WO)

            exponentials(0, 0, 0, 0)
            exponentials(1, 0, 0, 1)
            probs_hi(0, 0, 0, 0)
            passes(act, act_step)

            split_hi(C_WO + 1)
            for c in range(4):
                if c:
                    split_hi(C_WO + c + 1)
                for m in (2 * c, 2 * c + 1):
                    finish_x(0, m, col(V_NMLP, m))

            def mlp(layer, c0, finish):
                t0, r0, h0 = tile_of(c0), 8 * GROUPS * layer, HID_MLP[layer]

                def group(g, last):
                    for j in range(8):
                        c = c0 + j + 1
                        if not (last and j == 7):
                            act.wait_ge(raw_in[c % 2], 64 * g + raw_value(c))
                            act.wait_ge(mm_done, 16 * g + (t0 + 2 * j))
                            act.activation(wh[:, c % 2, :], raw[:, c % 2, :], ACT.Copy).then_inc(w_hi, 1)
                        elif layer == 0:
                            split_hi(C_PW1)
                        for m in (2 * j, 2 * j + 1):
                            if j < 4:
                                act.wait_ge(mm_done, 16 * g + (t0 + m + 1))
                                act.wait_ge(hid_lo, 8 * g + (CREDITS + h0 + m - 1))
                                act.activation(rt[:, m % 2, :], ps[:, (t0 + m) % 4, :],
                                               ACT.Relu).then_inc(relu_rdy, 1)
                                act.wait_ge(relu_rdy, 8 * g + (r0 + m + 1))
                                act.activation(hidh[:, m, :], rt[:, m % 2, :], ACT.Square).then_inc(hid_hi, 1)
                            elif last:
                                finish(m - 8)

                with act.Fori(0, GROUPS - 1) as g:
                    group(g, False)
                group(GROUPS - 1, True)

            mlp(0, C_MLP0, lambda m: finish_x(1, m, col(V_NMIX, KT + m)))

            split_hi(C_PW1 + 1)
            root(sg[:, 1, :], sg[:, 0, :], 3)

            def sigmoids(i):
                for h in range(2):
                    act.wait_ge(gate_read, 2 * (i + h) + 2)
                    act.activation(tg[:, h, :], tg[:, h, :], ACT.Sigmoid, bias=col(V_BP1, KT + i + h)).then_inc(
                        sg_rdy, 1)

            split_hi(C_PW1 + 2)
            sigmoids(0)
            split_hi(C_PW1 + 3)
            for i, s, e, k in tap_products():
                if s == 0:
                    act.wait_ge(glu_rdy, i + 1)
                    if i >= 2:
                        act.wait_ge(conv_rdy, i - 1)
                    dst = partial[:, e, :]
                else:
                    if k >= 3:
                        act.wait_ge(part_add, k - 2)
                    dst = tapb[:, k % 3, :]
                if k < 3:
                    act.wait_ge(r1_rdy, 2)
                j = DVE_TAPS + s
                act.activation(dst, glu[:, i % RING, j:j + SEQ], ACT.Copy, scale=col(V_DW, KT * j + i)).then_inc(
                    tp_rdy, 1)
                if e == 1 and i < KT - 1 and s == ACT_TAPS - 4:
                    split_hi(C_PW1 + i + 3)
                if e == 1 and i < KT - 1 and s == ACT_TAPS - 1:
                    sigmoids(i + 1)
                    split_hi(C_PW1 + i + 4)
            for m in range(KT):
                act.wait_ge(dev_rdy, m + 1)
                if m >= 2:
                    act.wait_ge(var_mm, m - 1)
                act.activation(tg[:, m % 2, :], conv[:, m, :], ACT.Square).then_inc(dsq_rdy, 1)
            root(sg[:, 1, :], sg[:, 0, :], 4)
            act.wait_ge(r1_rdy, 3)
            z0 = HID_MLP[1] - KT
            for m in range(KT):
                act.wait_ge(zt_rdy, m + 1)
                if m >= 2:
                    act.wait_ge(hid_lo, CREDITS + z0 + m - 1)
                act.activation(sg[:, m % 2, :], tg[:, m % 2, :], ACT.Silu, scale=col(V_LNG, m),
                               bias=col(V_LNB, m)).then_inc(zs_rdy, 1)
                act.wait_ge(zs_rdy, m + 1)
                act.activation(hidh[:, m, :], sg[:, m % 2, :], ACT.Copy).then_inc(hid_hi, 1)
            for c in range(4):
                if c:
                    split_hi(C_PW2 + c + 1)
                for m in (2 * c, 2 * c + 1):
                    finish_x(2, m, col(V_NMLP, KT + m))

            def copy_out(m):
                act.wait_ge(ftt_rdy, m + 1)
                act.activation(otok[:, :, P * m:P * m + P], ps[:, 5 + m % 2, :].rearrange("p (i n) -> p i n", n=P),
                               ACT.Copy).then_inc(ft_copied, 1)

            def finish_last(m):
                act.wait_ge(x_upd, UPD_FINAL[3] + m + 1)
                square_x(3, m)
                if m:
                    copy_out(m - 1)

            mlp(1, C_MLP1, finish_last)
            copy_out(KT - 1)
            root(n4f[:, 2, :], n4f[:, 1, :], 5)
            act.wait_ge(rfin_rdy, 1)
            act.wait_ge(ft_copied, KT)
            for i in range(2, QB):
                act.activation(otok[:, i, :], otok[:, i, :], ACT.Copy, scale=rfin[:, i:i + 1]).then_inc(o_act, 1)

        @block.vector
        def _(dve):
            links = [0]

            def link(ins):
                links[0] += 1
                ins.then_inc(chain, 1)
                dve.wait_ge(chain, links[0])

            def split_lo(c, n=CHUNK):
                dve.wait_ge(w_hi, c + 1)
                dve.tensor_tensor(wl[:, c % 2, 0:n], raw[:, c % 2, 0:n], wh[:, c % 2, 0:n].bitcast(F32),
                                  ALU.subtract).then_inc(w_lo, 1)

            def inverse_root(v, inv, y, t, r, n):
                dve.reciprocal(inv, v).then_inc(inv_rdy, 1)
                dve.wait_ge(act_root, n)
                link(dve.tensor_tensor(t, y, y, ALU.mult))
                link(dve.tensor_tensor(t, t, v, ALU.mult))
                link(dve.tensor_scalar(t, t, -0.5, 1.5, ALU.mult, ALU.add))
                return dve.tensor_tensor(r, y, t, ALU.mult)

            def x_lo(n, m, gain):
                dve.wait_ge(mv_hi, n + 1)
                dve.scalar_tensor_tensor(movl[:, m, :], xT[:, m, :], gain, movh[:, m, :].bitcast(F32), ALU.mult,
                                         ALU.subtract).then_inc(mv_lo, 1)

            dve.sem_inc(hid_lo, CREDITS)
            dve.sem_inc(pr_lo, FREE)

            def copy_x(k):
                dve.wait_ge(xt_rdy, k + 1)
                dve.tensor_copy(xT[:, k, :], ps[:, k % 4, :]).then_inc(xt_copied, 1)

            for k in range(4):
                copy_x(k)
            dve.wait_ge(vt_rdy, 1)
            dve.tensor_copy(vcol[:, :], ps[:, 7, 0:V_ALL]).then_inc(vcol_rdy, 1)
            dve.wait_ge(rev_mm, 1)
            for h in range(2):
                dve.tensor_copy(revs[:, 320 * h:320 * h + 320], ps[0:HEADS, 5 + h, 0:320]).then_inc(rev_rdy, 1)
            dve.wait_ge(vcol_rdy, 1)
            split_lo(C_WIN, 4 * W_IN)
            for k in range(KT):
                if k == 3:
                    split_lo(C_WIN + 1, 4 * W_IN)
                x_lo(k, k, col(V_NMIX, k))
                if k < 4:
                    copy_x(k + 4)
            dve.wait_ge(ssq_rdy, QB)
            link(dve.tensor_scalar(n4[:, 0, :], ssq, 1.0 / D, EPS, ALU.mult, ALU.add))
            inverse_root(n4[:, 0, :], n4[:, 1, :], n4[:, 2, :], n4[:, 3, :], r1, 1).then_inc(r1_rdy, 1)
            for i in range(QB):
                dve.wait_ge(proj_rdy, i + 1)
                for s, a, b in ((1, 256, 384), (2, 384, 448)):
                    last = dve.tensor_tensor_reduce(junk[:, i, a:b], proj[:, i, a:b], proj[:, i, a:b], 1.0, 0.0,
                                                    ALU.mult, ALU.add, stat[:, 4 * s + i:4 * s + i + 1])
                last.then_inc(stat_rdy, 1)
            dve.wait_ge(stat_rdy, 2 * QB)
            for s, n in enumerate((D_CQ, D_CKV, IDX_DIM)):
                link(dve.tensor_scalar(n12[:, 0, 4 * s:4 * s + 4], stat[:, 4 * s:4 * s + 4], 1.0 / n, EPS, ALU.mult,
                                       ALU.add))
            inverse_root(n12[:, 0, :], n12[:, 1, :], n12[:, 2, :], n12[:, 3, :], rs, 2).then_inc(rs_rdy, 1)
            dve.wait_ge(rs_rdy, 1)
            for i in range(QB):
                dve.tensor_scalar(projn[:, i, 256:384], proj[:, i, 256:384], rs[:, 4 + i:5 + i], None, ALU.mult)
                for h in range(2):
                    dve.tensor_scalar(projn[:, i, 384 + 64 * h:448 + 64 * h], proj[:, i, 384:448],
                                      rs[:, 8 + i:9 + i], None, ALU.mult)
                last = dve.tensor_scalar(wsc[:, 8 * i:8 * i + 8], proj[:, i, 448:456],
                                         IDX_HEADS ** -0.5 * IDX_DIM ** -0.5, None, ALU.mult)
            last.then_inc(projn_rdy, 1)
            split_lo(C_QIDX, SEQ)
            split_lo(C_QIDX + 1, SEQ)
            for t in range(4):
                dve.wait_ge(c_hi, t + 1)
                dve.scalar_tensor_tensor(cl[:, t, :], ps[:, t, :], col(V_QN, t), ch[:, t, :].bitcast(F32), ALU.mult,
                                         ALU.subtract).then_inc(c_lo, 1)
            for t in range(4):
                dve.wait_ge(qi_hi, t + 1)
                dve.tensor_tensor(qiL[:, t, :], ps[:, 4 + t, :], qiH[:, t, :].bitcast(F32), ALU.subtract).then_inc(
                    qi_lo, 1)
            dve.wait_ge(projn_rdy, 1)
            s = 0
            for i in range(1, QB):
                for h in range(IDX_HEADS):
                    part, w = score[:, SBLK[i]:SBLK[i + 1]], wsc[:, 8 * i + h:8 * i + h + 1]
                    dve.wait_ge(sc_relu, s + 1)
                    if h == 0:
                        dve.tensor_scalar(part, relu_s[:, s % 2, 0:P * (i + 1)], w, None, ALU.mult).then_inc(sc_acc, 1)
                    else:
                        dve.wait_ge(sc_acc, s)
                        dve.scalar_tensor_tensor(part, relu_s[:, s % 2, 0:P * (i + 1)], w, part, ALU.mult,
                                                 ALU.add).then_inc(sc_acc, 1)
                    s += 1

            def largest(i):
                dve.max(m8[i % 2], score[:, SBLK[i]:SBLK[i + 1]]).then_inc(taken, 1)

            def mark(i):
                part = score[:, SBLK[i]:SBLK[i + 1]]
                dve.match_replace(part, m8[i % 2], part, TAKEN).then_inc(taken, 1)

            def make_mask(i, marked):
                dve.wait_ge(taken, marked)
                dve.tensor_scalar(mask[:, BLK[i]:BLK[i + 1]], score[:, SBLK[i]:SBLK[i + 1]], TAKEN, MASKED,
                                  ALU.not_equal, ALU.mult).then_inc(mask_rdy, 1)

            rounds = TOPK // 8
            dve.wait_ge(sc_causal, 1)
            dve.sem_inc(taken, 1)
            with dve.Fori(0, PAIRS // 2) as g:
                for b in range(2):
                    p = 2 * g + b
                    for step in range(4):
                        if step < 3:
                            dve.wait_ge(pr_hi, 3 * p + (step + 1))
                            dve.scalar_tensor_tensor(flat(qkvL[step][:, bass.ds(p, 1), :]), ps[:, 3 * b + step, :],
                                                     D_NOPE ** -0.5 if step == 0 else 1.0,
                                                     flat(qkvH[step][:, bass.ds(p, 1), :]).bitcast(F32),
                                                     ALU.mult, ALU.subtract).then_inc(pr_lo, 1)
                        dve.wait_ge(taken, 4 * p + (step + 1))
                        wait_apart(dve)
                        (largest, mark)[step % 2](1)
            make_mask(1, 4 * PAIRS + 1)

            def logits(step, f, p, e):
                if not (isinstance(step, int) and step < 2):
                    dve.wait_ge(pt_rdy, 2 * step - 2)
                for ii in range(2):
                    i = 2 * f + ii
                    dve.wait_ge(bm_rdy, 2 * step + (ii + 1))
                    dve.wait_ge(lg_rdy, 2 * step + (ii + 1))
                    wait_apart(dve)
                    block = slice(OFF[i], OFF[i] + P * (i + 1))
                    dve.tensor_tensor_reduce(L[:, e, block], ps[:, 2 + ii, 0:P * (i + 1)], bm[e][:, block], 1.0,
                                             -3e38, ALU.add, ALU.max, rmax[:, e, ii:ii + 1]).then_inc(lg_done, 1)

            def minus_max(step, f, p, e):
                dve.wait_ge(lg_done, 2 * step + 2)
                dve.tensor_scalar(nmax[:, e, 0:2], rmax[:, e, 0:2], -1.0, None, ALU.mult).then_inc(nm_rdy, 1)

            def probs_lo(step, f, p, e):
                for ii in range(2):
                    i = 2 * f + ii
                    dve.wait_ge(pt_hi, 2 * step + (ii + 1))
                    part = slice(P * ii, P * ii + P)
                    dve.tensor_tensor(ptL[:, e, 0:i + 1, part],
                                      ps[:, 4 + ii, 0:P * (i + 1)].rearrange("p (j n) -> p j n", n=P),
                                      ptH[:, e, 0:i + 1, part].bitcast(F32), ALU.subtract).then_inc(pt_lo, 1)

            def reciprocals(step, f, p, e):
                dve.wait_ge(ex_done, 2 * step + 2)
                dve.reciprocal(rsum[:, e, 0:2], sums[:, e, 0:2]).then_inc(rc_rdy, 1)

            def output_lo(step, f, p, e):
                half = lambda t: flat(t[64 * e:64 * e + 64, bass.ds(p, 1), 2 * P * f:2 * P * (f + 1)])
                dve.wait_ge(o_hi, step + 1)
                dve.tensor_tensor(half(hidl), ps[64 * e:64 * e + 64, 6 + e, 0:2 * P], half(hidh).bitcast(F32),
                                  ALU.subtract).then_inc(o_lo, 1)

            def dve_step(f, g, hh):
                done = 2 * rounds + 1
                peeled = isinstance(g, int)
                a_round = f == 0 and not (peeled and hh == 1)
                if a_round:
                    base = 8 * g + (done + 4 * hh)
                    dve.wait_ge(taken, base)
                    wait_apart(dve)
                    largest(2)
                    largest(3)
                if a_round and peeled:
                    for r in range(2):
                        if r:
                            dve.wait_ge(taken, base + 4)
                            largest(2)
                            largest(3)
                        dve.wait_ge(taken, base + 4 * r + 2)
                        mark(2)
                        mark(3)
                    make_mask(2, base + 7)
                    make_mask(3, base + 8)
                ahead = later(f, g, hh, 2)
                if ahead:
                    logits(*ahead)
                    minus_max(*ahead)
                if a_round and not peeled:
                    dve.wait_ge(taken, base + 2)
                    wait_apart(dve)
                    mark(2)
                    mark(3)
                if later(f, g, hh, 1):
                    probs_lo(*later(f, g, hh, 1))
                if ahead:
                    reciprocals(*ahead)
                output_lo(*later(f, g, hh, 0))

            dve.wait_ge(sc_causal, QB - 1)
            for e in range(2):
                logits(e, 0, 0, e)
                minus_max(e, 0, 0, e)
            for e in range(2):
                reciprocals(e, 0, 0, e)
            probs_lo(0, 0, 0, 0)
            passes(dve, dve_step)

            split_lo(C_WO)
            split_lo(C_WO + 1)
            for c in range(4):
                if c:
                    split_lo(C_WO + c + 1)
                for m in (2 * c, 2 * c + 1):
                    dve.wait_ge(mm_done, m + 1)
                    dve.tensor_tensor(xT[:, m, :], ps[:, m % 4, :], xT[:, m, :], ALU.add).then_inc(x_upd, 1)
                    dve.wait_ge(x_upd, m + 1)
                    x_lo(KT + m, m, col(V_NMLP, m))

            def mlp(layer, c0, finish):
                t0, r0, h0, u0 = tile_of(c0), 8 * GROUPS * layer, HID_MLP[layer], UPD_MLP[layer]
                dve.wait_ge(ss_mm, 2 * layer + 1)
                link(dve.tensor_scalar(rbc, ps[:, 4, :], 1.0 / D, EPS, ALU.mult, ALU.add))
                link(dve.reciprocal(rbc, rbc))

                def group(g, last):
                    for j in range(8):
                        c = c0 + j + 1
                        if not (last and j == 7):
                            dve.wait_ge(w_hi, 8 * g + (c + 1))
                            dve.tensor_tensor(wl[:, c % 2, :], raw[:, c % 2, :], wh[:, c % 2, :].bitcast(F32),
                                              ALU.subtract).then_inc(w_lo, 1)
                        elif layer == 0:
                            split_lo(C_PW1)
                        for m in (2 * (j % 4), 2 * (j % 4) + 1):
                            if j < 4:
                                dve.wait_ge(relu_rdy, 8 * g + (r0 + m + 1))
                                dve.wait_ge(hid_lo, 8 * g + (CREDITS + h0 + m - 1))
                                dve.tensor_tensor(sqt[:, m % 2, :], rt[:, m % 2, :], rt[:, m % 2, :],
                                                  ALU.mult).then_inc(sqt_rdy, 1)
                                dve.wait_ge(sqt_rdy, 8 * g + (r0 + m + 1))
                                dve.wait_ge(hid_hi, 8 * g + (h0 + m + 1))
                                dve.tensor_tensor(hidl[:, m, :], sqt[:, m % 2, :], hidh[:, m, :].bitcast(F32),
                                                  ALU.subtract).then_inc(hid_lo, 1)
                            else:
                                dve.wait_ge(mm_done, 16 * g + (t0 + 8 + m + 1))
                                dve.wait_ge(x_upd, 8 * g + (u0 + m - 1))
                                dve.tensor_tensor(dt[:, m % 2, :], ps[:, (t0 + m) % 4, :], rbc,
                                                  ALU.mult).then_inc(dt_rdy, 1)
                                dve.wait_ge(dt_rdy, 8 * g + (r0 + m + 1))
                                dve.tensor_tensor(xT[:, m, :], xT[:, m, :], dt[:, m % 2, :], ALU.add).then_inc(
                                    x_upd, 1)
                                if last:
                                    finish(m)

                with dve.Fori(0, GROUPS - 1) as g:
                    group(g, False)
                group(GROUPS - 1, True)

            mlp(0, C_MLP0, lambda m: x_lo(2 * KT + m, m, col(V_NMIX, KT + m)))

            split_lo(C_PW1 + 1)
            dve.wait_ge(ss_mm, 2)
            link(dve.tensor_scalar(rbc, ps[:, 4, :], 1.0 / D, EPS, ALU.mult, ALU.add))
            inverse_root(rbc, sg[:, 0, :], sg[:, 1, :], sg[:, 0, :], rbc, 3).then_inc(r1_rdy, 1)
            dve.wait_ge(r1_rdy, 2)
            dve.wait_ge(pad_rdy, RING)
            t0 = tile_of(C_PW1)

            def gates(i):
                for h in range(2):
                    u = glu[:, (i + h) % RING, TAPS - 1:GW]
                    for gate, dst in enumerate((u, tg[:, h, :])):
                        n = 2 * (i + h) + gate
                        dve.wait_ge(mm_done, t0 + n + 1)
                        if i >= 2:
                            dve.wait_ge(glu_rdy, i)
                        if i >= RING:
                            dve.wait_ge(conv_rdy, i - 2)
                        dve.tensor_tensor(dst, ps[:, (t0 + n) % 4, :], rbc, ALU.mult).then_inc(gate_read, 1)
                split_lo(C_PW1 + i + 2)

            def gated(i):
                for h in range(2):
                    u = glu[:, (i + h) % RING, TAPS - 1:GW]
                    dve.wait_ge(sg_rdy, i + h + 1)
                    dve.wait_ge(gate_read, 2 * (i + h) + 1)
                    dve.scalar_tensor_tensor(u, u, col(V_BP1, i + h), tg[:, h, :], ALU.add, ALU.mult).then_inc(
                        glu_rdy, 1)

            def add_partial(i):
                dve.wait_ge(dve_taps, DVE_TAPS * (i + 2))
                for h in range(2):
                    dve.wait_ge(part_add, (ACT_TAPS - 1) * (i + 2) - 1 + h)
                    dve.tensor_tensor(conv[:, i + h, :], conv[:, i + h, :], partial[:, h, :], ALU.add).then_inc(
                        conv_rdy, 1)

            gates(0)
            gated(0)
            for i in range(0, KT, 2):
                for j in range(DVE_TAPS):
                    if j == 3:
                        split_lo(C_PW1 + i + 3)
                    if j == DVE_TAPS - 5 and i + 2 < KT:
                        gates(i + 2)
                    for h in range(2):
                        m, n = i + h, DVE_TAPS * i + 2 * j + h
                        u = glu[:, m % RING, j:j + SEQ]
                        if j == 0:
                            dve.wait_ge(glu_rdy, m + 1)
                            ins = dve.tensor_scalar(conv[:, m, :], u, col(V_DW, m), col(V_BDW, m), ALU.mult, ALU.add)
                        else:
                            dve.wait_ge(dve_taps, n - 1)
                            ins = dve.scalar_tensor_tensor(conv[:, m, :], u, col(V_DW, KT * j + m), conv[:, m, :],
                                                           ALU.mult, ALU.add)
                        ins.then_inc(dve_taps, 1)
                if i + 2 < KT:
                    gated(i + 2)
                add_partial(i)
            dve.wait_ge(mean_mm, 1)
            link(dve.tensor_scalar(mean, ps[:, 5, :], 1.0 / D, None, ALU.mult))
            dve.wait_ge(conv_rdy, KT)
            for m in range(KT):
                dve.tensor_tensor(conv[:, m, :], conv[:, m, :], mean, ALU.subtract).then_inc(dev_rdy, 1)
            dve.wait_ge(var_mm, KT)
            dve.wait_ge(dev_rdy, KT)
            link(dve.tensor_scalar(rbc, ps[:, 6, :], 1.0 / D, EPS, ALU.mult, ALU.add))
            inverse_root(rbc, sg[:, 0, :], sg[:, 1, :], sg[:, 0, :], rbc, 4).then_inc(r1_rdy, 1)
            dve.wait_ge(r1_rdy, 3)
            z0 = HID_MLP[1] - KT

            def z_lo(m):
                dve.wait_ge(hid_hi, z0 + m + 1)
                dve.tensor_tensor(hidl[:, m, :], sg[:, m % 2, :], hidh[:, m, :].bitcast(F32),
                                  ALU.subtract).then_inc(hid_lo, 1)

            for m in range(KT):
                if m >= 2:
                    dve.wait_ge(zs_rdy, m - 1)
                dve.tensor_tensor(tg[:, m % 2, :], conv[:, m, :], rbc, ALU.mult).then_inc(zt_rdy, 1)
                if m:
                    z_lo(m - 1)
            z_lo(KT - 1)
            t0, u0 = tile_of(C_PW2), UPD_FINAL[2]
            for c in range(4):
                if c:
                    split_lo(C_PW2 + c + 1)
                for m in (2 * c, 2 * c + 1):
                    dve.wait_ge(mm_done, t0 + m + 1)
                    dve.scalar_tensor_tensor(xT[:, m, :], ps[:, (t0 + m) % 4, :], col(V_BP2, m), xT[:, m, :], ALU.add,
                                             ALU.add).then_inc(x_upd, 1)
                    dve.wait_ge(x_upd, u0 + m + 1)
                    x_lo(3 * KT + m, m, col(V_NMLP, KT + m))

            def finish_last(m):
                dve.wait_ge(x_upd, UPD_FINAL[3] + m + 1)
                if m >= 2:
                    dve.wait_ge(ftt_rdy, m - 1)
                dve.tensor_scalar(ft[:, m % 2, :], xT[:, m, :], col(V_NFIN, m), None, ALU.mult).then_inc(ft_rdy, 1)

            mlp(1, C_MLP1, finish_last)
            dve.wait_ge(fss_mm, 1)
            link(dve.tensor_scalar(n4f[:, 0, :], ps[:, 7, 0:QB], 1.0 / D, EPS, ALU.mult, ALU.add))
            inverse_root(n4f[:, 0, :], n4f[:, 1, :], n4f[:, 2, :], n4f[:, 3, :], rfin, 5).then_inc(rfin_rdy, 1)
            dve.wait_ge(rfin_rdy, 1)
            dve.wait_ge(ft_copied, KT)
            for i in range(2):
                dve.tensor_scalar(otok[:, i, :], otok[:, i, :], rfin[:, i:i + 1], None, ALU.mult).then_inc(o_dve, 1)

        @block.tensor
        def _(pe):
            def product(dst, ah, al, bh, bl, start, stop):
                pe.matmul(dst, ah, bl, start=start, stop=False)
                pe.matmul(dst, ah, bh, start=False, stop=False)
                return pe.matmul(dst, al, bh, start=False, stop=stop)

            pe.wait_ge(const_rdy, 3)
            for i in range(QB):
                pe.wait_ge(x_in[i], 16)

            def transpose_x(k):
                for i in range(QB):
                    last = pe.transpose(ps[:, k % 4, P * i:P * i + P], xtok[:, i, P * k:P * k + P], ident[:, :])
                last.then_inc(xt_rdy, 1)

            for k in range(4):
                transpose_x(k)
            pe.wait_ge(vec_in, 16 * 14)
            pe.transpose(ps[:, 7, 0:V_ROWS], vrow[0:V_ROWS, 0, :], ident[0:V_ROWS, 0:V_ROWS])
            pe.transpose(ps[:, 7, V_DW:V_DW + P], vrow[:, 1, :], ident[:, :])
            rest = TAPS * KT - P
            pe.transpose(ps[:, 7, V_DW + P:V_ALL], vrow[0:rest, 2, :], ident[0:rest, 0:rest]).then_inc(vt_rdy, 1)
            pe.wait_ge(relb_in, 32)
            for h in range(2):
                last = pe.matmul(ps[0:HEADS, 5 + h, 0:320], relb, brow[:, 320 * h:320 * h + 320], start=True, stop=True)
            last.then_inc(rev_mm, 1)
            for k in range(4, KT):
                pe.wait_ge(xt_copied, k - 3)
                transpose_x(k)
            pe.wait_ge(rev_rdy, 2)
            pe.wait_ge(vcol_rdy, 1)
            for k in range(KT):
                pe.wait_ge(mv_lo, k + 1)
                c, kk = C_WIN + k // 4, k % 4
                if kk == 0:
                    pe.wait_ge(w_lo, c + 1)
                w = slice(W_IN * kk, W_IN * kk + W_IN)
                for i in range(QB):
                    t = slice(P * i, P * i + P)
                    last = product(ps[:, 4 + i, 0:W_IN], movh[:, k, t], movl[:, k, t], wh[:, c, w], wl[:, c, w],
                                   k == 0, k == KT - 1)
                    if k == KT - 1:
                        last.then_inc(pin_rdy, 1)
            pe.wait_ge(projn_q, QB)
            for t in range(4):
                if t == 2:
                    pe.wait_ge(projn_rdy, 1)
                for i in range(QB):
                    last = pe.transpose(ps[:, t, P * i:P * i + P], projn[:, i, P * t:P * t + P], ident[:, :])
                last.then_inc(ct_rdy, 1)

            pe.wait_ge(c_lo, 4)
            pe.wait_ge(proj_rdy, QB)
            pe.wait_ge(w_lo, C_QIDX + 2)
            for t in range(4):
                for k in range(2):
                    w = slice(P * t, P * t + P)
                    last = product(ps[:, 4 + t, :], wh[:, (C_QIDX + k) % 2, w], wl[:, (C_QIDX + k) % 2, w], ch[:, k, :],
                                   cl[:, k, :], k == 0, k == 1)
                last.then_inc(qi_rdy, 1)
            pe.wait_ge(qi_lo, 4)
            s = 0
            for i in range(1, QB):
                for h in range(IDX_HEADS):
                    if s >= 4:
                        pe.wait_ge(sc_relu, s - 3)
                    half, t, n = slice(64 * (h % 2), 64 * (h % 2) + 64), slice(P * i, P * i + P), P * (i + 1)
                    product(ps[:, s % 4, 0:n], qiH[half, h // 2, t], qiL[half, h // 2, t], ch[half, 3, 0:n],
                            cl[half, 3, 0:n], True, True).then_inc(sc_rdy, 1)
                    s += 1

            pe.wait_ge(sc_relu, s)
            pe.sem_inc(pr_rdy, FREE)
            with pe.Fori(0, PAIRS // 2) as g:
                for b in range(2):
                    p = 2 * g + b
                    wH, wL = swH[:, b, :, :], swL[:, b, :, :]
                    pe.wait_ge(sw_lo, p + 1)
                    for which in range(3):
                        pe.wait_ge(pr_lo, 3 * p + (FREE + which - 5))
                        bank = ps[:, 3 * b + which, :]
                        if which == 0:
                            for k in range(2):
                                last = product(bank, wH[:, k, :], wL[:, k, :], ch[:, k, :], cl[:, k, :], k == 0,
                                               k == 1)
                        elif which == 1:
                            last = product(bank, wH[:, 2, :], wL[:, 2, :], ch[:, 2, :], cl[:, 2, :], True, True)
                        else:
                            for j in range(QB):
                                t = slice(P * j, P * j + P)
                                last = product(bank[:, t], ch[:, 2, t], cl[:, 2, t], wH[:, 3, :], wL[:, 3, :], True,
                                               True)
                        last.then_inc(pr_rdy, 1)

            def logits(step, f, p, e):
                half = slice(64 * e, 64 * e + 64)
                for ii in range(2):
                    i = 2 * f + ii
                    t, w = slice(P * i, P * i + P), slice(0, P * (i + 1))
                    if step:
                        pe.wait_ge(lg_done, 2 * step + ii - 1)
                    product(ps[:, 2 + ii, w], *(x[half, p, y] for x, y in
                                                ((qkvH[0], t), (qkvL[0], t), (qkvH[1], w), (qkvL[1], w))),
                            True, True).then_inc(lg_rdy, 1)

            def transposes(step, f, p, e):
                for ii in range(2):
                    i = 2 * f + ii
                    pe.wait_ge(nr_done, 2 * step + ii + 1)
                    if step:
                        pe.wait_ge(pt_lo, 2 * step + ii - 1)
                    for j in range(i + 1):
                        last = pe.transpose(ps[:, 4 + ii, P * j:P * j + P],
                                            L[:, e, OFF[i] + P * j:OFF[i] + P * j + P], ident[:, :])
                    last.then_inc(pt_rdy, 1)

            def head_output(step, f, p, e):
                pe.wait_ge(pt_lo, 2 * step + 2)
                if step >= 2:
                    pe.wait_ge(o_lo, step - 1)
                for j in range(2 * f + 2):
                    keys, t = slice(P * j, P * j + P), slice(0 if j <= 2 * f else P, 2 * P)
                    last = product(ps[:, 6 + e, t], qkvH[2][:, p, keys], qkvL[2][:, p, keys], ptH[:, e, j, t],
                                   ptL[:, e, j, t], j == 0, j == 2 * f + 1)
                last.then_inc(pv_rdy, 1)

            pe.wait_ge(pr_lo, 3 * PAIRS + FREE)
            logits(0, 0, 0, 0)
            logits(1, 0, 0, 1)
            transposes(0, 0, 0, 0)
            for step in range(STEPS):
                f, pair, e = step // HEADS, step % HEADS // 2, step % 2
                for work, d in ((logits, 2), (transposes, 1), (head_output, 0)):
                    head = later(f, pair, e, d)
                    if head:
                        work(*head)

            def weight_product(bank, c, h, k, n, mh, ml):
                w = slice(256 * k + P * h, 256 * k + P * h + P)
                return product(ps[:, bank, :], wh[:, c % 2, w], wl[:, c % 2, w], mh[:, k, :], ml[:, k, :], k == 0,
                               k == n - 1)

            for t in range(KT):
                c, h = C_WO + t // 2, t % 2
                if h == 0:
                    pe.wait_ge(w_lo, c + 1)
                if t >= 4:
                    pe.wait_ge(x_upd, t - 3)
                for k in range(KT):
                    if t == 0:
                        pe.wait_ge(o_lo, HEADS + 2 * k + 2)
                    last = weight_product(t % 4, c, h, k, KT, hidh, hidl)
                last.then_inc(mm_done, 1)

            def square_sums(f):
                pe.wait_ge(ss_add, KT * (f + 1))
                pe.matmul(ps[:, 4, :], ones[:, :], ss, start=True, stop=True).then_inc(ss_mm, 1)

            def mlp(layer, c0, mv0, f, after):
                t0 = tile_of(c0)

                def tile(g, u):
                    c, h = c0 + u // 2, u % 2
                    if h == 0:
                        pe.wait_ge(w_lo, 8 * g + (c + 1))
                    if u < 4:
                        pe.wait_ge(x_upd, 8 * g + (UPD_MLP[layer] - 4 + u + 1))
                    elif u < 12:
                        pe.wait_ge(relu_rdy, 8 * g + (8 * GROUPS * layer + u - 3))
                    else:
                        pe.wait_ge(x_upd, 8 * g + (UPD_MLP[layer] + u - 11))
                    for k in range(KT):
                        if u == 0 and isinstance(g, int) and g == 0:
                            pe.wait_ge(mv_lo, mv0 + k + 1)
                        if u == 8:
                            pe.wait_ge(hid_lo, 8 * g + (CREDITS + HID_MLP[layer] + k + 1))
                        mh, ml = (movh, movl) if u < 8 else (hidh, hidl)
                        last = weight_product((t0 + u) % 4, c, h, k, KT, mh, ml)
                    last.then_inc(mm_done, 1)

                for u in range(16):
                    tile(0, u)
                    if u == 0:
                        square_sums(f)
                with pe.Fori(1, GROUPS - (1 if after else 0)) as g:
                    for u in range(16):
                        tile(g, u)
                if after:
                    for u in range(16):
                        tile(GROUPS - 1, u)
                        if u > 8:
                            after(u - 9)

            mlp(0, C_MLP0, KT, 0, None)

            t0 = tile_of(C_PW1)
            for t in range(2 * KT):
                c, h = C_PW1 + t // 2, t % 2
                if h == 0:
                    pe.wait_ge(w_lo, c + 1)
                if t < 4:
                    pe.wait_ge(x_upd, UPD_FINAL[1] + KT - 4 + t + 1)
                else:
                    pe.wait_ge(gate_read, t - 3)
                for k in range(KT):
                    if t == 0:
                        pe.wait_ge(mv_lo, 2 * KT + k + 1)
                    last = weight_product((t0 + t) % 4, c, h, k, KT, movh, movl)
                last.then_inc(mm_done, 1)
                if t == 1:
                    square_sums(1)
            for m in range(KT):
                pe.wait_ge(conv_rdy, m + 1)
                last = pe.matmul(ps[:, 5, :], ones[:, :], conv[:, m, :], start=m == 0, stop=m == KT - 1)
            last.then_inc(mean_mm, 1)
            for m in range(KT):
                pe.wait_ge(dsq_rdy, m + 1)
                pe.matmul(ps[:, 6, :], ones[:, :], tg[:, m % 2, :], start=m == 0, stop=m == KT - 1).then_inc(var_mm, 1)
            t0 = tile_of(C_PW2)
            for t in range(KT):
                c, h = C_PW2 + t // 2, t % 2
                if h == 0:
                    pe.wait_ge(w_lo, c + 1)
                if t >= 4:
                    pe.wait_ge(x_upd, UPD_FINAL[2] + t - 3)
                else:
                    pe.wait_ge(gate_read, 2 * KT - 3 + t)
                for k in range(KT):
                    if t == 0:
                        pe.wait_ge(hid_lo, CREDITS + HID_MLP[1] - KT + k + 1)
                    last = weight_product((t0 + t) % 4, c, h, k, KT, hidh, hidl)
                last.then_inc(mm_done, 1)

            def transpose_out(m):
                pe.wait_ge(ft_rdy, m + 1)
                if m >= 2:
                    pe.wait_ge(ft_copied, m - 1)
                for i in range(QB):
                    last = pe.transpose(ps[:, 5 + m % 2, P * i:P * i + P], ft[:, m % 2, P * i:P * i + P], ident[:, :])
                last.then_inc(ftt_rdy, 1)

            mlp(1, C_MLP1, 3 * KT, 2, transpose_out)
            transpose_out(KT - 1)
            pe.wait_ge(ss_add, 4 * KT)
            for i in range(QB):
                last = pe.matmul(ps[:, 7, i:i + 1], ss[:, P * i:P * i + P], ones[:, 0:1], start=True, stop=True)
            last.then_inc(fss_mm, 1)


def kernel(**inputs):
    import math as _math
    import numpy as _np
    import concourse.bacc as _bacc
    from concourse import mybir as _mybir
    from concourse.bass_utils import run_bass_kernel_spmd as _run

    dist = _np.maximum(SEQ - 1 - _np.arange(REV), 0)
    near = NB // 2
    large = near + (_np.log(_np.maximum(dist, 1).astype(_np.float32) / near) / _np.float32(_math.log(128 / near))
                    * (NB - near)).astype(_np.int32)
    bucket = _np.where(dist < near, dist, _np.minimum(large, NB - 1))
    bucket_rows = (bucket[None, :] == _np.arange(NB)[:, None]).astype(_np.float32)

    nc = _bacc.Bacc("TRN2", target_bir_lowering=False, num_devices=1)
    names = ("x", "norm_mix", "norm_mlp", "norm_final", "rel_bias", "attn_w_in", "attn_q_norm", "attn_kv_norm",
             "attn_kidx_norm", "attn_w_qidx", "attn_w_uq", "attn_w_uk", "attn_w_uv", "attn_w_o", "conv_w_pw1",
             "conv_b_pw1", "conv_w_dw", "conv_b_dw", "conv_ln_g", "conv_ln_b", "conv_w_pw2", "conv_b_pw2",
             "mlp_w_up", "mlp_w_down")
    arrays, args = {}, []
    for name in names:
        arrays[name] = _np.ascontiguousarray(inputs[name])
    arrays["norm_final"] = arrays["norm_final"].reshape(1, D)
    arrays["bucket_rows"] = bucket_rows
    for name, a in arrays.items():
        args.append(nc.dram_tensor(name, a.shape, _mybir.dt.float32, kind="ExternalInput").ap())
    args.append(nc.dram_tensor("out", (1, SEQ, D), _mybir.dt.float32, kind="ExternalOutput").ap())
    program(nc, *args)
    r = _run(nc, [arrays], core_ids=[0])
    return r.results[0]["out"]
```

```python
from contextlib import ExitStack

import concourse.bass as bass
from concourse import mybir
from concourse.alu_op_type import AluOpType as ALU

F32 = mybir.dt.float32
F32R = mybir.dt.float32r
ACT = mybir.ActivationFunctionType

P = 128
SEQ = 512
D = 1024
KT = D // P
QB = SEQ // P
HEADS = 16
PAIRS = HEADS // 2
D_NOPE = 64
D_CQ, D_CKV = 256, 128
IDX_HEADS, IDX_DIM = 8, 64
W_IN = D_CQ + D_CKV + IDX_DIM + IDX_HEADS
TOPK = min(256, SEQ // 4)
NB = 32
TAPS = 31
DVE_TAPS = (16, 16, 16, 14)
PE_TAPS = (4, 4, 4, 10)
ACT_TAPS = tuple(TAPS - a - b for a, b in zip(DVE_TAPS, PE_TAPS))
D_FF = 4 * D
EPS = 1e-6
MASKED = -1e30
NOT_YET = -3e38
TAKEN = -3.4e38

CHUNK = 16 * P
GROUPS = D_FF // P // 8
REV = SEQ + P

BLK = [0, 128, 384, 768, 1280]
OFF = [0, 128, 0, 384]
STEPS = 2 * HEADS
SBLK = [None, 0, 256, 640, 1152]

V_NMIX, V_NMLP, V_BP1, V_BDW, V_LNG, V_LNB, V_BP2, V_NFIN, V_QN, V_KVN, V_KIN = (
    0, 16, 32, 48, 56, 64, 72, 80, 88, 90, 91)
V_ROWS = 92
V_DW = V_ROWS
V_ALL = V_DW + TAPS * KT

C_WIN, C_QIDX, C_WO = 0, 2, 4
C_MLP0 = C_WO + 4
C_PW1 = C_MLP0 + 8 * GROUPS
C_PW2 = C_PW1 + 8
C_MLP1 = C_PW2 + 4

UPD_MLP = (KT, KT + KT * GROUPS + KT)
UPD_FINAL = (0, KT * GROUPS, KT * GROUPS + KT, 2 * KT * GROUPS + KT)
HID_MLP = (0, 8 * GROUPS + KT)
CREDITS, PROJ_CREDITS = 2, 6
PROJ_BANK = ((4, 5, 6), (7, 0, 1))


def tile_of(c):
    return 2 * (c - C_WO)


def raw_value(c):
    return sum(32 if C_PW1 <= d < C_PW2 else 16 for d in range(c % 2, c + 1, 2))


def program(nc, x, norm_mix, norm_mlp, norm_final, rel_bias, w_in, q_norm, kv_norm, kidx_norm, w_qidx, w_uq, w_uk,
            w_uv, w_o, w_pw1, b_pw1, w_dw, b_dw, ln_g, ln_b, w_pw2, b_pw2, w_up, w_down, bucket_rows, out):
    rev_dram = nc.dram_tensor("reversed_bias", (HEADS, P * REV), F32, kind="Internal").ap()
    ctx = ExitStack()
    with ctx:
        def sb(name, shape, dt=F32):
            return ctx.enter_context(nc.sbuf_tensor(name, shape, dt))

        def sem(name):
            return ctx.enter_context(nc.semaphore(name))

        xT = sb("xT", [P, KT, SEQ])
        movh = sb("movh", [P, KT, SEQ], F32R)
        movl = sb("movl", [P, KT, SEQ], F32R)
        hidh = sb("hidh", [P, KT, SEQ], F32R)
        hidl = sb("hidl", [P, KT, SEQ], F32R)
        raw = sb("raw", [P, 2, CHUNK])
        wh = sb("wh", [P, 2, CHUNK], F32R)
        wl = sb("wl", [P, 2, CHUNK], F32R)
        ch = sb("ch", [P, 4, SEQ], F32R)
        cl = sb("cl", [P, 4, SEQ], F32R)
        ptH = sb("ptH", [P, 2, QB, 2 * P], F32R)
        ptL = sb("ptL", [P, 2, QB, 2 * P], F32R)
        S1 = sb("S1", [P, 11392])
        ident = sb("ident", [P, P])
        ones = sb("ones", [P, P])
        vcol = sb("vcol", [P, V_ALL])
        small = sb("small", [P, 224])

        junk = S1[:, 0:4096].rearrange("p (i n) -> p i n", i=QB)
        vrow = S1[:, 4096:4480].rearrange("p (r n) -> p r n", r=3)
        relb = S1[0:NB, 4480:4480 + HEADS]
        revs = S1[0:HEADS, 4496:4496 + REV]
        brow = S1[0:NB, 5136:5136 + REV]
        proj = S1[:, 4096:4096 + QB * W_IN].rearrange("p (i n) -> p i n", i=QB)
        projn = S1[:, 5920:5920 + QB * 512].rearrange("p (i n) -> p i n", i=QB)
        xtok = S1[:, 7168:11264].rearrange("p (i n) -> p i n", i=QB)
        rawqkv = S1[:, 0:4096].rearrange("p (w n) -> p w n", w=4)
        mask = S1[:, 4096:5376]
        tb = S1[:, 5376:6400].rearrange("p (b n) -> p b n", b=2)
        bm = (S1[:, 10368:11264], S1[:, 6400:7296])
        score = S1[:, 7424:8576]
        relu_s = S1[:, 8576:9600].rearrange("p (b n) -> p b n", b=2)
        L = S1[:, 8576:10368].rearrange("p (b n) -> p b n", b=2)
        four = lambda t: t.rearrange("p b n -> p (b n)").rearrange("p (k n) -> p k n", n=SEQ)
        qkvH, qkvL = (hidh, movh, four(wh[:, :, :])), (hidl, movl, four(wl[:, :, :]))
        qiH, qiL = (t[:, :, :, :].rearrange("p b j n -> p (b j n)").rearrange("p (k n) -> p k n", n=SEQ)
                    for t in (ptH, ptL))
        swH, swL = (t[2][:, 6:8, :].rearrange("p b (w n) -> p b w n", n=P) for t in (qkvH, qkvL))
        rt = S1[:, 0:1024].rearrange("p (b n) -> p b n", b=2)
        sqt = S1[:, 1024:2048].rearrange("p (b n) -> p b n", b=2)
        dt = S1[:, 2048:3072].rearrange("p (b n) -> p b n", b=2)
        sqx = S1[:, 3072:4096].rearrange("p (b n) -> p b n", b=2)
        ss = S1[:, 4096:4608]
        rbc = S1[:, 4608:5120]
        GW = TAPS - 1 + SEQ
        RING = 4
        conv = S1[:, 0:4096].rearrange("p (k n) -> p k n", k=KT)
        glu = S1[:, 5120:5120 + RING * GW].rearrange("p (b n) -> p b n", b=RING)
        tg = S1[:, 7296:8320].rearrange("p (b n) -> p b n", b=2)
        partials = (conv[:, KT - 2:KT, :], S1[:, 8320:9344].rearrange("p (b n) -> p b n", b=2))
        tapb = S1[:, 9344:10880].rearrange("p (b n) -> p b n", b=3)
        diags = [S1[:, o:o + P] for o in (*range(4096, 4608, P), *range(10880, 11392, P))]
        rdiag = tapb[:, 0, :].rearrange("p (i n) -> p i n", i=QB)
        sg, mean = tapb[:, 0:2, :], tapb[:, 2, :]
        otok = S1[:, 5120:9216].rearrange("p (i n) -> p i n", i=QB)
        ft = S1[:, 9216:10240].rearrange("p (b n) -> p b n", b=2)

        ssq = small[:, 0:4]
        r1 = small[:, 4:8]
        n4 = small[:, 8:24].rearrange("p (a n) -> p a n", a=4)
        stat = small[:, 24:36]
        rs = small[:, 36:48]
        n12 = small[:, 48:96].rearrange("p (a n) -> p a n", a=4)
        wsc = small[:, 96:128]
        m8 = (small[:, 128:136], small[:, 188:196])
        rmax = small[:, 136:144].rearrange("p (b n) -> p b n", b=2)
        nmax = small[:, 144:152].rearrange("p (b n) -> p b n", b=2)
        n4f = small[:, 168:184].rearrange("p (a n) -> p a n", a=4)
        rfin = small[:, 184:188]
        sums = small[:, 152:160].rearrange("p (b n) -> p b n", b=2)
        rsum = small[:, 160:168].rearrange("p (b n) -> p b n", b=2)

        ps = ctx.enter_context(nc.psum_tensor("ps", [P, 8, 512], F32))

        x_in = [sem(f"x_in{i}") for i in range(QB)]
        raw_in = [sem(f"raw_in{b}") for b in range(2)]
        tb_in = [sem(f"tb_in{b}") for b in range(2)]
        vec_in, relb_in, qkv_in, rev_out, out_done = map(sem, ("vec_in", "relb_in", "qkv_in", "rev_out", "out_done"))
        w_hi, w_lo = map(sem, ("w_hi", "w_lo"))
        const_rdy, vt_rdy, vcol_rdy, rev_mm, rev_rdy = map(sem, ("const_rdy", "vt_rdy", "vcol_rdy", "rev_mm",
                                                                 "rev_rdy"))
        xt_rdy, xt_copied, mv_hi, mv_lo = map(sem, ("xt_rdy", "xt_copied", "mv_hi", "mv_lo"))
        ssq_rdy, inv_rdy, act_root, chain, r1_rdy = map(sem, ("ssq_rdy", "inv_rdy", "act_root", "chain", "r1_rdy"))
        pin_rdy, proj_rdy, stat_rdy, projn_rdy = map(sem, ("pin_rdy", "proj_rdy", "stat_rdy", "projn_rdy"))
        rs_rdy, projn_q = map(sem, ("rs_rdy", "projn_q"))
        ct_rdy, c_hi, c_lo, qi_rdy, qi_hi, qi_lo = map(sem, ("ct_rdy", "c_hi", "c_lo", "qi_rdy", "qi_hi", "qi_lo"))
        sc_rdy, sc_relu, sc_acc, sc_causal, taken = map(sem, ("sc_rdy", "sc_relu", "sc_acc", "sc_causal", "taken"))
        mask0_rdy, mask_rdy = map(sem, ("mask0_rdy", "mask_rdy"))
        sw_hi, sw_lo, pr_rdy, pr_hi, pr_lo = map(sem, ("sw_hi", "sw_lo", "pr_rdy", "pr_hi", "pr_lo"))
        seen = sem("seen")
        bm_rdy, lg_rdy, lg_done, nm_rdy, ex_done = map(sem, ("bm_rdy", "lg_rdy", "lg_done", "nm_rdy", "ex_done"))
        rc_rdy, pt_rdy, pt_hi, pt_lo = map(sem, ("rc_rdy", "pt_rdy", "pt_hi", "pt_lo"))
        nr_done = [sem(f"nr_done{ii}") for ii in range(2)]
        pv_rdy, o_hi, o_lo = map(sem, ("pv_rdy", "o_hi", "o_lo"))
        mm_done, x_upd, sq_rdy, ss_add, ss_mm = map(sem, ("mm_done", "x_upd", "sq_rdy", "ss_add", "ss_mm"))
        relu_rdy, sqt_rdy, hid_hi, hid_lo, dt_rdy = map(sem, ("relu_rdy", "sqt_rdy", "hid_hi", "hid_lo", "dt_rdy"))
        pad_rdy, gate_read, sg_rdy, glu_rdy, conv_rdy = map(sem, ("pad_rdy", "gate_read", "sg_rdy", "glu_rdy",
                                                                  "conv_rdy"))
        tp_rdy, part_add, dve_taps, diag_rdy, diag_used = map(sem, ("tp_rdy", "part_add", "dve_taps", "diag_rdy",
                                                                    "diag_used"))
        pe_added, rd_rdy, rb_mm, var_copied = map(sem, ("pe_added", "rd_rdy", "rb_mm", "var_copied"))
        mean_mm, dev_rdy, dsq_rdy, var_mm = map(sem, ("mean_mm", "dev_rdy", "dsq_rdy", "var_mm"))
        zt_rdy, zs_rdy, ft_rdy, ftt_rdy, ft_copied, fss_mm = map(sem, ("zt_rdy", "zs_rdy", "ft_rdy", "ftt_rdy",
                                                                       "ft_copied", "fss_mm"))
        rfin_rdy, o_dve, o_act = map(sem, ("rfin_rdy", "o_dve", "o_act"))

        def col(v, k=0):
            return vcol[:, v + k:v + k + 1]

        def flat(ap):
            return ap.rearrange("p a n -> p (a n)")

        def load_vectors(engine, *vectors):
            for v, src in vectors:
                rows = src.rearrange("l (k p) -> (l k) p", p=P)
                engine.dma_start(vrow[v:v + rows.shape[0], 0, :], rows).then_inc(vec_in, 16)

        def tap_products():
            n = k = 0
            for q, taps in enumerate(ACT_TAPS):
                for s in range(taps):
                    for e in range(2):
                        yield 2 * q + e, s, e, n, k
                        n += 1
                        k += s > 0

        def diagonals(i):
            q = i // 2
            d = 2 * sum(PE_TAPS[:q])
            for h in range(2):
                for j in range(DVE_TAPS[q], DVE_TAPS[q] + PE_TAPS[q]):
                    yield d, i + h, j
                    d += 1

        def later(f, g, hh, d):
            step, pair, e = 2 * g + (HEADS * f + hh + d), g + (hh + d) // 2, (hh + d) % 2
            if isinstance(g, int) and pair >= PAIRS:
                f, pair = f + 1, pair - PAIRS
            return (step, f, pair, e) if f < 2 else None

        def passes(engine, step):
            for f in range(2):
                with engine.Fori(0, PAIRS // 2 - 1) as g:
                    for hh in range(4):
                        step(f, 2 * g + hh // 2, hh % 2)
                for hh in range(4):
                    step(f, PAIRS - 2 + hh // 2, hh % 2)

        def wait_apart(engine):
            engine.sem_inc(seen, 1)

        block = ctx.enter_context(nc.Block())

        @block.sync
        def _(sp):
            def chunk_load(c, src):
                if c >= 2:
                    sp.wait_ge(w_lo, c - 1)
                k, n = src.shape[1], src.shape[2]
                sp.dma_start(raw[:, c % 2, 0:k * n].rearrange("p (k n) -> p k n", k=k), src).then_inc(
                    raw_in[c % 2], 16)

            x_v = x.rearrange("o (i p) d -> (o p) i d", p=P)
            for i in range(QB):
                sp.dma_start(xtok[:, i, :], x_v[:, i, :]).then_inc(x_in[i], 16)
            load_vectors(sp, (V_BP2, b_pw2), (V_NFIN, norm_final), (V_QN, q_norm), (V_KVN, kv_norm))
            for half in range(2):
                sp.dma_start(vrow[V_KIN:V_KIN + 1, 0, 64 * half:64 * half + 64], kidx_norm).then_inc(vec_in, 16)
            dw_rows = w_dw.rearrange("o j (k p) -> (o j k) p", p=P)
            sp.dma_start(vrow[:, 1, :], dw_rows[0:P, :]).then_inc(vec_in, 16)
            sp.dma_start(vrow[0:TAPS * KT - P, 2, :], dw_rows[P:TAPS * KT, :]).then_inc(vec_in, 16)
            w_in_v = w_in.rearrange("o (c k p) n -> (o p) c k n", p=P, k=4)
            for c in range(2):
                chunk_load(C_WIN + c, w_in_v[:, c])
            sp.wait_ge(rev_rdy, 2)
            for h in range(0, HEADS, 4):
                sp.dma_start(rev_dram[h:h + 4].rearrange("h (r n) -> h r n", r=P),
                             revs[h:h + 4, :].unsqueeze(1).to_broadcast([4, P, REV])).then_inc(rev_out, 16)
            w_qidx_v = w_qidx.rearrange("o (k p) n -> (o p) k n", p=P)
            for k in range(2):
                chunk_load(C_QIDX + k, w_qidx_v[:, k:k + 1, :])
            sp.wait_ge(stat_rdy, 2 * QB)
            sp.dma_start(rawqkv[:, 0:2, :], w_uq.rearrange("o (k p) n -> (o p) k n", p=P)).then_inc(qkv_in, 16)
            sp.dma_start(rawqkv[:, 2, :], w_uk.rearrange("o c h d -> (o c) (h d)")).then_inc(qkv_in, 16)
            sp.dma_start(rawqkv[:, 3, :], w_uv.rearrange("o c h d -> (o c) (h d)")).then_inc(qkv_in, 16)
            w_o_v = w_o.rearrange("o (k p) (c n) -> (o p) c k n", p=P, n=256)
            chunk_load(C_WO, w_o_v[:, 0])
            sp.wait_ge(rev_out, 64)
            chunk_load(C_WO + 1, w_o_v[:, 1])
            sp.wait_ge(c_lo, 4)
            def bias_load(step, f, p, e):
                toeplitz = rev_dram[bass.ds(2 * p + e, 1), P - 1:P - 1 + P * (REV - 1)].rearrange(
                    "o (r n) -> (o r) n", r=P)
                near = slice(SEQ - 2 * P * (f + 1), SEQ)
                sp.dma_start(tb[:, e, near], toeplitz[:, near]).then_inc(tb_in[e], 16)

            def bias_step(f, g, hh):
                head = later(f, g, hh, 2)
                if head:
                    sp.wait_ge(bm_rdy, 2 * head[0] - 2)
                    bias_load(*head)

            bias_load(0, 0, 0, 0)
            bias_load(1, 0, 0, 1)
            passes(sp, bias_step)
            for c in range(2, 4):
                chunk_load(C_WO + c, w_o_v[:, c])

            def mlp_loads(layer, c0):
                up_v = w_up.rearrange("l (k p) n -> l p k n", p=P)[layer]
                down_v = w_down.rearrange("l (g k p) n -> l p g k n", p=P, k=8)[layer]
                with sp.Fori(0, GROUPS) as g:
                    for j in range(8):
                        c = c0 + j
                        sp.wait_ge(w_lo, 8 * g + (c - 1))
                        if j < 4:
                            src = up_v[:, :, bass.ds(g * 1024 + j * 256, 256)]
                        else:
                            src = down_v[:, bass.ds(g, 1), :, (j - 4) * 256:(j - 3) * 256].rearrange(
                                "p o k n -> p (o k) n")
                        sp.dma_start(raw[:, c % 2, :].rearrange("p (k n) -> p k n", k=8), src).then_inc(
                            raw_in[c % 2], 16)

            mlp_loads(0, C_MLP0)
            pw1_v = w_pw1.rearrange("o (k p) (h c n) -> (o p) c k h n", p=P, h=2, n=P)
            for i in range(8):
                c = C_PW1 + i
                sp.wait_ge(w_lo, c - 1)
                for h in range(2):
                    sp.dma_start(raw[:, c % 2, :].rearrange("p (k h n) -> p k h n", k=KT, h=2)[:, :, h, :],
                                 pw1_v[:, i, :, h, :]).then_inc(raw_in[c % 2], 16)
            pw2_v = w_pw2.rearrange("o (k p) (c n) -> (o p) c k n", p=P, n=256)
            for c in range(4):
                chunk_load(C_PW2 + c, pw2_v[:, c])
            mlp_loads(1, C_MLP1)
            out_v = out.rearrange("o (i p) d -> (o p) i d", p=P)
            for i in range(QB):
                sp.wait_ge(o_dve if i < 2 else o_act, i % 2 + 1)
                sp.dma_start(out_v[:, i, :], otok[:, i, :]).then_inc(out_done, 16)
            sp.wait_ge(out_done, 16 * QB)

        @block.gpsimd
        def _(pool):
            pool.memset(ident[:, :], 0.0).then_inc(const_rdy, 1)
            pool.memset(ones[:, :], 1.0).then_inc(const_rdy, 1)
            pool.wait_ge(const_rdy, 2)
            pool.affine_select(out=ident[:, :], in_=ident[:, :], compare_op=ALU.not_equal, fill=1.0, base=0,
                               pattern=[[-1, P]], channel_multiplier=1).then_inc(const_rdy, 1)
            pool.wait_ge(projn_rdy, 1)
            pool.wait_ge(projn_q, QB)
            pool.memset(mask[:, 0:P], 0.0).then_inc(mask0_rdy, 1)
            pool.wait_ge(mask0_rdy, 1)
            pool.affine_select(out=mask[:, 0:P], in_=mask[:, 0:P], compare_op=ALU.is_ge, fill=MASKED, base=0,
                               pattern=[[-1, P]], channel_multiplier=1).then_inc(mask0_rdy, 1)

            def slices_lo(p, b):
                pool.wait_ge(sw_hi, p + 1)
                wait_apart(pool)
                pool.tensor_tensor(swL[:, b, :, :], rawqkv[:, :, bass.ds(p * P, P)], swH[:, b, :, :].bitcast(F32),
                                   ALU.subtract).then_inc(sw_lo, 1)

            slices_lo(0, 0)
            slices_lo(1, 1)
            for i in range(1, QB):
                pool.wait_ge(sc_acc, IDX_HEADS * i)
                diag = score[:, SBLK[i + 1] - P:SBLK[i + 1]]
                pool.affine_select(out=diag, in_=diag, compare_op=ALU.is_ge, fill=NOT_YET, base=0,
                                   pattern=[[-1, P]], channel_multiplier=1).then_inc(sc_causal, 1)
            with pool.Fori(1, PAIRS // 2) as g:
                for b in range(2):
                    slices_lo(2 * g + b, b)

            def bias_and_mask(step, f, p, e):
                pool.wait_ge(tb_in[e], (HEADS // 2 * f + 1 + p) * 16)
                if isinstance(step, int) and step < 2:
                    pool.wait_ge(mask0_rdy, 2)
                else:
                    pool.wait_ge(lg_done, 2 * step - 2)
                if isinstance(step, int) and step == HEADS * f:
                    pool.wait_ge(mask_rdy, 2 * f + 1)
                for ii in range(2):
                    i = 2 * f + ii
                    pool.tensor_tensor(bm[e][:, OFF[i]:OFF[i] + P * (i + 1)], tb[:, e, SEQ - P * (i + 1):SEQ],
                                       mask[:, BLK[i]:BLK[i + 1]], ALU.add).then_inc(bm_rdy, 1)

            def normalise(step, f, p, e):
                pool.wait_ge(rc_rdy, step + 1)
                wait_apart(pool)
                for ii in range(f, 2):
                    i = 2 * f + ii
                    block = L[:, e, OFF[i]:OFF[i] + P * (i + 1)]
                    pool.tensor_scalar(block, block, rsum[:, e, ii:ii + 1], 1.0, ALU.mult, ALU.mult).then_inc(
                        nr_done[ii], 1)

            def pool_step(f, g, hh):
                normalise(*later(f, g, hh, 0))
                if later(f, g, hh, 2):
                    bias_and_mask(*later(f, g, hh, 2))

            bias_and_mask(0, 0, 0, 0)
            bias_and_mask(1, 0, 0, 1)
            passes(pool, pool_step)

            def sum_squares(f):
                for m in range(KT):
                    pool.wait_ge(sq_rdy, KT * f + m + 1)
                    if m == 0:
                        pool.tensor_scalar(ss, sqx[:, 0, :], 1.0, 1.0, ALU.mult, ALU.mult).then_inc(ss_add, 1)
                    else:
                        pool.wait_ge(ss_add, KT * f + m)
                        pool.tensor_tensor(ss, ss, sqx[:, m % 2, :], ALU.add).then_inc(ss_add, 1)

            sum_squares(0)
            for b in range(RING):
                pool.memset(glu[:, b, 0:TAPS - 1], 0.0).then_inc(pad_rdy, 1)
            pool.wait_ge(ss_mm, 1)
            sum_squares(1)
            for i, s, e, n, k in tap_products():
                if s:
                    pool.wait_ge(tp_rdy, n + 1)
                    if s > 1:
                        pool.wait_ge(part_add, k - 1)
                    partial = partials[i // 2 % 2]
                    pool.tensor_tensor(partial[:, e, :], partial[:, e, :], tapb[:, k % 3, :], ALU.add).then_inc(
                        part_add, 1)
            pool.wait_ge(ss_mm, 2)
            sum_squares(2)
            pool.wait_ge(ss_mm, 3)
            sum_squares(3)

        @block.scalar
        def _(act):
            def split_hi(c, n=CHUNK):
                act.wait_ge(raw_in[c % 2], raw_value(c))
                if c in (C_QIDX, C_QIDX + 1):
                    act.wait_ge(pin_rdy, QB)
                elif c in (C_WO, C_WO + 1):
                    act.wait_ge(pv_rdy, HEADS + HEADS // 2 * (c - C_WO + 1))
                elif c > C_WO + 1:
                    act.wait_ge(mm_done, tile_of(c) - 2)
                act.activation(wh[:, c % 2, 0:n], raw[:, c % 2, 0:n], ACT.Copy).then_inc(w_hi, 1)

            def square_x(f, m):
                if f or m >= 2:
                    act.wait_ge(ss_add, KT * f + m - 1)
                act.activation(sqx[:, m % 2, :], xT[:, m, :], ACT.Square).then_inc(sq_rdy, 1)

            def finish_x(f, m, gain):
                act.wait_ge(x_upd, UPD_FINAL[f] + m + 1)
                act.activation(movh[:, m, :], xT[:, m, :], ACT.Copy, scale=gain).then_inc(mv_hi, 1)
                square_x(f, m)

            def root(dst, src, n):
                act.wait_ge(inv_rdy, n)
                act.activation(dst, src, ACT.Sqrt).then_inc(act_root, 1)

            load_vectors(act, (V_NMIX, norm_mix), (V_NMLP, norm_mlp), (V_BP1, b_pw1), (V_BDW, b_dw), (V_LNG, ln_g),
                         (V_LNB, ln_b))
            act.dma_start(relb, rel_bias).then_inc(relb_in, 16)
            act.dma_start(brow, bucket_rows).then_inc(relb_in, 16)
            split_hi(C_WIN, 4 * W_IN)
            act.wait_ge(vcol_rdy, 1)
            for k in range(KT):
                if k == 2:
                    split_hi(C_WIN + 1, 4 * W_IN)
                act.wait_ge(xt_copied, k + 1)
                act.activation(movh[:, k, :], xT[:, k, :], ACT.Copy, scale=col(V_NMIX, k)).then_inc(mv_hi, 1)
            for i in range(QB):
                act.wait_ge(x_in[i], 16)
                act.activation(junk[:, i, :], xtok[:, i, :], ACT.Square, accum_out=ssq[:, i:i + 1]).then_inc(
                    ssq_rdy, 1)
            root(n4[:, 2, :], n4[:, 1, :], 1)
            act.wait_ge(r1_rdy, 1)
            act.wait_ge(rev_out, 64)
            for i in range(QB):
                act.wait_ge(pin_rdy, i + 1)
                act.activation(proj[:, i, :], ps[:, 4 + i, 0:W_IN], ACT.Copy, scale=r1[:, i:i + 1]).then_inc(
                    proj_rdy, 1)
                act.wait_ge(proj_rdy, i + 1)
                act.activation(junk[:, i, 0:256], proj[:, i, 0:256], ACT.Square,
                               accum_out=stat[:, i:i + 1]).then_inc(stat_rdy, 1)
            root(n12[:, 2, :], n12[:, 1, :], 2)
            act.wait_ge(rs_rdy, 1)
            for i in range(QB):
                act.activation(projn[:, i, 0:256], proj[:, i, 0:256], ACT.Copy, scale=rs[:, i:i + 1]).then_inc(
                    projn_q, 1)
            split_hi(C_QIDX, SEQ)
            split_hi(C_QIDX + 1, SEQ)
            for t in range(4):
                act.wait_ge(ct_rdy, t + 1)
                act.activation(ch[:, t, :], ps[:, t, :], ACT.Copy, scale=col(V_QN, t)).then_inc(c_hi, 1)
            for t in range(4):
                act.wait_ge(qi_rdy, t + 1)
                act.activation(qiH[:, t, :], ps[:, 4 + t, :], ACT.Copy).then_inc(qi_hi, 1)

            def slices_hi(p, b):
                act.activation(swH[:, b, :, :], rawqkv[:, :, bass.ds(p * P, P)], ACT.Copy).then_inc(sw_hi, 1)

            act.wait_ge(qkv_in, 48)
            slices_hi(0, 0)
            slices_hi(1, 1)
            s = 0
            for i in range(1, QB):
                for h in range(IDX_HEADS):
                    act.wait_ge(sc_rdy, s + 1)
                    if s >= 2:
                        act.wait_ge(sc_acc, s - 1)
                    act.activation(relu_s[:, s % 2, 0:P * (i + 1)], ps[:, s % 4, 0:P * (i + 1)],
                                   ACT.Relu).then_inc(sc_relu, 1)
                    s += 1

            def pair_hi(p, b):
                for which in range(3):
                    act.wait_ge(pr_rdy, 3 * p + (which + 1))
                    act.activation(flat(qkvH[which][:, bass.ds(p, 1), :]), ps[:, PROJ_BANK[b][which], :], ACT.Copy,
                                   scale=D_NOPE ** -0.5 if which == 0 else 1.0).then_inc(pr_hi, 1)

            with act.Fori(0, PAIRS // 2 - 1) as g:
                for b in range(2):
                    pair_hi(2 * g + b, b)
                    slices_hi(2 * g + (b + 2), b)
            pair_hi(PAIRS - 2, 0)
            pair_hi(PAIRS - 1, 1)

            def exponentials(step, f, p, e):
                act.wait_ge(nm_rdy, step + 1)
                for ii in range(2):
                    i = 2 * f + ii
                    block = L[:, e, OFF[i]:OFF[i] + P * (i + 1)]
                    act.activation(block, block, ACT.Exp, bias=nmax[:, e, ii:ii + 1],
                                   accum_out=sums[:, e, ii:ii + 1]).then_inc(ex_done, 1)

            def probs_hi(step, f, p, e):
                for ii in range(2):
                    i = 2 * f + ii
                    act.wait_ge(pt_rdy, 2 * step + (ii + 1))
                    act.activation(ptH[:, e, 0:i + 1, P * ii:P * ii + P],
                                   ps[:, 4 + ii, 0:P * (i + 1)].rearrange("p (j n) -> p j n", n=P),
                                   ACT.Copy).then_inc(pt_hi, 1)

            def output_hi(step, f, p, e):
                act.wait_ge(pv_rdy, step + 1)
                act.activation(flat(hidh[64 * e:64 * e + 64, bass.ds(p, 1), 2 * P * f:2 * P * (f + 1)]),
                               ps[64 * e:64 * e + 64, 6 + e, 0:2 * P], ACT.Copy).then_inc(o_hi, 1)

            def act_step(f, g, hh):
                for work, d in ((probs_hi, 1), (exponentials, 2), (output_hi, 0)):
                    head = later(f, g, hh, d)
                    if head:
                        work(*head)
                if f == 1 and isinstance(g, int) and g == PAIRS - 2 and hh == 0:
                    split_hi(C_WO)

            exponentials(0, 0, 0, 0)
            exponentials(1, 0, 0, 1)
            probs_hi(0, 0, 0, 0)
            passes(act, act_step)

            split_hi(C_WO + 1)
            for c in range(4):
                if c:
                    split_hi(C_WO + c + 1)
                for m in (2 * c, 2 * c + 1):
                    finish_x(0, m, col(V_NMLP, m))

            def mlp(layer, c0, finish):
                t0, r0, h0 = tile_of(c0), 8 * GROUPS * layer, HID_MLP[layer]

                def group(g, last):
                    for j in range(8):
                        c = c0 + j + 1
                        if not (last and j == 7):
                            act.wait_ge(raw_in[c % 2], 64 * g + raw_value(c))
                            act.wait_ge(mm_done, 16 * g + (t0 + 2 * j))
                            act.activation(wh[:, c % 2, :], raw[:, c % 2, :], ACT.Copy).then_inc(w_hi, 1)
                        elif layer == 0:
                            split_hi(C_PW1)
                        for m in (2 * j, 2 * j + 1):
                            if j < 4:
                                act.wait_ge(mm_done, 16 * g + (t0 + m + 1))
                                act.wait_ge(hid_lo, 8 * g + (CREDITS + h0 + m - 1))
                                act.activation(rt[:, m % 2, :], ps[:, (t0 + m) % 4, :],
                                               ACT.Relu).then_inc(relu_rdy, 1)
                                act.wait_ge(relu_rdy, 8 * g + (r0 + m + 1))
                                act.activation(hidh[:, m, :], rt[:, m % 2, :], ACT.Square).then_inc(hid_hi, 1)
                            elif last:
                                finish(m - 8)

                with act.Fori(0, GROUPS - 1) as g:
                    group(g, False)
                group(GROUPS - 1, True)

            mlp(0, C_MLP0, lambda m: finish_x(1, m, col(V_NMIX, KT + m)))

            split_hi(C_PW1 + 1)
            split_hi(C_PW1 + 2)
            root(n4f[:, 2, :], n4f[:, 1, :], 3)

            def sigmoids(i):
                for h in range(2):
                    act.wait_ge(gate_read, 2 * (i + h) + 2)
                    act.activation(tg[:, h, :], tg[:, h, :], ACT.Sigmoid, bias=col(V_BP1, KT + i + h)).then_inc(
                        sg_rdy, 1)

            sigmoids(0)
            split_hi(C_PW1 + 3)
            act.wait_ge(ss_mm, 2)
            for i, s, e, n, k in tap_products():
                taps = ACT_TAPS[i // 2]
                if s == e == 0:
                    waiting = list(diagonals(i))
                if s == 0:
                    act.wait_ge(glu_rdy, i + 1)
                    if i >= 4:
                        act.wait_ge(conv_rdy, i - 3)
                    dst = partials[i // 2 % 2][:, e, :]
                else:
                    if k >= 3:
                        act.wait_ge(part_add, k - 2)
                    dst = tapb[:, k % 3, :]
                if k < 3:
                    act.wait_ge(r1_rdy, 2)
                j = TAPS - taps + s
                act.activation(dst, glu[:, i % RING, j:j + SEQ], ACT.Copy, scale=col(V_DW, KT * j + i)).then_inc(
                    tp_rdy, 1)
                if e == 1 and s >= 1:
                    count = len(diags) if s == 1 else 3 if i == KT - 1 or s >= taps - 2 else 0
                    for d, m, j in waiting[:count]:
                        if d >= len(diags):
                            act.wait_ge(diag_used, d - len(diags) + 1)
                        act.activation(diags[d % len(diags)], ident[:, :], ACT.Copy,
                                       scale=col(V_DW, KT * j + m)).then_inc(diag_rdy, 1)
                    del waiting[:count]
                if e == 1 and i < KT - 1 and s == taps - 4:
                    split_hi(C_PW1 + i + 3)
                if e == 1 and i < KT - 1 and s == taps - 1:
                    sigmoids(i + 1)
                    split_hi(C_PW1 + i + 4)
            for m in range(KT):
                act.wait_ge(dev_rdy, m + 1)
                if m >= 2:
                    act.wait_ge(var_mm, m - 1)
                act.activation(tg[:, m % 2, :], conv[:, m, :], ACT.Square).then_inc(dsq_rdy, 1)
            root(n4f[:, 2, :], n4f[:, 1, :], 4)
            act.activation(rmax[:, 0, 0:1], ones[:, 0:1], ACT.Silu).then_inc(zs_rdy, 1)
            act.wait_ge(r1_rdy, 3)
            z0 = HID_MLP[1] - KT
            for m in range(KT):
                act.wait_ge(zt_rdy, m + 1)
                if m >= 2:
                    act.wait_ge(hid_lo, CREDITS + z0 + m - 1)
                act.activation(sg[:, m % 2, :], tg[:, m % 2, :], ACT.Silu, scale=col(V_LNG, m),
                               bias=col(V_LNB, m)).then_inc(zs_rdy, 1)
                act.wait_ge(zs_rdy, m + 2)
                act.activation(hidh[:, m, :], sg[:, m % 2, :], ACT.Copy).then_inc(hid_hi, 1)
            for c in range(4):
                if c:
                    split_hi(C_PW2 + c + 1)
                for m in (2 * c, 2 * c + 1):
                    finish_x(2, m, col(V_NMLP, KT + m))

            def copy_out(m):
                act.wait_ge(ftt_rdy, m + 1)
                act.activation(otok[:, :, P * m:P * m + P], ps[:, 5 + m % 2, :].rearrange("p (i n) -> p i n", n=P),
                               ACT.Copy).then_inc(ft_copied, 1)

            def finish_last(m):
                act.wait_ge(x_upd, UPD_FINAL[3] + m + 1)
                square_x(3, m)
                if m:
                    copy_out(m - 1)

            mlp(1, C_MLP1, finish_last)
            copy_out(KT - 1)
            root(n4f[:, 2, :], n4f[:, 1, :], 5)
            act.wait_ge(rfin_rdy, 1)
            act.wait_ge(ft_copied, KT)
            for i in range(2, QB):
                act.activation(otok[:, i, :], otok[:, i, :], ACT.Copy, scale=rfin[:, i:i + 1]).then_inc(o_act, 1)

        @block.vector
        def _(dve):
            links = [0]

            def link(ins):
                links[0] += 1
                ins.then_inc(chain, 1)
                dve.wait_ge(chain, links[0])

            def split_lo(c, n=CHUNK):
                dve.wait_ge(w_hi, c + 1)
                dve.tensor_tensor(wl[:, c % 2, 0:n], raw[:, c % 2, 0:n], wh[:, c % 2, 0:n].bitcast(F32),
                                  ALU.subtract).then_inc(w_lo, 1)

            def inverse_root(v, inv, y, t, r, n):
                dve.reciprocal(inv, v).then_inc(inv_rdy, 1)
                dve.wait_ge(act_root, n)
                link(dve.tensor_tensor(t, y, y, ALU.mult))
                link(dve.tensor_tensor(t, t, v, ALU.mult))
                link(dve.tensor_scalar(t, t, -0.5, 1.5, ALU.mult, ALU.add))
                return dve.tensor_tensor(r, y, t, ALU.mult)

            def x_lo(n, m, gain):
                dve.wait_ge(mv_hi, n + 1)
                dve.scalar_tensor_tensor(movl[:, m, :], xT[:, m, :], gain, movh[:, m, :].bitcast(F32), ALU.mult,
                                         ALU.subtract).then_inc(mv_lo, 1)

            dve.sem_inc(hid_lo, CREDITS)
            dve.sem_inc(pr_lo, PROJ_CREDITS)

            def copy_x(k):
                dve.wait_ge(xt_rdy, k + 1)
                dve.tensor_copy(xT[:, k, :], ps[:, k % 4, :]).then_inc(xt_copied, 1)

            for k in range(4):
                copy_x(k)
            dve.wait_ge(vt_rdy, 1)
            dve.tensor_copy(vcol[:, :], ps[:, 7, 0:V_ALL]).then_inc(vcol_rdy, 1)
            dve.wait_ge(rev_mm, 1)
            for h in range(2):
                dve.tensor_copy(revs[:, 320 * h:320 * h + 320], ps[0:HEADS, 5 + h, 0:320]).then_inc(rev_rdy, 1)
            dve.wait_ge(vcol_rdy, 1)
            split_lo(C_WIN, 4 * W_IN)
            for k in range(KT):
                if k == 3:
                    split_lo(C_WIN + 1, 4 * W_IN)
                x_lo(k, k, col(V_NMIX, k))
                if k < 4:
                    copy_x(k + 4)
            dve.wait_ge(ssq_rdy, QB)
            link(dve.tensor_scalar(n4[:, 0, :], ssq, 1.0 / D, EPS, ALU.mult, ALU.add))
            inverse_root(n4[:, 0, :], n4[:, 1, :], n4[:, 2, :], n4[:, 3, :], r1, 1).then_inc(r1_rdy, 1)
            for i in range(QB):
                dve.wait_ge(proj_rdy, i + 1)
                for s, a, b in ((1, 256, 384), (2, 384, 448)):
                    last = dve.tensor_tensor_reduce(junk[:, i, a:b], proj[:, i, a:b], proj[:, i, a:b], 1.0, 0.0,
                                                    ALU.mult, ALU.add, stat[:, 4 * s + i:4 * s + i + 1])
                last.then_inc(stat_rdy, 1)
            dve.wait_ge(stat_rdy, 2 * QB)
            for s, n in enumerate((D_CQ, D_CKV, IDX_DIM)):
                link(dve.tensor_scalar(n12[:, 0, 4 * s:4 * s + 4], stat[:, 4 * s:4 * s + 4], 1.0 / n, EPS, ALU.mult,
                                       ALU.add))
            inverse_root(n12[:, 0, :], n12[:, 1, :], n12[:, 2, :], n12[:, 3, :], rs, 2).then_inc(rs_rdy, 1)
            dve.wait_ge(rs_rdy, 1)
            for i in range(QB):
                dve.tensor_scalar(projn[:, i, 256:384], proj[:, i, 256:384], rs[:, 4 + i:5 + i], None, ALU.mult)
                for h in range(2):
                    dve.tensor_scalar(projn[:, i, 384 + 64 * h:448 + 64 * h], proj[:, i, 384:448],
                                      rs[:, 8 + i:9 + i], None, ALU.mult)
                last = dve.tensor_scalar(wsc[:, 8 * i:8 * i + 8], proj[:, i, 448:456],
                                         IDX_HEADS ** -0.5 * IDX_DIM ** -0.5, None, ALU.mult)
            last.then_inc(projn_rdy, 1)
            split_lo(C_QIDX, SEQ)
            split_lo(C_QIDX + 1, SEQ)
            for t in range(4):
                dve.wait_ge(c_hi, t + 1)
                dve.scalar_tensor_tensor(cl[:, t, :], ps[:, t, :], col(V_QN, t), ch[:, t, :].bitcast(F32), ALU.mult,
                                         ALU.subtract).then_inc(c_lo, 1)
            for t in range(4):
                dve.wait_ge(qi_hi, t + 1)
                dve.tensor_tensor(qiL[:, t, :], ps[:, 4 + t, :], qiH[:, t, :].bitcast(F32), ALU.subtract).then_inc(
                    qi_lo, 1)
            def largest(i):
                dve.max(m8[i % 2], score[:, SBLK[i]:SBLK[i + 1]]).then_inc(taken, 1)

            def mark(i):
                part = score[:, SBLK[i]:SBLK[i + 1]]
                dve.match_replace(part, m8[i % 2], part, TAKEN).then_inc(taken, 1)

            def make_mask(i, marked):
                dve.wait_ge(taken, marked)
                dve.tensor_scalar(mask[:, BLK[i]:BLK[i + 1]], score[:, SBLK[i]:SBLK[i + 1]], TAKEN, MASKED,
                                  ALU.not_equal, ALU.mult).then_inc(mask_rdy, 1)

            dve.wait_ge(projn_rdy, 1)
            rounds = TOPK // 8
            s = 0
            for i in range(1, QB):
                for h in range(IDX_HEADS):
                    part, w = score[:, SBLK[i]:SBLK[i + 1]], wsc[:, 8 * i + h:8 * i + h + 1]
                    r = IDX_HEADS * (i - 2) + h
                    if 0 <= r < rounds:
                        dve.wait_ge(sc_causal, 1)
                        if r:
                            dve.wait_ge(taken, 2 * r)
                        largest(1)
                    dve.wait_ge(sc_relu, s + 1)
                    if h == 0:
                        dve.tensor_scalar(part, relu_s[:, s % 2, 0:P * (i + 1)], w, None, ALU.mult).then_inc(sc_acc, 1)
                    else:
                        dve.wait_ge(sc_acc, s)
                        dve.scalar_tensor_tensor(part, relu_s[:, s % 2, 0:P * (i + 1)], w, part, ALU.mult,
                                                 ALU.add).then_inc(sc_acc, 1)
                    if 0 <= r < rounds:
                        dve.wait_ge(taken, 2 * r + 1)
                        mark(1)
                    s += 1
            make_mask(1, 2 * rounds)
            dve.wait_ge(sc_causal, 2)
            with dve.Fori(0, PAIRS // 2) as g:
                for b in range(2):
                    p = 2 * g + b
                    for which in range(3):
                        dve.wait_ge(pr_hi, 3 * p + (which + 1))
                        dve.scalar_tensor_tensor(flat(qkvL[which][:, bass.ds(p, 1), :]), ps[:, PROJ_BANK[b][which], :],
                                                 D_NOPE ** -0.5 if which == 0 else 1.0,
                                                 flat(qkvH[which][:, bass.ds(p, 1), :]).bitcast(F32),
                                                 ALU.mult, ALU.subtract).then_inc(pr_lo, 1)
                        if which < 2:
                            dve.wait_ge(taken, 2 * p + (2 * rounds + which))
                            wait_apart(dve)
                            (largest, mark)[which](2)

            def logits(step, f, p, e):
                if not (isinstance(step, int) and step < 2):
                    dve.wait_ge(pt_rdy, 2 * step - 2)
                for ii in range(2):
                    i = 2 * f + ii
                    dve.wait_ge(bm_rdy, 2 * step + (ii + 1))
                    dve.wait_ge(lg_rdy, 2 * step + (ii + 1))
                    wait_apart(dve)
                    block = slice(OFF[i], OFF[i] + P * (i + 1))
                    dve.tensor_tensor_reduce(L[:, e, block], ps[:, 2 + ii, 0:P * (i + 1)], bm[e][:, block], 1.0,
                                             -3e38, ALU.add, ALU.max, rmax[:, e, ii:ii + 1]).then_inc(lg_done, 1)

            def minus_max(step, f, p, e):
                dve.wait_ge(lg_done, 2 * step + 2)
                dve.tensor_scalar(nmax[:, e, 0:2], rmax[:, e, 0:2], -1.0, None, ALU.mult).then_inc(nm_rdy, 1)

            def probs_lo(step, f, p, e):
                for ii in range(2):
                    i = 2 * f + ii
                    dve.wait_ge(pt_hi, 2 * step + (ii + 1))
                    part = slice(P * ii, P * ii + P)
                    dve.tensor_tensor(ptL[:, e, 0:i + 1, part],
                                      ps[:, 4 + ii, 0:P * (i + 1)].rearrange("p (j n) -> p j n", n=P),
                                      ptH[:, e, 0:i + 1, part].bitcast(F32), ALU.subtract).then_inc(pt_lo, 1)

            def reciprocals(step, f, p, e):
                dve.wait_ge(ex_done, 2 * step + 2)
                dve.reciprocal(rsum[:, e, 0:2], sums[:, e, 0:2]).then_inc(rc_rdy, 1)
                if f == 1:
                    block = L[:, e, 0:OFF[3]]
                    dve.wait_ge(rc_rdy, step + 1)
                    dve.tensor_scalar(block, block, rsum[:, e, 0:1], None, ALU.mult).then_inc(nr_done[0], 1)

            def output_lo(step, f, p, e):
                half = lambda t: flat(t[64 * e:64 * e + 64, bass.ds(p, 1), 2 * P * f:2 * P * (f + 1)])
                dve.wait_ge(o_hi, step + 1)
                dve.tensor_tensor(half(hidl), ps[64 * e:64 * e + 64, 6 + e, 0:2 * P], half(hidh).bitcast(F32),
                                  ALU.subtract).then_inc(o_lo, 1)

            def dve_step(f, g, hh):
                last = isinstance(g, int) and g == PAIRS - 1
                a_round, blocks = f == 0 and not (last and hh == 1), (2, 3) if hh == 0 else (3,)
                base = 6 * g + (2 * rounds + 2 * PAIRS + 4 * hh)
                if a_round:
                    dve.wait_ge(taken, base)
                    wait_apart(dve)
                    for i in blocks:
                        largest(i)
                if a_round and last:
                    dve.wait_ge(taken, base + 2)
                    mark(2)
                    mark(3)
                    make_mask(2, base + 3)
                    dve.wait_ge(taken, base + 4)
                    largest(3)
                    dve.wait_ge(taken, base + 5)
                    mark(3)
                    make_mask(3, base + 6)
                ahead = later(f, g, hh, 2)
                if ahead:
                    logits(*ahead)
                    minus_max(*ahead)
                if a_round and not last:
                    dve.wait_ge(taken, base + len(blocks))
                    wait_apart(dve)
                    for i in blocks:
                        mark(i)
                if later(f, g, hh, 1):
                    probs_lo(*later(f, g, hh, 1))
                if ahead:
                    reciprocals(*ahead)
                output_lo(*later(f, g, hh, 0))
                if f == 1 and isinstance(g, int) and g == PAIRS - 2 and hh == 1:
                    split_lo(C_WO)

            dve.wait_ge(sc_causal, QB - 1)
            for e in range(2):
                logits(e, 0, 0, e)
                minus_max(e, 0, 0, e)
            for e in range(2):
                reciprocals(e, 0, 0, e)
            probs_lo(0, 0, 0, 0)
            passes(dve, dve_step)

            split_lo(C_WO + 1)
            for c in range(4):
                if c:
                    split_lo(C_WO + c + 1)
                for m in (2 * c, 2 * c + 1):
                    dve.wait_ge(mm_done, m + 1)
                    dve.tensor_tensor(xT[:, m, :], ps[:, m % 4, :], xT[:, m, :], ALU.add).then_inc(x_upd, 1)
                    dve.wait_ge(x_upd, m + 1)
                    x_lo(KT + m, m, col(V_NMLP, m))

            def mlp(layer, c0, finish):
                t0, r0, h0, u0 = tile_of(c0), 8 * GROUPS * layer, HID_MLP[layer], UPD_MLP[layer]
                dve.wait_ge(ss_mm, 2 * layer + 1)
                link(dve.tensor_scalar(rbc, ps[:, 4, :], 1.0 / D, EPS, ALU.mult, ALU.add))
                link(dve.reciprocal(rbc, rbc))

                def group(g, last):
                    for j in range(8):
                        c = c0 + j + 1
                        if not (last and j == 7):
                            dve.wait_ge(w_hi, 8 * g + (c + 1))
                            dve.tensor_tensor(wl[:, c % 2, :], raw[:, c % 2, :], wh[:, c % 2, :].bitcast(F32),
                                              ALU.subtract).then_inc(w_lo, 1)
                        elif layer == 0:
                            split_lo(C_PW1)
                        for m in (2 * (j % 4), 2 * (j % 4) + 1):
                            if j < 4:
                                dve.wait_ge(relu_rdy, 8 * g + (r0 + m + 1))
                                dve.wait_ge(hid_lo, 8 * g + (CREDITS + h0 + m - 1))
                                dve.tensor_tensor(sqt[:, m % 2, :], rt[:, m % 2, :], rt[:, m % 2, :],
                                                  ALU.mult).then_inc(sqt_rdy, 1)
                                dve.wait_ge(sqt_rdy, 8 * g + (r0 + m + 1))
                                dve.wait_ge(hid_hi, 8 * g + (h0 + m + 1))
                                dve.tensor_tensor(hidl[:, m, :], sqt[:, m % 2, :], hidh[:, m, :].bitcast(F32),
                                                  ALU.subtract).then_inc(hid_lo, 1)
                            else:
                                dve.wait_ge(mm_done, 16 * g + (t0 + 8 + m + 1))
                                dve.wait_ge(x_upd, 8 * g + (u0 + m - 1))
                                dve.tensor_tensor(dt[:, m % 2, :], ps[:, (t0 + m) % 4, :], rbc,
                                                  ALU.mult).then_inc(dt_rdy, 1)
                                dve.wait_ge(dt_rdy, 8 * g + (r0 + m + 1))
                                dve.tensor_tensor(xT[:, m, :], xT[:, m, :], dt[:, m % 2, :], ALU.add).then_inc(
                                    x_upd, 1)
                                if last:
                                    finish(m)

                with dve.Fori(0, GROUPS - 1) as g:
                    group(g, False)
                group(GROUPS - 1, True)

            mlp(0, C_MLP0, lambda m: x_lo(2 * KT + m, m, col(V_NMIX, KT + m)))

            split_lo(C_PW1 + 1)
            split_lo(C_PW1 + 2)

            def norm_factors(sums, n, root_n):
                link(dve.tensor_scalar(n4f[:, 0, :], sums, 1.0 / D, EPS, ALU.mult, ALU.add))
                link(inverse_root(n4f[:, 0, :], n4f[:, 1, :], n4f[:, 2, :], n4f[:, 3, :], rfin, root_n))
                for i in range(QB):
                    dve.tensor_scalar(rdiag[:, i, :], ident[:, :], rfin[:, i:i + 1], None, ALU.mult).then_inc(
                        rd_rdy, 1)
                dve.wait_ge(rb_mm, n)
                dve.tensor_copy(rbc, ps[:, 4, :]).then_inc(r1_rdy, 1)
                dve.wait_ge(r1_rdy, n + 1)

            dve.wait_ge(ss_mm, 2)
            norm_factors(ps[:, 4, 0:QB], 1, 3)
            dve.wait_ge(pad_rdy, RING)
            t0 = tile_of(C_PW1)

            def gates(i):
                for h in range(2):
                    u = glu[:, (i + h) % RING, TAPS - 1:GW]
                    for gate, dst in enumerate((u, tg[:, h, :])):
                        n = 2 * (i + h) + gate
                        dve.wait_ge(mm_done, t0 + n + 1)
                        if i >= 2:
                            dve.wait_ge(glu_rdy, i)
                        if i >= RING:
                            dve.wait_ge(conv_rdy, i - 2)
                        dve.tensor_tensor(dst, ps[:, (t0 + n) % 4, :], rbc, ALU.mult).then_inc(gate_read, 1)
                if i:
                    split_lo(C_PW1 + i + 2)

            def gated(i):
                for h in range(2):
                    u = glu[:, (i + h) % RING, TAPS - 1:GW]
                    dve.wait_ge(sg_rdy, i + h + 1)
                    dve.wait_ge(gate_read, 2 * (i + h) + 1)
                    dve.scalar_tensor_tensor(u, u, col(V_BP1, i + h), tg[:, h, :], ALU.add, ALU.mult).then_inc(
                        glu_rdy, 1)

            def add_partial(i):
                q = i // 2
                dve.wait_ge(dve_taps, 2 * sum(DVE_TAPS[:q + 1]))
                for h in range(2):
                    dve.wait_ge(diag_used, 2 * sum(PE_TAPS[:q]) + PE_TAPS[q] * (h + 1))
                    dve.tensor_tensor(conv[:, i + h, :], conv[:, i + h, :], ps[:, 6 + h, :], ALU.add).then_inc(
                        pe_added, 1)
                for h in range(2):
                    dve.wait_ge(pe_added, i + h + 1)
                    dve.wait_ge(part_add, 2 * (sum(ACT_TAPS[:q + 1]) - q - 1) - 1 + h)
                    dve.tensor_tensor(conv[:, i + h, :], conv[:, i + h, :], partials[q % 2][:, h, :], ALU.add).then_inc(
                        conv_rdy, 1)

            gates(0)
            gated(0)
            for i in range(0, KT, 2):
                taps = DVE_TAPS[i // 2]
                for j in range(taps):
                    if j == 3:
                        split_lo(C_PW1 + i + 3)
                    if j == taps - 5 and i + 2 < KT:
                        gates(i + 2)
                    if j == taps - 1 and i + 2 < KT:
                        gated(i + 2)
                    for h in range(2):
                        m, n = i + h, 2 * sum(DVE_TAPS[:i // 2]) + 2 * j + h
                        u = glu[:, m % RING, j:j + SEQ]
                        if j == 0:
                            dve.wait_ge(glu_rdy, m + 1)
                            if i == KT - 2:
                                dve.wait_ge(conv_rdy, i)
                            ins = dve.tensor_scalar(conv[:, m, :], u, col(V_DW, m), col(V_BDW, m), ALU.mult, ALU.add)
                        else:
                            dve.wait_ge(dve_taps, n - 1)
                            ins = dve.scalar_tensor_tensor(conv[:, m, :], u, col(V_DW, KT * j + m), conv[:, m, :],
                                                           ALU.mult, ALU.add)
                        ins.then_inc(dve_taps, 1)
                add_partial(i)
            dve.wait_ge(mean_mm, 1)
            link(dve.tensor_scalar(mean, ps[:, 5, :], 1.0 / D, None, ALU.mult))
            dve.wait_ge(conv_rdy, KT)
            for m in range(KT):
                dve.tensor_tensor(conv[:, m, :], conv[:, m, :], mean, ALU.subtract).then_inc(dev_rdy, 1)
            dve.wait_ge(var_mm, KT)
            dve.wait_ge(dev_rdy, KT)
            dve.tensor_copy(rbc, ps[:, 6, :]).then_inc(var_copied, 1)
            dve.wait_ge(var_mm, KT + 1)
            norm_factors(ps[:, 7, 0:QB], 2, 4)
            z0 = HID_MLP[1] - KT

            def z_lo(m):
                dve.wait_ge(hid_hi, z0 + m + 1)
                dve.tensor_tensor(hidl[:, m, :], sg[:, m % 2, :], hidh[:, m, :].bitcast(F32),
                                  ALU.subtract).then_inc(hid_lo, 1)

            for m in range(KT):
                if m >= 2:
                    dve.wait_ge(zs_rdy, m)
                dve.tensor_tensor(tg[:, m % 2, :], conv[:, m, :], rbc, ALU.mult).then_inc(zt_rdy, 1)
                if m:
                    z_lo(m - 1)
            z_lo(KT - 1)
            t0, u0 = tile_of(C_PW2), UPD_FINAL[2]
            for c in range(4):
                if c:
                    split_lo(C_PW2 + c + 1)
                for m in (2 * c, 2 * c + 1):
                    dve.wait_ge(mm_done, t0 + m + 1)
                    dve.scalar_tensor_tensor(xT[:, m, :], ps[:, (t0 + m) % 4, :], col(V_BP2, m), xT[:, m, :], ALU.add,
                                             ALU.add).then_inc(x_upd, 1)
                    dve.wait_ge(x_upd, u0 + m + 1)
                    x_lo(3 * KT + m, m, col(V_NMLP, KT + m))

            def finish_last(m):
                dve.wait_ge(x_upd, UPD_FINAL[3] + m + 1)
                if m >= 2:
                    dve.wait_ge(ftt_rdy, m - 1)
                dve.tensor_scalar(ft[:, m % 2, :], xT[:, m, :], col(V_NFIN, m), None, ALU.mult).then_inc(ft_rdy, 1)

            mlp(1, C_MLP1, finish_last)
            dve.wait_ge(fss_mm, 1)
            link(dve.tensor_scalar(n4f[:, 0, :], ps[:, 7, 0:QB], 1.0 / D, EPS, ALU.mult, ALU.add))
            inverse_root(n4f[:, 0, :], n4f[:, 1, :], n4f[:, 2, :], n4f[:, 3, :], rfin, 5).then_inc(rfin_rdy, 1)
            dve.wait_ge(rfin_rdy, 1)
            dve.wait_ge(ft_copied, KT)
            for i in range(2):
                dve.tensor_scalar(otok[:, i, :], otok[:, i, :], rfin[:, i:i + 1], None, ALU.mult).then_inc(o_dve, 1)

        @block.tensor
        def _(pe):
            def product(dst, ah, al, bh, bl, start, stop):
                pe.matmul(dst, ah, bl, start=start, stop=False)
                pe.matmul(dst, ah, bh, start=False, stop=False)
                return pe.matmul(dst, al, bh, start=False, stop=stop)

            pe.wait_ge(const_rdy, 3)

            def transpose_x(k, i):
                return pe.transpose(ps[:, k % 4, P * i:P * i + P], xtok[:, i, P * k:P * k + P], ident[:, :])

            for i in range(QB):
                pe.wait_ge(x_in[i], 16)
                for k in range(4):
                    last = transpose_x(k, i)
                    if i == QB - 1:
                        last.then_inc(xt_rdy, 1)
            pe.wait_ge(vec_in, 16 * 14)
            pe.transpose(ps[:, 7, 0:V_ROWS], vrow[0:V_ROWS, 0, :], ident[0:V_ROWS, 0:V_ROWS])
            pe.transpose(ps[:, 7, V_DW:V_DW + P], vrow[:, 1, :], ident[:, :])
            rest = TAPS * KT - P
            pe.transpose(ps[:, 7, V_DW + P:V_ALL], vrow[0:rest, 2, :], ident[0:rest, 0:rest]).then_inc(vt_rdy, 1)
            pe.wait_ge(relb_in, 32)
            for h in range(2):
                last = pe.matmul(ps[0:HEADS, 5 + h, 0:320], relb, brow[:, 320 * h:320 * h + 320], start=True, stop=True)
            last.then_inc(rev_mm, 1)
            for k in range(4, KT):
                pe.wait_ge(xt_copied, k - 3)
                for i in range(QB):
                    last = transpose_x(k, i)
                last.then_inc(xt_rdy, 1)
            pe.wait_ge(rev_rdy, 2)
            pe.wait_ge(vcol_rdy, 1)
            for k in range(KT):
                pe.wait_ge(mv_lo, k + 1)
                c, kk = C_WIN + k // 4, k % 4
                if kk == 0:
                    pe.wait_ge(w_lo, c + 1)
                w = slice(W_IN * kk, W_IN * kk + W_IN)
                for i in range(QB):
                    t = slice(P * i, P * i + P)
                    last = product(ps[:, 4 + i, 0:W_IN], movh[:, k, t], movl[:, k, t], wh[:, c, w], wl[:, c, w],
                                   k == 0, k == KT - 1)
                    if k == KT - 1:
                        last.then_inc(pin_rdy, 1)
            pe.wait_ge(projn_q, QB)
            for t in range(4):
                if t == 2:
                    pe.wait_ge(projn_rdy, 1)
                for i in range(QB):
                    last = pe.transpose(ps[:, t, P * i:P * i + P], projn[:, i, P * t:P * t + P], ident[:, :])
                last.then_inc(ct_rdy, 1)

            pe.wait_ge(c_lo, 4)
            pe.wait_ge(proj_rdy, QB)
            pe.wait_ge(w_lo, C_QIDX + 2)
            for t in range(4):
                for k in range(2):
                    w = slice(P * t, P * t + P)
                    last = product(ps[:, 4 + t, :], wh[:, (C_QIDX + k) % 2, w], wl[:, (C_QIDX + k) % 2, w], ch[:, k, :],
                                   cl[:, k, :], k == 0, k == 1)
                last.then_inc(qi_rdy, 1)
            pe.wait_ge(qi_lo, 4)
            s = 0
            for i in range(1, QB):
                for h in range(IDX_HEADS):
                    if s >= 4:
                        pe.wait_ge(sc_relu, s - 3)
                    half, t, n = slice(64 * (h % 2), 64 * (h % 2) + 64), slice(P * i, P * i + P), P * (i + 1)
                    product(ps[:, s % 4, 0:n], qiH[half, h // 2, t], qiL[half, h // 2, t], ch[half, 3, 0:n],
                            cl[half, 3, 0:n], True, True).then_inc(sc_rdy, 1)
                    s += 1

            with pe.Fori(0, PAIRS // 2) as g:
                for b in range(2):
                    p = 2 * g + b
                    wH, wL = swH[:, b, :, :], swL[:, b, :, :]
                    pe.wait_ge(sw_lo, p + 1)
                    if b == 1:
                        pe.wait_ge(sc_relu, s)
                    for which in range(3):
                        pe.wait_ge(pr_lo, 3 * p + (PROJ_CREDITS + which - 5))
                        bank = ps[:, PROJ_BANK[b][which], :]
                        if which == 0:
                            for k in range(2):
                                last = product(bank, wH[:, k, :], wL[:, k, :], ch[:, k, :], cl[:, k, :], k == 0,
                                               k == 1)
                        elif which == 1:
                            last = product(bank, wH[:, 2, :], wL[:, 2, :], ch[:, 2, :], cl[:, 2, :], True, True)
                        else:
                            for j in range(QB):
                                t = slice(P * j, P * j + P)
                                last = product(bank[:, t], ch[:, 2, t], cl[:, 2, t], wH[:, 3, :], wL[:, 3, :], True,
                                               True)
                        last.then_inc(pr_rdy, 1)

            def logits(step, f, p, e):
                half = slice(64 * e, 64 * e + 64)
                for ii in range(2):
                    i = 2 * f + ii
                    t, w = slice(P * i, P * i + P), slice(0, P * (i + 1))
                    if step:
                        pe.wait_ge(lg_done, 2 * step + ii - 1)
                    product(ps[:, 2 + ii, w], *(x[half, p, y] for x, y in
                                                ((qkvH[0], t), (qkvL[0], t), (qkvH[1], w), (qkvL[1], w))),
                            True, True).then_inc(lg_rdy, 1)

            def transposes(step, f, p, e):
                for ii in range(2):
                    i = 2 * f + ii
                    pe.wait_ge(nr_done[ii], step + 1)
                    if step:
                        pe.wait_ge(pt_lo, 2 * step + ii - 1)
                    for j in range(i + 1):
                        last = pe.transpose(ps[:, 4 + ii, P * j:P * j + P],
                                            L[:, e, OFF[i] + P * j:OFF[i] + P * j + P], ident[:, :])
                    last.then_inc(pt_rdy, 1)

            def head_output(step, f, p, e):
                pe.wait_ge(pt_lo, 2 * step + 2)
                if step >= 2:
                    pe.wait_ge(o_lo, step - 1)
                for j in range(2 * f + 2):
                    keys, t = slice(P * j, P * j + P), slice(0 if j <= 2 * f else P, 2 * P)
                    last = product(ps[:, 6 + e, t], qkvH[2][:, p, keys], qkvL[2][:, p, keys], ptH[:, e, j, t],
                                   ptL[:, e, j, t], j == 0, j == 2 * f + 1)
                last.then_inc(pv_rdy, 1)

            pe.wait_ge(pr_lo, 3 * PAIRS + PROJ_CREDITS)
            logits(0, 0, 0, 0)
            logits(1, 0, 0, 1)
            transposes(0, 0, 0, 0)
            for step in range(STEPS):
                f, pair, e = step // HEADS, step % HEADS // 2, step % 2
                for work, d in ((logits, 2), (transposes, 1), (head_output, 0)):
                    head = later(f, pair, e, d)
                    if head:
                        work(*head)

            def weight_product(bank, c, h, k, n, mh, ml):
                w = slice(256 * k + P * h, 256 * k + P * h + P)
                return product(ps[:, bank, :], wh[:, c % 2, w], wl[:, c % 2, w], mh[:, k, :], ml[:, k, :], k == 0,
                               k == n - 1)

            for t in range(KT):
                c, h = C_WO + t // 2, t % 2
                if h == 0:
                    pe.wait_ge(w_lo, c + 1)
                if t >= 4:
                    pe.wait_ge(x_upd, t - 3)
                for k in range(KT):
                    if t == 0:
                        pe.wait_ge(o_lo, HEADS + 2 * k + 2)
                    last = weight_product(t % 4, c, h, k, KT, hidh, hidl)
                last.then_inc(mm_done, 1)

            def by_token(bank, tile, column=ones[:, 0:1]):
                for i in range(QB):
                    last = pe.matmul(ps[:, bank, i:i + 1], tile[:, P * i:P * i + P], column, start=True,
                                     stop=True)
                return last

            def spread(n):
                for i in range(QB):
                    pe.wait_ge(rd_rdy, QB * (n - 1) + i + 1)
                    last = pe.matmul(ps[:, 4, P * i:P * i + P], ones[:, :], rdiag[:, i, :], start=True, stop=True)
                last.then_inc(rb_mm, 1)

            def square_sums(f):
                pe.wait_ge(ss_add, KT * (f + 1))
                pe.matmul(ps[:, 4, :], ones[:, :], ss, start=True, stop=True).then_inc(ss_mm, 1)

            def mlp(layer, c0, mv0, f, after):
                t0 = tile_of(c0)

                def tile(g, u):
                    c, h = c0 + u // 2, u % 2
                    if h == 0:
                        pe.wait_ge(w_lo, 8 * g + (c + 1))
                    if u < 4:
                        pe.wait_ge(x_upd, 8 * g + (UPD_MLP[layer] - 4 + u + 1))
                    elif u < 12:
                        pe.wait_ge(relu_rdy, 8 * g + (8 * GROUPS * layer + u - 3))
                    else:
                        pe.wait_ge(x_upd, 8 * g + (UPD_MLP[layer] + u - 11))
                    for k in range(KT):
                        if u == 0 and isinstance(g, int) and g == 0:
                            pe.wait_ge(mv_lo, mv0 + k + 1)
                        if u == 8:
                            pe.wait_ge(hid_lo, 8 * g + (CREDITS + HID_MLP[layer] + k + 1))
                        mh, ml = (movh, movl) if u < 8 else (hidh, hidl)
                        last = weight_product((t0 + u) % 4, c, h, k, KT, mh, ml)
                    last.then_inc(mm_done, 1)

                for u in range(16):
                    tile(0, u)
                    if u == 0:
                        square_sums(f)
                with pe.Fori(1, GROUPS - (1 if after else 0)) as g:
                    for u in range(16):
                        tile(g, u)
                if after:
                    for u in range(16):
                        tile(GROUPS - 1, u)
                        if u > 8:
                            after(u - 9)

            mlp(0, C_MLP0, KT, 0, None)

            t0 = tile_of(C_PW1)

            def pointwise(t):
                c, h = C_PW1 + t // 2, t % 2
                if h == 0:
                    pe.wait_ge(w_lo, c + 1)
                if t < 4:
                    pe.wait_ge(x_upd, UPD_FINAL[1] + KT - 4 + t + 1)
                else:
                    pe.wait_ge(gate_read, t - 3)
                for k in range(KT):
                    if t == 0:
                        pe.wait_ge(mv_lo, 2 * KT + k + 1)
                    last = weight_product((t0 + t) % 4, c, h, k, KT, movh, movl)
                last.then_inc(mm_done, 1)

            def convolve(i):
                first, last = DVE_TAPS[i // 2], DVE_TAPS[i // 2] + PE_TAPS[i // 2] - 1
                for d, m, j in diagonals(i):
                    if j == first:
                        pe.wait_ge(glu_rdy, m + 1)
                        if m >= 2:
                            pe.wait_ge(pe_added, m - 1)
                    pe.wait_ge(diag_rdy, d + 1)
                    pe.matmul(ps[:, 6 + m % 2, :], diags[d % len(diags)], glu[:, m % RING, j:j + SEQ],
                              start=j == first, stop=j == last).then_inc(diag_used, 1)

            for t in range(2 * KT):
                pointwise(t)
                if t == 1:
                    pe.wait_ge(ss_add, 2 * KT)
                    by_token(4, ss).then_inc(ss_mm, 1)
                if t == 2:
                    spread(1)
                if t % 4 == 3 and t > 3:
                    convolve((t - 3) // 2 - 2)

            def add_features(m):
                pe.wait_ge(conv_rdy, m + 1)
                return pe.matmul(ps[:, 5, :], ones[:, :], conv[:, m, :], start=m == 0, stop=m == KT - 1)

            for m in range(4):
                add_features(m)
            convolve(KT - 2)
            for m in range(4, KT):
                last = add_features(m)
            last.then_inc(mean_mm, 1)
            for m in range(KT):
                pe.wait_ge(dsq_rdy, m + 1)
                pe.matmul(ps[:, 6, :], ones[:, :], tg[:, m % 2, :], start=m == 0, stop=m == KT - 1).then_inc(var_mm, 1)
            pe.wait_ge(var_copied, 1)
            by_token(7, rbc, ident[:, 0:1]).then_inc(var_mm, 1)
            spread(2)
            t0 = tile_of(C_PW2)
            for t in range(KT):
                c, h = C_PW2 + t // 2, t % 2
                if h == 0:
                    pe.wait_ge(w_lo, c + 1)
                if t >= 4:
                    pe.wait_ge(x_upd, UPD_FINAL[2] + t - 3)
                else:
                    pe.wait_ge(gate_read, 2 * KT - 3 + t)
                for k in range(KT):
                    if t == 0:
                        pe.wait_ge(hid_lo, CREDITS + HID_MLP[1] - KT + k + 1)
                    last = weight_product((t0 + t) % 4, c, h, k, KT, hidh, hidl)
                last.then_inc(mm_done, 1)

            def transpose_out(m):
                pe.wait_ge(ft_rdy, m + 1)
                if m >= 2:
                    pe.wait_ge(ft_copied, m - 1)
                for i in range(QB):
                    last = pe.transpose(ps[:, 5 + m % 2, P * i:P * i + P], ft[:, m % 2, P * i:P * i + P], ident[:, :])
                last.then_inc(ftt_rdy, 1)

            mlp(1, C_MLP1, 3 * KT, 2, transpose_out)
            transpose_out(KT - 1)
            pe.wait_ge(ss_add, 4 * KT)
            by_token(7, ss).then_inc(fss_mm, 1)


def kernel(**inputs):
    import math as _math
    import numpy as _np
    import concourse.bacc as _bacc
    from concourse import mybir as _mybir
    from concourse.bass_utils import run_bass_kernel_spmd as _run

    dist = _np.maximum(SEQ - 1 - _np.arange(REV), 0)
    near = NB // 2
    large = near + (_np.log(_np.maximum(dist, 1).astype(_np.float32) / near) / _np.float32(_math.log(128 / near))
                    * (NB - near)).astype(_np.int32)
    bucket = _np.where(dist < near, dist, _np.minimum(large, NB - 1))
    bucket_rows = (bucket[None, :] == _np.arange(NB)[:, None]).astype(_np.float32)

    nc = _bacc.Bacc("TRN2", target_bir_lowering=False, num_devices=1)
    names = ("x", "norm_mix", "norm_mlp", "norm_final", "rel_bias", "attn_w_in", "attn_q_norm", "attn_kv_norm",
             "attn_kidx_norm", "attn_w_qidx", "attn_w_uq", "attn_w_uk", "attn_w_uv", "attn_w_o", "conv_w_pw1",
             "conv_b_pw1", "conv_w_dw", "conv_b_dw", "conv_ln_g", "conv_ln_b", "conv_w_pw2", "conv_b_pw2",
             "mlp_w_up", "mlp_w_down")
    arrays, args = {}, []
    for name in names:
        arrays[name] = _np.ascontiguousarray(inputs[name])
    arrays["norm_final"] = arrays["norm_final"].reshape(1, D)
    arrays["bucket_rows"] = bucket_rows
    for name, a in arrays.items():
        args.append(nc.dram_tensor(name, a.shape, _mybir.dt.float32, kind="ExternalInput").ap())
    args.append(nc.dram_tensor("out", (1, SEQ, D), _mybir.dt.float32, kind="ExternalOutput").ap())
    program(nc, *args)
    r = _run(nc, [arrays], core_ids=[0])
    return r.results[0]["out"]
```
